# Optimizing a Trainium2 kernel written in Bass

```python
import jax, jax.numpy as jnp
from jax import lax
import numpy as np
import math

D_MODEL = 1024
BATCH = 1
SEQ = 256
DEPTH = 2

GRID_W = 64
CTX_LEN = 256
D_FF = 2752
N_MOD = 9
EPS = 1e-6
D_FOURIER = D_MODEL // 2
FOURIER_CH = 128
FOURIER_GROUPS = D_FOURIER // FOURIER_CH
D_SGU = D_MODEL // 2
SGU_CH = 128
SGU_GROUPS = D_SGU // SGU_CH
CHUNK = 128
HEAD_DIM = 128
N_HEADS = D_MODEL // HEAD_DIM
N_KV_HEADS = 2
GROUP = N_HEADS // N_KV_HEADS
ROPE_AXIS_DIM = HEAD_DIM // 2
ROPE_THETA = 10000.0
Q_BLOCK = 128


def rms_norm(x, g):
    xf = x.astype(jnp.float32)
    y = xf * lax.rsqrt(jnp.mean(jnp.square(xf), axis=-1, keepdims=True) + EPS)
    return (y * g.astype(jnp.float32)).astype(x.dtype)

def adaln(cvec, w_mod, b_mod):
    m = jax.nn.silu(cvec) @ w_mod + b_mod
    m = m.reshape(m.shape[0], 1, N_MOD, D_MODEL)
    return [m[:, :, i] for i in range(N_MOD)]

def modulated_norm(x, g, shift, scale):
    return rms_norm(x, g) * (1 + scale) + shift

def swiglu(h, w_gu, w_down):
    gate, up = jnp.split(h @ w_gu, 2, axis=-1)
    return (jax.nn.silu(gate) * up) @ w_down

def ffn_half_step(x, mods, g, w_gu, w_down):
    shift, scale, gate = mods
    return x + 0.5 * gate * swiglu(modulated_norm(x, g, shift, scale), w_gu, w_down)

def fourier_mix(a):
    b_, n, _ = a.shape
    a4 = a.reshape(b_, n, FOURIER_GROUPS, FOURIER_CH).astype(jnp.float32)
    f = jnp.fft.fftn(a4, axes=(1, 3), norm="ortho").real
    return f.reshape(b_, n, D_FOURIER).astype(a.dtype)

def chunk_sgu(u, v, g_v, w_s, b_s):
    b_, n, _ = v.shape
    vh = rms_norm(v.reshape(b_, n, SGU_GROUPS, SGU_CH), g_v)
    vc = vh.reshape(b_, n // CHUNK, CHUNK, SGU_GROUPS, SGU_CH)
    mixed = jnp.einsum('hpq,bcqhd->bcphd', w_s, vc) + b_s.T[None, None, :, :, None]
    return u * mixed.reshape(b_, n, D_SGU)

def fourier_sgu_mixer(h, w_in, g_v, w_s, b_s, w_out):
    a, uv = jnp.split(h @ w_in, [D_FOURIER], axis=-1)
    u, v = jnp.split(jax.nn.gelu(uv), 2, axis=-1)
    out = jnp.concatenate([fourier_mix(a), chunk_sgu(u, v, g_v, w_s, b_s)], axis=-1)
    return out @ w_out

def axial_angles(rows):
    row = jnp.repeat(jnp.arange(rows, dtype=jnp.float32), GRID_W)
    col = jnp.tile(jnp.arange(GRID_W, dtype=jnp.float32), rows)
    inv_freq = ROPE_THETA ** (-jnp.arange(0, ROPE_AXIS_DIM, 2, dtype=jnp.float32) / ROPE_AXIS_DIM)
    return row[:, None] * inv_freq, col[:, None] * inv_freq

def rotate(x, ang):
    full = jnp.concatenate([ang, ang], axis=-1)[:, None, :]
    cos = jnp.cos(full).astype(x.dtype)
    sin = jnp.sin(full).astype(x.dtype)
    x1, x2 = jnp.split(x, 2, axis=-1)
    return x * cos + jnp.concatenate([-x2, x1], axis=-1) * sin

def axial_rope(x, ang_row, ang_col):
    xr, xc = jnp.split(x, 2, axis=-1)
    return jnp.concatenate([rotate(xr, ang_row), rotate(xc, ang_col)], axis=-1)

def project_kv(kv, g_k):
    b_, n, _ = kv.shape
    k, v = jnp.split(kv, 2, axis=-1)
    k = rms_norm(k.reshape(b_, n, N_KV_HEADS, HEAD_DIM), g_k)
    return k, v.reshape(b_, n, N_KV_HEADS, HEAD_DIM)

def project_q(q, g_q):
    b_, n, _ = q.shape
    return rms_norm(q.reshape(b_, n, N_HEADS, HEAD_DIM), g_q)

def gqa_attend(q, k, v):
    b_, nq = q.shape[:2]
    qg = q.reshape(b_, nq, N_KV_HEADS, GROUP, HEAD_DIM)
    s = jnp.einsum('bqkgd,bskd->bkgqs', qg, k, preferred_element_type=jnp.float32) * (HEAD_DIM ** -0.5)
    p = jax.nn.softmax(s, axis=-1).astype(v.dtype)
    o = jnp.einsum('bkgqs,bskd->bqkgd', p, v)
    return o.reshape(b_, nq, N_HEADS * HEAD_DIM)

def blocked_attention(q, k_all, v_all):
    b_, n = q.shape[:2]
    n_blk = n // Q_BLOCK
    qb = jnp.moveaxis(q.reshape(b_, n_blk, Q_BLOCK, N_HEADS, HEAD_DIM), 1, 0)
    o = lax.map(lambda qblk: gqa_attend(qblk, k_all, v_all), qb)
    return jnp.moveaxis(o, 0, 1).reshape(b_, n, N_HEADS * HEAD_DIM)

def first_inputs(seed: int = 0) -> dict:
    key = jax.random.key(seed)
    ks = jax.random.split(key, 24)
    n_even = (DEPTH + 1) // 2
    n_odd = DEPTH // 2

    def nrm(k, shape, fan_in, s=1.0):
        return s * jax.random.normal(k, shape, jnp.float32) * (fan_in ** -0.5)

    def gain(k, shape):
        return 1.0 + 0.05 * jax.random.normal(k, shape, jnp.float32)

    return {
        "x": jax.random.normal(ks[0], (BATCH, SEQ, D_MODEL), jnp.float32),
        "c": jax.random.normal(ks[1], (BATCH, D_MODEL), jnp.float32),
        "ctx": jax.random.normal(ks[2], (BATCH, CTX_LEN, D_MODEL), jnp.float32),
        "c_ctx": jax.random.normal(ks[3], (D_MODEL,), jnp.float32),
        "w_mod": nrm(ks[4], (DEPTH, D_MODEL, N_MOD * D_MODEL), D_MODEL, 0.5),
        "b_mod": 0.02 * jax.random.normal(ks[5], (DEPTH, N_MOD * D_MODEL), jnp.float32),
        "g_ffn1": gain(ks[6], (DEPTH, D_MODEL)),
        "w_ffn1_gu": nrm(ks[7], (DEPTH, D_MODEL, 2 * D_FF), D_MODEL),
        "w_ffn1_down": nrm(ks[8], (DEPTH, D_FF, D_MODEL), D_FF),
        "g_mix": gain(ks[9], (DEPTH, D_MODEL)),
        "g_ffn2": gain(ks[10], (DEPTH, D_MODEL)),
        "w_ffn2_gu": nrm(ks[11], (DEPTH, D_MODEL, 2 * D_FF), D_MODEL),
        "w_ffn2_down": nrm(ks[12], (DEPTH, D_FF, D_MODEL), D_FF),
        "g_final": gain(ks[13], (D_MODEL,)),
        "w_in_ab": nrm(ks[14], (n_even, D_MODEL, D_FOURIER + 2 * D_SGU), D_MODEL),
        "g_v": gain(ks[15], (n_even, SGU_GROUPS, SGU_CH)),
        "w_s": nrm(ks[16], (n_even, SGU_GROUPS, CHUNK, CHUNK), CHUNK, 0.5),
        "b_s": 1.0 + 0.02 * jax.random.normal(ks[17], (n_even, SGU_GROUPS, CHUNK), jnp.float32),
        "w_out_ab": nrm(ks[18], (n_even, D_FOURIER + D_SGU, D_MODEL), D_FOURIER + D_SGU),
        "w_qkv": nrm(ks[19], (n_odd, D_MODEL, (N_HEADS + 2 * N_KV_HEADS) * HEAD_DIM), D_MODEL),
        "g_q": gain(ks[20], (n_odd, HEAD_DIM)),
        "g_k": gain(ks[21], (n_odd, HEAD_DIM)),
        "w_o": nrm(ks[22], (n_odd, N_HEADS * HEAD_DIM, D_MODEL), N_HEADS * HEAD_DIM),
    }

def first_block(x, c, ctx, c_ctx, w_mod, b_mod, g_ffn1, w_ffn1_gu, w_ffn1_down, g_mix,
              g_ffn2, w_ffn2_gu, w_ffn2_down, g_final, w_in_ab, g_v, w_s, b_s, w_out_ab,
              w_qkv, g_q, g_k, w_o):
    n_tok = x.shape[1]
    ROWS = n_tok // GRID_W
    ang_row, ang_col = axial_angles(ROWS)
    q_cols = N_HEADS * HEAD_DIM

    for l in range(DEPTH):
        last = l == DEPTH - 1
        even = l % 2 == 0
        j = l // 2
        mx = adaln(c, w_mod[l], b_mod[l])
        mc = adaln(c_ctx[None], w_mod[l], b_mod[l])
        ctx_live = (not last) or (not even)

        x = ffn_half_step(x, mx[0:3], g_ffn1[l], w_ffn1_gu[l], w_ffn1_down[l])
        if ctx_live:
            ctx = ffn_half_step(ctx, mc[0:3], g_ffn1[l], w_ffn1_gu[l], w_ffn1_down[l])

        hx = modulated_norm(x, g_mix[l], mx[3], mx[4])
        if even:
            out_x = fourier_sgu_mixer(hx, w_in_ab[j], g_v[j], w_s[j], b_s[j], w_out_ab[j])
            if not last:
                hc = modulated_norm(ctx, g_mix[l], mc[3], mc[4])
                out_c = fourier_sgu_mixer(hc, w_in_ab[j], g_v[j], w_s[j], b_s[j], w_out_ab[j])
        else:
            hc = modulated_norm(ctx, g_mix[l], mc[3], mc[4])
            qkv_x = hx @ w_qkv[j]
            q_x = axial_rope(project_q(qkv_x[..., :q_cols], g_q[j]), ang_row, ang_col)
            k_x, v_x = project_kv(qkv_x[..., q_cols:], g_k[j])
            k_x = axial_rope(k_x, ang_row, ang_col)
            if last:
                k_c, v_c = project_kv(hc @ w_qkv[j][:, q_cols:], g_k[j])
            else:
                qkv_c = hc @ w_qkv[j]
                k_c, v_c = project_kv(qkv_c[..., q_cols:], g_k[j])
                q_c = project_q(qkv_c[..., :q_cols], g_q[j])
                out_c = gqa_attend(q_c, k_c, v_c) @ w_o[j]
            k_all = jnp.concatenate([k_x, k_c], axis=1)
            v_all = jnp.concatenate([v_x, v_c], axis=1)
            out_x = blocked_attention(q_x, k_all, v_all) @ w_o[j]

        x = x + mx[5] * out_x
        x = ffn_half_step(x, mx[6:9], g_ffn2[l], w_ffn2_gu[l], w_ffn2_down[l])
        if not last:
            ctx = ctx + mc[5] * out_c
            ctx = ffn_half_step(ctx, mc[6:9], g_ffn2[l], w_ffn2_gu[l], w_ffn2_down[l])

    return rms_norm(x, g_final)


DEPTH_2 = 4

N_MIXERS = 3
N_RET = (DEPTH_2 + 2) // 3
N_MOBA = (DEPTH_2 + 1) // 3
N_DIFF = DEPTH_2 // 3

RET_HEADS = 4
RET_DK = D_MODEL // RET_HEADS
RET_DV = 2 * RET_DK
RET_CHUNK = 128
ROPE_BASE = 10000.0

ATTN_HEADS = 16
HEAD_DIM_2 = D_MODEL // ATTN_HEADS
MOBA_BLOCK = 256
MOBA_TOPK = 3
MOBA_Q_CHUNK = 16
DIFF_HEADS = ATTN_HEADS // 2
DIFF_V_DIM = 2 * HEAD_DIM_2
ATTN_Q_BLOCK = 128

REL_BUCKETS = 32
REL_MAX_EXACT = REL_BUCKETS // 2
REL_MAX_DISTANCE = 1024

D_FF_2 = 4 * D_MODEL
NEG = -1e30


def _rmsnorm(x, w):
    xf = x.astype(jnp.float32)
    y = xf * lax.rsqrt(jnp.mean(xf * xf, axis=-1, keepdims=True) + EPS)
    return y.astype(x.dtype) * w

def _rel_bucket(dist):
    n = jnp.maximum(dist, 0)
    nf = jnp.maximum(n, 1).astype(jnp.float32)
    large = REL_MAX_EXACT + (jnp.log(nf / REL_MAX_EXACT) / math.log(REL_MAX_DISTANCE / REL_MAX_EXACT)
                             * (REL_BUCKETS - REL_MAX_EXACT)).astype(jnp.int32)
    large = jnp.minimum(large, REL_BUCKETS - 1)
    return jnp.where(n < REL_MAX_EXACT, n, large)

def _rotary(x):
    S, d = x.shape[2], x.shape[3]
    inv_freq = ROPE_BASE ** (-jnp.arange(0, d, 2, dtype=jnp.float32) / d)
    ang = jnp.arange(S, dtype=jnp.float32)[:, None] * inv_freq[None, :]
    cos, sin = jnp.cos(ang), jnp.sin(ang)
    x1, x2 = x[..., : d // 2], x[..., d // 2:]
    return jnp.concatenate([x1 * cos - x2 * sin, x1 * sin + x2 * cos], axis=-1)

def _squared_relu_mlp(h, w_up, w_down):
    u = jax.nn.relu(h @ w_up)
    return (u * u) @ w_down

def _retention_mixer(h, w_in, w_out):
    B, S, _ = h.shape
    H, dk, dv, C = RET_HEADS, RET_DK, RET_DV, RET_CHUNK
    N = S // C
    proj = (h @ w_in).astype(jnp.float32)
    q, k, v, g = jnp.split(proj, [H * dk, 2 * H * dk, 2 * H * dk + H * dv], axis=-1)
    q = _rotary(q.reshape(B, S, H, dk).transpose(0, 2, 1, 3))
    k = _rotary(k.reshape(B, S, H, dk).transpose(0, 2, 1, 3)) * (dk ** -0.5)
    v = v.reshape(B, S, H, dv).transpose(0, 2, 1, 3)

    log_gamma = jnp.log(1.0 - 2.0 ** (-5.0 - jnp.arange(H, dtype=jnp.float32)))
    pos = jnp.arange(C, dtype=jnp.float32)
    rel = pos[:, None] - pos[None, :]
    inner_decay = jnp.where(rel >= 0, jnp.exp(jnp.maximum(rel, 0.0)[None] * log_gamma[:, None, None]), 0.0)

    qc = q.reshape(B, H, N, C, dk)
    kc = k.reshape(B, H, N, C, dk)
    vc = v.reshape(B, H, N, C, dv)
    s_in = jnp.einsum('bhnid,bhnjd->bhnij', qc, kc) * inner_decay[:, None]
    inner = jnp.einsum('bhnij,bhnjv->bhniv', s_in, vc)
    q_dec = qc * jnp.exp((pos + 1.0)[None, :] * log_gamma[:, None])[:, None, :, None]
    k_dec = kc * jnp.exp((C - 1.0 - pos)[None, :] * log_gamma[:, None])[:, None, :, None]
    chunk_decay = jnp.exp(C * log_gamma)[:, None, None]

    def step(state, xs):
        qn, kn, vn = xs
        out = jnp.einsum('bhid,bhdv->bhiv', qn, state)
        state = state * chunk_decay + jnp.einsum('bhjd,bhjv->bhdv', kn, vn)
        return state, out

    xs = (jnp.moveaxis(q_dec, 2, 0), jnp.moveaxis(k_dec, 2, 0), jnp.moveaxis(vc, 2, 0))
    _, cross = lax.scan(step, jnp.zeros((B, H, dk, dv), jnp.float32), xs)
    o = (inner + jnp.moveaxis(cross, 0, 2)).reshape(B, H, S, dv)
    o = o * lax.rsqrt(jnp.mean(o * o, axis=-1, keepdims=True) + EPS)
    o = o.transpose(0, 2, 1, 3).reshape(B, S, H * dv)
    return ((jax.nn.silu(g) * o) @ w_out).astype(h.dtype)

def _moba_mixer(h, w_in, q_norm_w, k_norm_w, w_out, rel_bias):
    B, S, _ = h.shape
    H, d, BS, QC = ATTN_HEADS, HEAD_DIM_2, MOBA_BLOCK, MOBA_Q_CHUNK
    proj = h @ w_in
    q, k, v = jnp.split(proj, 3, axis=-1)
    q = _rmsnorm(q.reshape(B, S, H, d), q_norm_w).transpose(0, 2, 1, 3).astype(jnp.float32) * (d ** -0.5)
    k = _rmsnorm(k.reshape(B, S, H, d), k_norm_w).transpose(0, 2, 1, 3).astype(jnp.float32)
    v = v.reshape(B, S, H, d).transpose(0, 2, 1, 3)
    NB = -(-S // BS)
    pad = NB * BS - S
    k_pad = jnp.pad(k, ((0, 0), (0, 0), (0, pad), (0, 0)))
    v_pad = jnp.pad(v, ((0, 0), (0, 0), (0, pad), (0, 0)))
    kb = k_pad.reshape(B, H, NB, BS, d)
    vb = v_pad.reshape(B, H, NB, BS, d)
    k_mean = kb.mean(axis=3)
    topk = min(MOBA_TOPK, NB)
    bias_t = rel_bias.T.astype(jnp.float32)
    head_idx = jnp.arange(H)[None, :, None, None, None]
    in_block = jnp.arange(BS)
    gather = jax.vmap(jax.vmap(lambda blocks, ix: blocks[ix]))

    def chunk(c):
        t0 = c * QC
        b = t0 // BS
        t = t0 + jnp.arange(QC)
        qc = lax.dynamic_slice_in_dim(q, t0, QC, axis=2)
        gate = jnp.einsum('bhqd,bhnd->bhqn', qc, k_mean)
        gate = jnp.where(jnp.arange(NB) < b, gate, NEG)
        _, idx = lax.top_k(gate, topk)
        valid = idx < b
        k_sel = gather(kb, idx)
        v_sel = gather(vb, idx)
        s_sel = jnp.einsum('bhqd,bhqkjd->bhqkj', qc, k_sel)
        kpos = idx[..., None] * BS + in_block
        s_sel = s_sel + bias_t[head_idx, _rel_bucket(t[:, None, None] - kpos)]
        s_sel = jnp.where(valid[..., None], s_sel, NEG)
        k_own = lax.dynamic_slice_in_dim(k_pad, b * BS, BS, axis=2)
        v_own = lax.dynamic_slice_in_dim(v_pad, b * BS, BS, axis=2)
        dist = t[:, None] - (b * BS + in_block)[None, :]
        s_own = jnp.einsum('bhqd,bhjd->bhqj', qc, k_own) + bias_t[:, _rel_bucket(dist)]
        s_own = jnp.where(dist >= 0, s_own, NEG)
        scores = jnp.concatenate([s_sel.reshape(B, H, QC, topk * BS), s_own], axis=-1)
        p = jax.nn.softmax(scores, axis=-1)
        p_sel = p[..., : topk * BS].reshape(B, H, QC, topk, BS)
        p_own = p[..., topk * BS:]
        return (jnp.einsum('bhqkj,bhqkjd->bhqd', p_sel, v_sel)
                + jnp.einsum('bhqj,bhjd->bhqd', p_own, v_own))

    outs = lax.map(chunk, jnp.arange(S // QC))
    o = outs.transpose(1, 2, 0, 3, 4).reshape(B, H, S, d).transpose(0, 2, 1, 3).reshape(B, S, H * d)
    return (o @ w_out).astype(h.dtype)

def _diff_mixer(h, w_in, q_norm_w, k_norm_w, lambdas, subln_w, w_out, rel_bias, lambda_init):
    B, S, _ = h.shape
    H2, d, QB = 2 * DIFF_HEADS, HEAD_DIM_2, ATTN_Q_BLOCK
    proj = h @ w_in
    q, k, v = jnp.split(proj, 3, axis=-1)
    q = _rmsnorm(q.reshape(B, S, H2, d), q_norm_w).transpose(0, 2, 1, 3).astype(jnp.float32) * (d ** -0.5)
    k = _rmsnorm(k.reshape(B, S, H2, d), k_norm_w).transpose(0, 2, 1, 3).astype(jnp.float32)
    v = v.reshape(B, S, DIFF_HEADS, DIFF_V_DIM).transpose(0, 2, 1, 3)
    lam = lambdas.astype(jnp.float32)
    lambda_full = jnp.exp(jnp.sum(lam[0] * lam[1])) - jnp.exp(jnp.sum(lam[2] * lam[3])) + lambda_init
    bias_t = rel_bias.T.astype(jnp.float32)
    kpos = jnp.arange(S)

    def block(c):
        t0 = c * QB
        t = t0 + jnp.arange(QB)
        qb = lax.dynamic_slice_in_dim(q, t0, QB, axis=2)
        dist = t[:, None] - kpos[None, :]
        s = jnp.einsum('bhqd,bhkd->bhqk', qb, k) + bias_t[:, _rel_bucket(dist)]
        s = jnp.where(dist >= 0, s, NEG)
        p = jax.nn.softmax(s, axis=-1).reshape(B, DIFF_HEADS, 2, QB, S)
        attn = p[:, :, 0] - lambda_full * p[:, :, 1]
        return jnp.einsum('bhqk,bhkv->bhqv', attn, v)

    outs = lax.map(block, jnp.arange(S // QB))
    o = outs.transpose(1, 2, 0, 3, 4).reshape(B, DIFF_HEADS, S, DIFF_V_DIM)
    o = _rmsnorm(o, subln_w) * (1.0 - lambda_init)
    o = o.transpose(0, 2, 1, 3).reshape(B, S, DIFF_HEADS * DIFF_V_DIM)
    return (o @ w_out).astype(h.dtype)

def second_inputs(seed: int = 0) -> dict:
    key = jax.random.key(seed)
    ks = jax.random.split(key, 18)

    def nrm(k, shape, scale):
        return jax.random.normal(k, shape, jnp.float32) * scale

    D = D_MODEL
    ret_in = 2 * RET_HEADS * RET_DK + 2 * RET_HEADS * RET_DV
    return {
        "x": nrm(ks[0], (BATCH, SEQ, D), 1.0),
        "rel_bias": nrm(ks[1], (REL_BUCKETS, ATTN_HEADS), 0.5),
        "norm1": 1.0 + nrm(ks[2], (DEPTH_2, D), 0.02),
        "norm2": 1.0 + nrm(ks[3], (DEPTH_2, D), 0.02),
        "w_up": nrm(ks[4], (DEPTH_2, D, D_FF_2), D ** -0.5),
        "w_down": nrm(ks[5], (DEPTH_2, D_FF_2, D), D_FF_2 ** -0.5),
        "ret_w_in": nrm(ks[6], (N_RET, D, ret_in), D ** -0.5),
        "ret_w_out": nrm(ks[7], (N_RET, RET_HEADS * RET_DV, D), (RET_HEADS * RET_DV) ** -0.5),
        "moba_w_in": nrm(ks[8], (N_MOBA, D, 3 * ATTN_HEADS * HEAD_DIM_2), D ** -0.5),
        "moba_q_norm": 1.0 + nrm(ks[9], (N_MOBA, HEAD_DIM_2), 0.02),
        "moba_k_norm": 1.0 + nrm(ks[10], (N_MOBA, HEAD_DIM_2), 0.02),
        "moba_w_out": nrm(ks[11], (N_MOBA, ATTN_HEADS * HEAD_DIM_2, D), (ATTN_HEADS * HEAD_DIM_2) ** -0.5),
        "diff_w_in": nrm(ks[12], (N_DIFF, D, 3 * ATTN_HEADS * HEAD_DIM_2), D ** -0.5),
        "diff_q_norm": 1.0 + nrm(ks[13], (N_DIFF, HEAD_DIM_2), 0.02),
        "diff_k_norm": 1.0 + nrm(ks[14], (N_DIFF, HEAD_DIM_2), 0.02),
        "diff_lambda": nrm(ks[15], (N_DIFF, 4, HEAD_DIM_2), 0.1),
        "diff_subln": 1.0 + nrm(ks[16], (N_DIFF, DIFF_V_DIM), 0.02),
        "diff_w_out": nrm(ks[17], (N_DIFF, DIFF_HEADS * DIFF_V_DIM, D), (DIFF_HEADS * DIFF_V_DIM) ** -0.5),
    }

def second_block(x, rel_bias, norm1, norm2, w_up, w_down, ret_w_in, ret_w_out,
              moba_w_in, moba_q_norm, moba_k_norm, moba_w_out,
              diff_w_in, diff_q_norm, diff_k_norm, diff_lambda, diff_subln, diff_w_out):
    for i in range(DEPTH_2):
        kind, j = i % N_MIXERS, i // N_MIXERS
        h = _rmsnorm(x, norm1[i])
        if kind == 0:
            m = _retention_mixer(h, ret_w_in[j], ret_w_out[j])
        elif kind == 1:
            m = _moba_mixer(h, moba_w_in[j], moba_q_norm[j], moba_k_norm[j], moba_w_out[j], rel_bias)
        else:
            lambda_init = 0.8 - 0.6 * math.exp(-0.3 * i)
            m = _diff_mixer(h, diff_w_in[j], diff_q_norm[j], diff_k_norm[j], diff_lambda[j],
                            diff_subln[j], diff_w_out[j], rel_bias, lambda_init)
        x = x + m
        x = x + _squared_relu_mlp(_rmsnorm(x, norm2[i]), w_up[i], w_down[i])
    return x


def setup_inputs(seed=0):
    out = dict(first_inputs(seed))
    for name, value in second_inputs(seed + 1).items():
        if name != "x":
            out[name + "_2"] = value
    return out


def reference(
    x, c, ctx, c_ctx, w_mod, b_mod, g_ffn1, w_ffn1_gu, w_ffn1_down, g_mix, g_ffn2, w_ffn2_gu,
    w_ffn2_down, g_final, w_in_ab, g_v, w_s, b_s, w_out_ab, w_qkv, g_q, g_k, w_o, rel_bias_2,
    norm1_2, norm2_2, w_up_2, w_down_2, ret_w_in_2, ret_w_out_2, moba_w_in_2, moba_q_norm_2,
    moba_k_norm_2, moba_w_out_2, diff_w_in_2, diff_q_norm_2, diff_k_norm_2, diff_lambda_2,
    diff_subln_2, diff_w_out_2,
):
    x = first_block(
        x, c, ctx, c_ctx, w_mod, b_mod, g_ffn1, w_ffn1_gu, w_ffn1_down, g_mix, g_ffn2,
        w_ffn2_gu, w_ffn2_down, g_final, w_in_ab, g_v, w_s, b_s, w_out_ab, w_qkv, g_q, g_k, w_o,
    )
    return second_block(
        x, rel_bias_2, norm1_2, norm2_2, w_up_2, w_down_2, ret_w_in_2, ret_w_out_2, moba_w_in_2,
        moba_q_norm_2, moba_k_norm_2, moba_w_out_2, diff_w_in_2, diff_q_norm_2, diff_k_norm_2,
        diff_lambda_2, diff_subln_2, diff_w_out_2,
    )


_drawn_inputs = setup_inputs


def setup_inputs(seed=0):
    import zlib

    import numpy as np

    out = dict(_drawn_inputs(seed))
    spreads = {}
    factors = {'g_ffn1': 2.993,
     'g_ffn2': 3.191,
     'g_v': 8.0,
     'b_s': 8.0,
     'g_q': 8.0,
     'g_k': 8.0,
     'moba_q_norm_2': 8.0,
     'moba_k_norm_2': 8.0,
     'diff_q_norm_2': 8.0,
     'diff_k_norm_2': 8.0,
     'diff_subln_2': 21.648}
    for name, (base, spread) in spreads.items():
        noise = np.random.default_rng([zlib.crc32(name.encode()), seed]).standard_normal(out[name].shape)
        drawn = base * np.exp(spread * noise) if base else spread * noise
        out[name] = __import__('jax').numpy.asarray(drawn.astype(out[name].dtype))
    for name, factor in factors.items():
        out[name] = (out[name] * factor).astype(out[name].dtype)
    return out
```

```python
import concourse.bass as bass
from concourse import mybir
from contextlib import ExitStack, contextmanager

F32 = mybir.dt.float32
F32R = mybir.dt.float32r
ALU = mybir.AluOpType
ACT = mybir.ActivationFunctionType
AX = mybir.AxisListType.X

P = 128
D = 1024
KT = D // P
SEQ = 256
TT = SEQ // P
FF_T = 22
FF2_T = 32
N_MOD = 9
EPS = 1e-6
RING = 4
UNIT = 2048
LAMBDA_INIT = 0.8 - 0.6 * 2.718281828459045 ** (-0.3 * 2)

V_FFN1, V_MIX, V_FFN2, V_FINAL, V_N1, V_N2 = 0, 16, 32, 48, 56, 88
V_GV, V_GQ, V_GK, V_MQ, V_MK, V_DQ, V_DK, V_SUB = 120, 124, 125, 126, 127, 128, 129, 130
V_C, V_BMOD, V_PAIR, V_N = 131, 147, 147 + 2 * 72, 147 + 2 * 72 + 2

A_OUT = 2048


class Track:

    def __init__(self, eng):
        self.eng = eng
        self.count, self.per, self.reg = {}, {}, None

    def value(self, name):
        v = self.count.get(name, 0)
        if self.reg is not None and self.per.get(name, 0):
            return self.reg * self.per[name] + v
        return v

    def add(self, name, n=1):
        self.count[name] = self.count.get(name, 0) + n

    def due(self, name, n=1):
        self.add(name, n)
        return self.now(name)

    def at(self, name, total):
        self.count[name] = total
        return self.now(name)

    def now(self, name):
        assert self.count.get(name, 0) > 0, name
        return self.value(name)

    def begun(self, name):
        return self.count.get(name, 0) > 0

    def sent(self, name, n=1):
        self.add(name, n)
        return n

    @contextmanager
    def loop(self, n, per):
        before = dict(self.count)
        assert self.reg is None
        with self.eng.Fori(0, n) as i:
            self.reg, self.per = i, per
            yield i
            self.reg = None
        made = {k: v - before.get(k, 0) for k, v in self.count.items() if v != before.get(k, 0)}
        assert made == {k: v for k, v in per.items() if v}, (made, per)
        for k, v in made.items():
            self.count[k] += v * (n - 1)


class Gemm:

    def __init__(self, name, kt, tiles, mode, kind, src, **kw):
        self.name, self.kt, self.tiles, self.mode, self.kind, self.src = name, kt, tiles, mode, kind, src
        self.kw = kw
        if kind == "mod":
            self.nb, self.units, self.parts, self.group = 16, tiles // 2, 1, 4
        elif kt == 8:
            self.nb, self.units, self.parts, self.group = 16, tiles // 2, 2, 4
        elif kt == 16:
            self.nb, self.units, self.parts, self.group = 16, tiles, 1, 4
        else:
            self.nb, self.units, self.parts, self.group = kt // 2, tiles * 2, 1, 8
        self.half = (self.nb + 1) // 2


def gemm_list():
    out = []

    def add(*a, **kw):
        out.append(Gemm(*a, **kw))
        return out[-1]

    for l in range(2):
        add("mod", 8, 72, "mod", "mod", "act", l=l)
    add("gu1_0", 8, 44, "wide", "glu", "h")
    add("down1_0", 22, 8, "wide", "res", "act", gate=(0, 2))
    add("in_ab", 8, 12, "wide", "plain", "h", at=A_OUT, w=512)
    add("out_ab", 8, 8, "wide", "res", "h", gate=(0, 5))
    add("gu2_0", 8, 44, "wide", "glu", "h")
    add("down2_0", 22, 8, "wide", "res", "act", gate=(0, 8))
    add("gu1_1", 8, 44, "wide", "glu", "h")
    add("down1_1", 22, 8, "wide", "res", "act", gate=(1, 2))
    add("q", 8, 8, "xonly", "plain", "h", at=A_OUT, w=256)
    add("kv", 8, 4, "wide", "plain", "h", at=A_OUT + 2048, w=512)
    add("o", 8, 8, "cat", "res", "h", gate=(1, 5))
    add("gu2_1", 8, 44, "cat", "glu", "h")
    add("down2_1", 22, 8, "cat", "res", "act", gate=(1, 8))
    for i in range(4):
        if i % 3 == 0:
            add(f"ret_in{i // 3}", 8, 48, "cat", "plain", "h", at=A_OUT, w=256)
            add(f"ret_out{i // 3}", 16, 8, "cat", "res", "h", gate=None)
        elif i == 1:
            add("moba_in", 8, 24, "cat", "plain", "h", at=A_OUT, w=256)
            add("moba_out", 8, 8, "cat", "res", "h", gate=None)
        else:
            add("diff_in", 8, 24, "cat", "plain", "h", at=A_OUT, w=256)
            add("diff_out", 8, 8, "cat", "res", "h", gate=None)
        add(f"up{i}", 8, 32, "cat", "relu2", "h")
        add(f"down{i}", 32, 8, "cat", "res", "act", gate=None)
    u = s = 0
    for g in out:
        g.u0, g.s0 = u, s
        u += g.units
        s += g.units
    return out


class Program:
    def __init__(self, nc, io):
        self.nc, self.io = nc, io
        self.gemms = gemm_list()
        self.by_name = {g.name + (str(g.kw["l"]) if g.name == "mod" else ""): g for g in self.gemms}
        mixer = {"out_ab": 12, "o": 16, "ret_out0": 16, "ret_out1": 16, "moba_out": 16, "diff_out": 8}
        h, a, tiles = 0, 1, 0
        self.h_total, self.act_total, self.evacuated = {}, {}, {}
        for g in self.gemms:
            if g.kind == "mod":
                continue
            if g.src == "h":
                h += mixer.get(g.name, 0 if g.name == "kv" else 16 if g.mode in ("wide", "xonly") else 8)
                self.h_total[g.name] = h
            else:
                a += g.kt
                self.act_total[g.name] = a
            tiles += g.tiles
            self.evacuated[g.name] = 4 + tiles
        self.x_tiles = sum(g.tiles for g in self.gemms if g.kind == "res")
        self.split = [(g, k) for g in self.gemms for k in range(g.units)]

    def allocate(self, ctx):
        nc = self.nc

        def sb(name, cols, dt=F32):
            return ctx.enter_context(nc.sbuf_tensor(name, [P, cols], dt))

        here = -(-nc.sbuf_base // 32) * 32
        self.ar = sb("arena", 22528)
        self.act = nc.alloc_sbuf_tensor_at("act_parts", [P, 22528], F32R, offset=here)
        self.h = sb("h_parts", 8192, F32R)
        self.raw = [sb(f"raw{k}", UNIT) for k in range(RING)]
        self.wh = [sb(f"w_hi{k}", UNIT, F32R) for k in range(2)]
        self.wl = [sb(f"w_lo{k}", UNIT, F32R) for k in range(2)]
        self.x = sb("x_stream", KT * SEQ)
        self.ctx_ = sb("ctx_stream", KT * SEQ)
        self.ones = sb("ones", P)
        self.ident = sb("ident", P)
        self.mods = [sb(f"mods{l}", 144) for l in range(2)]
        self.vec = sb("vectors", V_N)
        self.tmp = sb("tmp", 1024)
        self.c_parts = sb("c_parts", 4 * KT, F32R)
        self.dist_bias = nc.dram_tensor("dist_bias", (P, 16, 2 * SEQ - 1), F32)
        self.mhalf = sb("minus_half", 64)
        self.ms = sb("mean_square", 2)
        self.rstd = sb("rstd", 2)
        ps = [ctx.enter_context(nc.psum_tensor(f"ps{k}", [P, 512], F32)) for k in range(8)]
        self.acc, self.X = ps[:4], ps[4:]
        self.loaded = ctx.enter_context(nc.semaphore("loaded"))
        self.mod_done = ctx.enter_context(nc.semaphore("mod_done"))
        self.rows_ready = ctx.enter_context(nc.semaphore("rows_ready"))
        self.table_ready = ctx.enter_context(nc.semaphore("table_ready"))
        self.table_done = ctx.enter_context(nc.semaphore("table_done"))
        self.table_taken = ctx.enter_context(nc.semaphore("table_taken"))
        self.table_kept = ctx.enter_context(nc.semaphore("table_kept"))
        self.wh_ready = ctx.enter_context(nc.semaphore("wh_ready"))
        self.wl_ready = ctx.enter_context(nc.semaphore("wl_ready"))
        self.acc_done = ctx.enter_context(nc.semaphore("acc_done"))
        self.bank_free = ctx.enter_context(nc.semaphore("bank_free"))
        self.lo_ready = ctx.enter_context(nc.semaphore("lo_ready"))
        self.th_ready = ctx.enter_context(nc.semaphore("th_ready"))
        self.glu_ready = ctx.enter_context(nc.semaphore("glu_ready"))
        self.x_ready = ctx.enter_context(nc.semaphore("x_ready"))
        self.h_ready = ctx.enter_context(nc.semaphore("h_ready"))
        self.sq_ready = ctx.enter_context(nc.semaphore("sq_ready"))
        self.stat_ready = ctx.enter_context(nc.semaphore("stat_ready"))
        self.ms_ready = ctx.enter_context(nc.semaphore("ms_ready"))
        self.rstd_ready = ctx.enter_context(nc.semaphore("rstd_ready"))
        self.diag_ready = ctx.enter_context(nc.semaphore("diag_ready"))
        self.bc_ready = ctx.enter_context(nc.semaphore("bc_ready"))
        self.xn_ready = ctx.enter_context(nc.semaphore("xn_ready"))
        self.y_ready = ctx.enter_context(nc.semaphore("y_ready"))
        self.dve_seq = ctx.enter_context(nc.semaphore("dve_seq"))
        self.act_seq = ctx.enter_context(nc.semaphore("act_seq"))
        self.pool_seq = ctx.enter_context(nc.semaphore("pool_seq"))
        self.mods_ready = ctx.enter_context(nc.semaphore("mods_ready"))
        self.csq_ready = ctx.enter_context(nc.semaphore("csq_ready"))
        self.csil_ready = ctx.enter_context(nc.semaphore("csil_ready"))
        self.cst_ready = ctx.enter_context(nc.semaphore("cst_ready"))
        self.gelu_a = ctx.enter_context(nc.semaphore("gelu_a"))
        self.gelu_b = ctx.enter_context(nc.semaphore("gelu_b"))
        self.gelu_c = ctx.enter_context(nc.semaphore("gelu_c"))
        self.gelu_d = ctx.enter_context(nc.semaphore("gelu_d"))
        self.y_done = ctx.enter_context(nc.semaphore("y_done"))
        self.yev_ready = ctx.enter_context(nc.semaphore("yev_ready"))
        self.fo_done = ctx.enter_context(nc.semaphore("fo_done"))
        self.vt_done = ctx.enter_context(nc.semaphore("vt_done"))
        self.vt_ready = ctx.enter_context(nc.semaphore("vt_ready"))
        self.mix_done = ctx.enter_context(nc.semaphore("mix_done"))
        self.qg_ready = ctx.enter_context(nc.semaphore("qg_ready"))
        self.rot_done = ctx.enter_context(nc.semaphore("rot_done"))
        self.rope_ready = ctx.enter_context(nc.semaphore("rope_ready"))
        self.rt_done = ctx.enter_context(nc.semaphore("rt_done"))
        self.rt_ready = ctx.enter_context(nc.semaphore("rt_ready"))
        self.hb_done = ctx.enter_context(nc.semaphore("hb_done"))
        self.s_done = ctx.enter_context(nc.semaphore("s_done"))
        self.nm_ready = ctx.enter_context(nc.semaphore("nm_ready"))
        self.p_ready = ctx.enter_context(nc.semaphore("p_ready"))
        self.pn_ready = ctx.enter_context(nc.semaphore("pn_ready"))
        self.t_done = ctx.enter_context(nc.semaphore("t_done"))
        self.pt_ready = ctx.enter_context(nc.semaphore("pt_ready"))
        self.pv_done = ctx.enter_context(nc.semaphore("pv_done"))
        self.o_evac = ctx.enter_context(nc.semaphore("o_evac"))
        self.b_done = ctx.enter_context(nc.semaphore("b_done"))
        self.b_ready = ctx.enter_context(nc.semaphore("b_ready"))
        self.rk_ready = ctx.enter_context(nc.semaphore("rk_ready"))
        self.st_done = ctx.enter_context(nc.semaphore("st_done"))
        self.st_ready = ctx.enter_context(nc.semaphore("st_ready"))
        self.od_done = ctx.enter_context(nc.semaphore("od_done"))
        self.silu_a = ctx.enter_context(nc.semaphore("silu_a"))
        self.g_ready = ctx.enter_context(nc.semaphore("g_ready"))
        self.lam_a = ctx.enter_context(nc.semaphore("lam_a"))
        self.lam_ready = ctx.enter_context(nc.semaphore("lam_ready"))
        self.stored = ctx.enter_context(nc.semaphore("stored"))
        self.rel_ready = ctx.enter_context(nc.semaphore("rel_ready"))
        self.og_ready = ctx.enter_context(nc.semaphore("og_ready"))
        self.kr_ready = ctx.enter_context(nc.semaphore("kr_ready"))
        self.ost_ready = ctx.enter_context(nc.semaphore("ost_ready"))
        self.raw_full = [ctx.enter_context(nc.semaphore(f"raw_full{k}")) for k in range(RING)]

    def sync_program(self, sp):
        t = Track(sp)
        io = self.io
        for dst, src in ((self.vec, io["vectors"]), (self.ones, io["ones"]), (self.ident, io["ident"]),
                         (self.x, io["x"]), (self.ctx_, io["ctx"])):
            sp.dma_start(dst[:], src).then_inc(self.loaded, t.sent("loaded", 16))

        def load(g, k, src):
            u = g.u0 + k
            if u >= RING:
                sp.wait_ge(self.wl_ready, t.due("wl_ready", 2))
            slot = u % RING
            sp.dma_start(
                self.raw[slot][:, 0:g.nb * P], src) \
                .then_inc(self.raw_full[slot], t.sent(f"raw_full{slot}", 16))

        for g in self.gemms:
            w = io[g.name + str(g.kw["l"])] if g.name == "mod" else io[g.name]
            for k in range(min(RING, g.units)):
                load(g, k, w[k])
            n = (g.units - RING) // RING
            if n > 0:
                per = {f"raw_full{k}": 16 for k in range(RING)}
                per["wl_ready"] = RING * 2
                with t.loop(n, per) as i:
                    for k in range(RING):
                        load(g, RING + k, w[bass.ds(i * RING + (RING + k), 1)].rearrange("o p n -> (o p) n"))
            for k in range(RING + max(n, 0) * RING, g.units):
                load(g, k, w[k])
        sp.wait_ge(self.x_ready, t.due("x_ready", self.x_tiles))
        sp.dma_start(io["out"], self.x[:]).then_inc(self.stored, t.sent("stored", 16))
        sp.wait_ge(self.stored, t.now("stored"))

    def act_split(self, t, s, gate=None):
        act = t.eng
        if s >= len(self.split):
            return
        g, k = self.split[s]
        slot, w = (g.u0 + k) % RING, s % 2
        act.wait_ge(self.raw_full[slot], t.due(f"raw_full{slot}", 16))
        for a, b in ((0, g.half), (g.half, g.nb)):
            self.nc.scalar.activation(
                self.wh[w][:, a * P:b * P], self.raw[slot][:, a * P:b * P], ACT.Copy) \
                .then_inc(self.wh_ready, t.sent("wh_ready"))

    def dve_split(self, t, s):
        dve = t.eng
        if s >= len(self.split):
            return
        g, k = self.split[s]
        slot, w = (g.u0 + k) % RING, s % 2
        for a, b in ((0, g.half), (g.half, g.nb)):
            dve.wait_ge(self.wh_ready, t.due("wh_ready"))
            self.nc.vector.tensor_tensor(
                self.wl[w][:, a * P:b * P], self.raw[slot][:, a * P:b * P],
                self.wh[w][:, a * P:b * P].bitcast(F32), ALU.subtract).then_inc(self.wl_ready, t.sent("wl_ready"))

    def raw_per(self, g):
        return {f"raw_full{k}": 16 * g.group // RING for k in range(RING)}

    def pe_gemm(self, t, name):
        pe = t.eng
        g = self.by_name[name]
        nc = self.nc
        src = self.act if g.src == "act" else self.h

        def block(bank, w, blk, kt, first, last):
            hi, lo = self.wh[w][:, blk * P:blk * P + P], self.wl[w][:, blk * P:blk * P + P]
            acc = self.acc[bank]
            if g.mode == "cat":
                prods = [(acc[:, 0:512], hi, src[:, kt * 512:kt * 512 + 512]),
                         (acc[:, 0:256], lo, src[:, kt * 512:kt * 512 + 256])]
            else:
                n = 256 if g.mode == "xonly" else 512
                a_hi, a_lo = src[:, kt * 1024:kt * 1024 + n], src[:, kt * 1024 + 512:kt * 1024 + 512 + n]
                prods = [(acc[:, 0:n], hi, a_hi), (acc[:, 0:n], lo, a_hi), (acc[:, 0:n], hi, a_lo)]
            if last:
                prods = prods[1:] + prods[:1]
            for j, (o, wgt, mov) in enumerate(prods):
                ins = nc.tensor.matmul(o, wgt, mov, start=first and j == 0, stop=last and j == len(prods) - 1)
            return ins

        def unit(k):
            w = (g.s0 + k) % 2
            if g.kt == 8:
                for j in range(2):
                    pe.wait_ge(self.bank_free, t.due("bank_free"))
                    pe.wait_ge(self.wl_ready, t.due("wl_ready"))
                    for kt in range(8):
                        ins = block((2 * k + j) % 4, w, 8 * j + kt, kt, kt == 0, kt == 7)
                    ins.then_inc(self.acc_done, t.sent("acc_done"))
            else:
                per_tile = g.kt // g.nb
                tile, part = k // per_tile, k % per_tile
                if part == 0:
                    pe.wait_ge(self.bank_free, t.due("bank_free"))
                for a, b in ((0, g.half), (g.half, g.nb)):
                    pe.wait_ge(self.wl_ready, t.due("wl_ready"))
                    for blk in range(a, b):
                        kt = part * g.nb + blk
                        ins = block(tile % 4, w, blk, kt, kt == 0, kt == g.kt - 1)
                ins.then_inc(self.acc_done, t.sent("acc_done"))

        if g.src == "h":
            pe.wait_ge(self.h_ready, t.at("h_ready", self.h_total[g.name]))
        else:
            pe.wait_ge(self.glu_ready, t.at("glu_ready", self.act_total[g.name]))
        n = g.units // g.group
        if n > 1:
            tiles = g.group * g.tiles // g.units
            with t.loop(n, {"bank_free": tiles, "wl_ready": 2 * g.group, "acc_done": g.parts * g.group}):
                for k in range(g.group):
                    unit(k)
        else:
            n = 0
        for k in range(n * g.group, g.units):
            unit(k)

    def act_gemm(self, t, name):
        act = t.eng
        g = self.by_name[name]
        nc, tmp = self.nc, self.tmp
        if g.s0 == 0:
            self.act_split(t, 0)
            self.act_split(t, 1)

        def unit(k):
            act.wait_ge(self.acc_done, t.due("acc_done", g.parts))
            if g.kind == "mod" and k % 2:
                group = k // 2 % 2
                nc.scalar.activation(
                    self.ar[0:4, 512 * group:512 * group + 512], self.acc[group][0:4, :], ACT.Copy) \
                    .then_inc(self.rows_ready, t.sent("rows_ready"))
            self.act_split(t, g.s0 + k + 2)
            per_tile = g.kt // g.nb if g.kt > 16 else 1
            if g.kind == "mod" or k % per_tile != per_tile - 1:
                return
            tile0 = 2 * k if g.kt == 8 else k // per_tile
            tiles = 2 if g.kt == 8 else 1
            if g.kind == "glu" and g.mode == "wide":
                act.wait_ge(self.glu_ready, t.now("glu_ready"))
                nc.scalar.activation(
                    tmp[:, 0:512], self.acc[tile0 % 4][:], ACT.Tanh, scale=0.5) \
                    .then_inc(self.th_ready, t.sent("th_ready"))
                t.add("glu_ready")
                return
            if g.mode != "cat":
                return
            used = {"plain": "bank_free", "res": "x_ready", "glu": "glu_ready", "relu2": "glu_ready"}[g.kind]
            if used == "glu_ready":
                act.wait_ge(self.glu_ready, t.now("glu_ready"))
            elif used == "x_ready":
                act.wait_ge(self.x_ready, t.now("x_ready"))
            else:
                act.wait_ge(self.bank_free, t.now("bank_free"))
            for j in range(tiles):
                nc.scalar.activation(
                    tmp[:, j * 256:j * 256 + 256], self.acc[(tile0 + j) % 4][:, 256:512], ACT.Copy) \
                    .then_inc(self.lo_ready, t.sent("lo_ready"))
            t.add(used, 1 if g.kind == "glu" else tiles)
            if g.kind == "glu":
                act.wait_ge(self.g_ready, t.due("g_ready"))
                nc.scalar.activation(
                    tmp[:, 512:768], tmp[:, 0:256], ACT.Tanh, scale=0.5).then_inc(self.th_ready, t.sent("th_ready"))

        n = (g.units - 2) // g.group
        if n > 1:
            per = self.raw_per(g)
            per["wh_ready"] = 2 * g.group
            per["acc_done"] = g.parts * g.group
            if g.kind == "glu":
                per["glu_ready"] = per["th_ready"] = g.group
            if g.kind == "mod":
                per["rows_ready"] = 2
            if g.mode == "cat":
                tiles = g.group * g.tiles // g.units
                per["lo_ready"] = tiles
                if g.kind == "glu":
                    per["g_ready"] = g.group
                else:
                    per[{"plain": "bank_free", "res": "x_ready", "relu2": "glu_ready"}[g.kind]] = tiles
            with t.loop(n, per):
                for k in range(g.group):
                    unit(k)
        else:
            n = 0
        for k in range(n * g.group, g.units):
            unit(k)
        if g.kind != "mod" and not (g.mode == "cat" and g.kind == "plain"):
            t.add("bank_free", g.tiles)
        if g.kind == "res" and g.mode == "wide":
            t.add("x_ready", g.tiles)

    def dve_gemm(self, t, name):
        dve = t.eng
        g = self.by_name[name]
        nc, tmp, v = self.nc, self.tmp, self.nc.vector
        if g.s0 == 0:
            self.dve_split(t, 0)
            self.dve_split(t, 1)

        def cols(tensor, base, stride, k, n):
            if t.reg is None:
                return tensor[:, base + stride * k:base + stride * k + n]
            return tensor[:, bass.ds(t.reg * (stride * step) + (base + stride * k), n)]

        def unit(k):
            dve.wait_ge(self.acc_done, t.due("acc_done", g.parts))
            self.dve_split(t, g.s0 + k + 2)
            per_tile = g.kt // g.nb if g.kt > 16 else 1
            if g.kind == "mod" or k % per_tile != per_tile - 1:
                return
            tile0 = 2 * k if g.kt == 8 else k // per_tile
            tiles = 2 if g.kt == 8 else 1
            banks = [self.acc[(tile0 + j) % 4] for j in range(tiles)]
            if g.kind == "glu":
                w = 512 if g.mode == "wide" else 256
                if g.mode == "wide":
                    gate, up, th, a = banks[0][:], banks[1][:], tmp[:, 0:512], tmp[:, 512:1024]
                else:
                    gate, up, th, a = tmp[:, 0:256], tmp[:, 256:512], tmp[:, 512:768], tmp[:, 768:1024]
                    dve.wait_ge(self.lo_ready, t.due("lo_ready"))
                    v.tensor_tensor(
                        gate, banks[0][:, 0:256], gate, ALU.add).then_inc(self.bank_free, t.sent("bank_free"))
                    dve.wait_ge(self.bank_free, t.now("bank_free"))
                    dve.wait_ge(self.lo_ready, t.due("lo_ready"))
                    v.tensor_tensor(up, banks[1][:, 0:256], up, ALU.add).then_inc(self.bank_free, t.sent("bank_free"))
                    dve.wait_ge(self.bank_free, t.now("bank_free"))
                    v.memset(self.ms[:, 0:1], 0.0).then_inc(self.g_ready, t.sent("g_ready"))
                dve.wait_ge(self.th_ready, t.due("th_ready"))
                if g.mode == "wide":
                    v.scalar_tensor_tensor(
                        th, th, 1.0, gate, ALU.add, ALU.mult).then_inc(self.bank_free, t.sent("bank_free"))
                    dve.wait_ge(self.bank_free, t.now("bank_free"))
                    v.scalar_tensor_tensor(
                        a, th, 0.5, up, ALU.mult, ALU.mult).then_inc(self.bank_free, t.sent("bank_free"))
                    dve.wait_ge(self.bank_free, t.now("bank_free"))
                else:
                    v.scalar_tensor_tensor(
                        th, th, 1.0, gate, ALU.add, ALU.mult).then_inc(self.dve_seq, t.sent("dve_seq"))
                    dve.wait_ge(self.dve_seq, t.now("dve_seq"))
                    v.scalar_tensor_tensor(
                        a, th, 0.5, up, ALU.mult, ALU.mult).then_inc(self.dve_seq, t.sent("dve_seq"))
                    dve.wait_ge(self.dve_seq, t.now("dve_seq"))
                stride = 2 * w
                hi, lo = cols(self.act, 0, stride, k, w), cols(self.act, w, stride, k, w)
                v.tensor_copy(hi, a).then_inc(self.dve_seq, t.sent("dve_seq"))
                dve.wait_ge(self.dve_seq, t.now("dve_seq"))
                v.tensor_tensor(lo, a, hi.bitcast(F32), ALU.subtract).then_inc(self.glu_ready, t.sent("glu_ready"))
                dve.wait_ge(self.glu_ready, t.now("glu_ready"))
                return
            for j in range(tiles):
                tile, bank = tile0 + j, banks[j]
                lo_sum = tmp[:, j * 256:j * 256 + 256]
                if g.mode == "cat":
                    dve.wait_ge(self.lo_ready, t.due("lo_ready"))
                if g.kind == "plain":
                    w = g.kw["w"]
                    dst = cols(self.ar, g.kw["at"], w, tile, w)
                    if g.mode == "cat":
                        v.tensor_tensor(
                            dst, bank[:, 0:256], lo_sum, ALU.add).then_inc(self.bank_free, t.sent("bank_free"))
                    else:
                        v.tensor_copy(dst, bank[:, 0:w]).then_inc(self.bank_free, t.sent("bank_free"))
                elif g.kind == "relu2":
                    v.tensor_tensor(
                        lo_sum, bank[:, 0:256], lo_sum, ALU.add).then_inc(self.bank_free, t.sent("bank_free"))
                    dve.wait_ge(self.bank_free, t.now("bank_free"))
                    a = tmp[:, 512 + j * 256:768 + j * 256]
                    v.scalar_tensor_tensor(
                        a, lo_sum, 0.0, lo_sum, ALU.max, ALU.mult).then_inc(self.dve_seq, t.sent("dve_seq"))
                    dve.wait_ge(self.dve_seq, t.now("dve_seq"))
                    hi, lo = cols(self.act, 0, 512, tile, 256), cols(self.act, 256, 512, tile, 256)
                    v.tensor_copy(hi, a).then_inc(self.dve_seq, t.sent("dve_seq"))
                    dve.wait_ge(self.dve_seq, t.now("dve_seq"))
                    v.tensor_tensor(
                        lo, a, hi.bitcast(F32), ALU.subtract).then_inc(self.glu_ready, t.sent("glu_ready"))
                    dve.wait_ge(self.glu_ready, t.now("glu_ready"))
                else:
                    x = self.x[:, tile * 256:tile * 256 + 256]
                    if g.mode == "wide":
                        l, m = g.kw["gate"]
                        for s, res in ((0, self.x), (1, self.ctx_)):
                            r = res[:, tile * 256:tile * 256 + 256]
                            gate = self.mods[l][:, (m * 8 + tile) * 2 + s:(m * 8 + tile) * 2 + s + 1]
                            ins = v.scalar_tensor_tensor(
                                r, bank[:, s * 256:s * 256 + 256], gate, r, ALU.mult, ALU.add)
                            if s:
                                ins.then_inc(self.bank_free, t.sent("bank_free"))
                            else:
                                ins.then_inc(self.x_ready, t.sent("x_ready"))
                        continue
                    v.tensor_tensor(
                        lo_sum, bank[:, 0:256], lo_sum, ALU.add).then_inc(self.bank_free, t.sent("bank_free"))
                    dve.wait_ge(self.bank_free, t.now("bank_free"))
                    if g.kw["gate"]:
                        l, m = g.kw["gate"]
                        gate = self.mods[l][:, (m * 8 + tile) * 2:(m * 8 + tile) * 2 + 1]
                        v.scalar_tensor_tensor(
                            x, lo_sum, gate, x, ALU.mult, ALU.add).then_inc(self.x_ready, t.sent("x_ready"))
                    else:
                        v.tensor_tensor(x, lo_sum, x, ALU.add).then_inc(self.x_ready, t.sent("x_ready"))

        n, step = (g.units - 2) // g.group, g.group * g.tiles // g.units
        if g.kind == "glu":
            step = g.group
        if n > 1 and g.kind != "res":
            per = {"wh_ready": 2 * g.group, "wl_ready": 2 * g.group, "acc_done": g.parts * g.group}
            tiles = g.group * g.tiles // g.units
            if g.kind != "mod":
                per["bank_free"] = tiles
            if g.mode == "cat":
                per["lo_ready"] = tiles
            if g.kind == "glu":
                per["glu_ready"] = per["th_ready"] = g.group
                per["dve_seq"] = g.group * (1 if g.mode == "wide" else 3)
                if g.mode == "cat":
                    per["g_ready"] = g.group
            if g.kind == "relu2":
                per["glu_ready"] = tiles
                per["dve_seq"] = 2 * tiles
            with t.loop(n, per):
                for k in range(g.group):
                    unit(k)
        else:
            n = 0
        for k in range(n * g.group, g.units):
            unit(k)
        dve.wait_ge(self.bank_free, t.now("bank_free"))

    T_OH, T_REL, T_OUT = 1024, 1536, 2048

    def pe_start(self, t):
        pe = t.eng
        pe.wait_ge(self.table_ready, t.due("table_ready", 2 * 16))
        pe.wait_ge(self.rel_ready, t.due("rel_ready"))
        self.nc.tensor.matmul(self.X[3][0:16, 0:2 * SEQ - 1], self.a(self.T_REL, 16, 0, 33),
                              self.a(self.T_OH, 2 * SEQ - 1, 0, 33), start=True, stop=True) \
            .then_inc(self.table_done, t.sent("table_done"))

    def act_start(self, t):
        act = t.eng
        self.nc.scalar.dma_start(self.a(self.T_OH, 2 * SEQ - 1, 0, 33), self.io["bucket"]) \
            .then_inc(self.table_ready, t.sent("table_ready", 16))
        self.nc.scalar.dma_start(self.a(self.T_REL, 16, 0, 32), self.io["rel_bias"]) \
            .then_inc(self.table_ready, t.sent("table_ready", 16))
        act.wait_ge(self.loaded, t.due("loaded", 5 * 16))
        self.nc.scalar.activation(
            self.tmp[:, 16:32], self.vec[:, V_C:V_C + 16], ACT.Tanh, scale=0.5) \
            .then_inc(self.csq_ready, t.sent("csq_ready"))
        t.add("bank_free", 4)
        t.add("glu_ready")
        act.wait_ge(self.table_done, t.due("table_done"))
        self.nc.scalar.activation(
            self.a(self.T_OUT, 2 * SEQ - 1, 0, 16), self.X[3][0:16, 0:2 * SEQ - 1], ACT.Copy) \
            .then_inc(self.table_taken, t.sent("table_taken"))
        act.wait_ge(self.table_taken, t.now("table_taken"))
        rows = self.a(self.T_OUT, 2 * SEQ - 1, 0, 16).unsqueeze(1).broadcast_to([16, P, 2 * SEQ - 1])
        self.nc.scalar.dma_start(self.dist_bias[:].rearrange("p h m -> h p m"), rows) \
            .then_inc(self.table_kept, t.sent("table_kept", 16))

    def pool_start(self, t):
        pool = t.eng
        self.nc.gpsimd.memset(self.mhalf[:], -0.5).then_inc(self.pool_seq, t.sent("pool_seq"))
        pool.wait_ge(self.pool_seq, t.now("pool_seq"))

    def dve_start(self, t):
        dve = t.eng
        v = self.nc.vector
        v.memset(self.ms[:], 0.0).then_inc(self.bank_free, t.sent("bank_free", 4))
        v.memset(self.rstd[:], 0.0).then_inc(self.glu_ready, t.sent("glu_ready"))
        v.memset(self.a(self.T_REL, 16, 32, 33), -1e30).then_inc(self.rel_ready, t.sent("rel_ready"))
        dve.wait_ge(self.loaded, t.due("loaded", 5 * 16))
        dve.wait_ge(self.csq_ready, t.due("csq_ready"))
        th, c = self.tmp[:, 16:32], self.vec[:, V_C:V_C + 16]
        v.scalar_tensor_tensor(th, th, 1.0, c, ALU.add, ALU.mult).then_inc(self.dve_seq, t.sent("dve_seq"))
        dve.wait_ge(self.dve_seq, t.now("dve_seq"))
        sc = self.tmp[:, 0:16]
        v.tensor_scalar(sc, th, 0.5, None, ALU.mult).then_inc(self.dve_seq, t.sent("dve_seq"))
        dve.wait_ge(self.dve_seq, t.now("dve_seq"))
        parts = self.c_parts[:].rearrange("p (k h s) -> p k h s", k=KT, h=2)
        sc = sc.rearrange("p (k s) -> p k s", k=KT)
        v.tensor_copy(parts[:, :, 0, :], sc).then_inc(self.dve_seq, t.sent("dve_seq"))
        dve.wait_ge(self.dve_seq, t.now("dve_seq"))
        v.tensor_tensor(parts[:, :, 1, :], sc, parts[:, :, 0, :].bitcast(F32), ALU.subtract) \
            .then_inc(self.csil_ready, t.sent("csil_ready"))

    def pe_mod(self, t, l):
        pe = t.eng
        nc = self.nc
        if l == 0:
            pe.wait_ge(self.csil_ready, t.due("csil_ready"))
        pair = self.vec[0:4, V_PAIR:V_PAIR + 2]

        def unit(k):
            for half in range(2):
                pe.wait_ge(self.wl_ready, t.due("wl_ready"))
                for j in (2 * half, 2 * half + 1):
                    kt = 4 * (k % 2) + j
                    for w in (self.wh[k % 2], self.wl[k % 2]):
                        ins = nc.tensor.matmul(self.acc[k // 2][0:4, :], self.c_parts[:, 4 * kt:4 * kt + 4],
                                               w[:, 512 * j:512 * j + 512], start=kt == 0 and w is self.wh[k % 2],
                                               stop=kt == KT - 1 and w is self.wl[k % 2])
            ins.then_inc(self.acc_done, t.sent("acc_done"))

        def columns(g, i):
            pe.wait_ge(self.rows_ready, t.due("rows_ready"))
            for j in range(4):
                ins = nc.tensor.matmul(self.X[l][:, bass.ds(i * 16 + (8 * g + 2 * j), 2)],
                                       self.ar[0:4, 512 * g + P * j:512 * g + P * j + P], pair, start=True, stop=True)
            return ins

        with t.loop(9, {"wl_ready": 8, "acc_done": 4, "rows_ready": 2, "mod_done": 1}) as i:
            unit(0)
            unit(1)
            unit(2)
            columns(0, i)
            unit(3)
            columns(1, i).then_inc(self.mod_done, t.sent("mod_done"))

    def dve_mod(self, t, l):
        dve = t.eng
        g, v, m = self.by_name[f"mod{l}"], self.nc.vector, self.mods[l]
        dve.wait_ge(self.mod_done, t.due("mod_done", 9))
        b = self.vec[:, V_BMOD + 72 * l:V_BMOD + 72 * l + 72].unsqueeze(2).broadcast_to([P, 72, 2])
        v.tensor_tensor(
            m[:].rearrange("p (a b) -> p a b", b=2), self.X[l][:, 0:144].rearrange("p (a b) -> p a b", b=2), b,
            ALU.add).then_inc(self.dve_seq, t.sent("dve_seq"))
        dve.wait_ge(self.dve_seq, t.now("dve_seq"))
        for scale, gain, gate in ((1, V_FFN1, 2), (4, V_MIX, None), (7, V_FFN2, 8)):
            cut = m[:, scale * 16:scale * 16 + 16].rearrange("p (a b) -> p a b", b=2)
            gb = self.vec[:, gain + 8 * l:gain + 8 * l + 8].unsqueeze(2).broadcast_to([P, 8, 2])
            v.scalar_tensor_tensor(cut, cut, 1.0, gb, ALU.add, ALU.mult).then_inc(self.dve_seq, t.sent("dve_seq"))
            if gate:
                cut = m[:, gate * 16:gate * 16 + 16]
                v.tensor_scalar(cut, cut, 0.5, None, ALU.mult).then_inc(self.dve_seq, t.sent("dve_seq"))
        dve.wait_ge(self.dve_seq, t.now("dve_seq"))
        v.memset(self.ms[:, 0:1], 0.0).then_inc(self.mods_ready, t.sent("mods_ready"))
        dve.wait_ge(self.mods_ready, t.now("mods_ready"))

    def norm_cols(self, what, s):
        if what[0] == "mod":
            _, l, m = what
            return (lambda kt: self.mods[l][:, ((m + 1) * 8 + kt) * 2 + s:((m + 1) * 8 + kt) * 2 + s + 1],
                    lambda kt: self.mods[l][:, (m * 8 + kt) * 2 + s:(m * 8 + kt) * 2 + s + 1])
        return (lambda kt: self.vec[:, what[1] + kt:what[1] + kt + 1]), (lambda kt: 0.0)

    def norm_dst(self, wide, s, kt):
        if wide:
            return [self.h[:, kt * 1024 + 512 * p + 256 * s:kt * 1024 + 512 * p + 256 * s + 256] for p in (0, 1)]
        return [self.h[:, kt * 512 + 256 * p:kt * 512 + 256 * p + 256] for p in (0, 1)]

    def act_norm(self, t, what, s, wide):
        act = t.eng
        src = self.ctx_ if s else self.x
        nc = self.nc
        if what[0] == "mod":
            act.wait_ge(self.mods_ready, t.at("mods_ready", 2))
            act.wait_ge(self.table_kept, t.now("table_kept"))
        if t.begun("x_ready"):
            act.wait_ge(self.x_ready, t.now("x_ready"))
        act.wait_ge(self.bank_free, t.now("bank_free"))
        for kt in range(KT):
            nc.scalar.activation(
                self.ar[:, kt * 256:kt * 256 + 256], src[:, kt * 256:kt * 256 + 256], ACT.Square) \
                .then_inc(self.sq_ready, t.sent("sq_ready"))
        a, b = self.norm_cols(what, s)
        for kt in range(KT):
            y = self.tmp[:, kt % 3 * 256:kt % 3 * 256 + 256]
            act.wait_ge(self.xn_ready, t.due("xn_ready"))
            if what[0] == "final":
                nc.scalar.activation(
                    src[:, kt * 256:kt * 256 + 256], y, ACT.Identity, scale=a(kt)) \
                    .then_inc(self.y_ready, t.sent("y_ready"))
                continue
            nc.scalar.activation(
                y, y, ACT.Identity, scale=a(kt), bias=b(kt)).then_inc(self.act_seq, t.sent("act_seq"))
            act.wait_ge(self.act_seq, t.now("act_seq"))
            nc.scalar.activation(self.norm_dst(wide, s, kt)[0], y, ACT.Copy).then_inc(self.y_ready, t.sent("y_ready"))
        if what[0] == "final":
            act.wait_ge(self.y_ready, t.now("y_ready"))

    def pe_norm(self, t, what, s, wide):
        pe = t.eng
        nc = self.nc
        pe.wait_ge(self.sq_ready, t.due("sq_ready", KT))
        for tt in range(TT):
            for kt in range(KT):
                ins = nc.tensor.matmul(self.X[0][:, tt:tt + 1],
                                       self.ar[:, kt * 256 + tt * P:kt * 256 + tt * P + P], self.ones[:, 0:1],
                                       start=kt == 0, stop=kt == KT - 1)
        ins.then_inc(self.stat_ready, t.sent("stat_ready"))
        t.add("rstd_ready")
        pe.wait_ge(self.diag_ready, t.due("diag_ready"))
        for tt in range(TT):
            ins = nc.tensor.matmul(self.X[1][:, tt * P:tt * P + P], self.ones[:],
                                   self.tmp[:, 768 + tt * P:768 + tt * P + P], start=True, stop=True)
        ins.then_inc(self.bc_ready, t.sent("bc_ready"))

    def pool_norm(self, t):
        pool = t.eng
        pool.wait_ge(self.ms_ready, t.due("ms_ready"))
        self.nc.gpsimd.tensor_tensor(
            self.rstd[:], self.ms[:], self.mhalf[:, 0:2], ALU.pow).then_inc(self.rstd_ready, t.sent("rstd_ready"))

    def dve_norm(self, t, what, s, wide):
        dve = t.eng
        v, src = self.nc.vector, self.ctx_ if s else self.x
        dve.wait_ge(self.stat_ready, t.due("stat_ready"))
        dve.wait_ge(self.dve_seq, t.now("dve_seq"))
        v.tensor_scalar(
            self.ms[:], self.X[0][:, 0:2], 1.0 / D, EPS, ALU.mult, ALU.add) \
            .then_inc(self.ms_ready, t.sent("ms_ready"))
        dve.wait_ge(self.rstd_ready, t.due("rstd_ready"))
        for tt in range(TT):
            ins = v.tensor_scalar(self.tmp[:, 768 + tt * P:768 + tt * P + P], self.ident[:],
                                  self.rstd[:, tt:tt + 1], None, ALU.mult)
            if tt == TT - 1:
                ins.then_inc(self.diag_ready, t.sent("diag_ready"))
            else:
                ins.then_inc(self.dve_seq, t.sent("dve_seq"))
                dve.wait_ge(self.dve_seq, t.now("dve_seq"))
        dve.wait_ge(self.bc_ready, t.due("bc_ready"))
        if t.begun("x_ready"):
            dve.wait_ge(self.x_ready, t.now("x_ready"))
        dve.wait_ge(self.bank_free, t.now("bank_free"))

        def low(kt):
            y = self.tmp[:, kt % 3 * 256:kt % 3 * 256 + 256]
            dve.wait_ge(self.y_ready, t.due("y_ready"))
            if what[0] == "final":
                return
            hi, lo = self.norm_dst(wide, s, kt)
            v.tensor_tensor(lo, y, hi.bitcast(F32), ALU.subtract).then_inc(self.h_ready, t.sent("h_ready"))

        for kt in range(KT):
            if kt >= 3 and what[0] != "final":
                dve.wait_ge(self.h_ready, t.now("h_ready"))
            v.tensor_tensor(
                self.tmp[:, kt % 3 * 256:kt % 3 * 256 + 256], src[:, kt * 256:kt * 256 + 256], self.X[1][:, 0:256],
                ALU.mult).then_inc(self.xn_ready, t.sent("xn_ready"))
            if kt >= 2:
                low(kt - 2)
        low(KT - 2)
        low(KT - 1)
        dve.wait_ge(self.h_ready, t.now("h_ready"))

    def load_consts(self, t, parts):
        for dst, src in parts:
            self.nc.scalar.dma_start(dst, src).then_inc(self.cst_ready, t.sent("cst_ready", 16))

    def a(self, col, n, p0=0, p1=P):
        return self.ar[p0:p1, col:col + n]

    def dve_stat(self, t, src, dst, d, ready="stat_ready", n=1):
        dve = t.eng
        dve.wait_ge({"stat_ready": self.stat_ready, "ost_ready": self.ost_ready}[ready], t.due(ready, n))
        self.nc.vector.tensor_scalar(
            dst, src, 1.0 / d, EPS, ALU.mult, ALU.add).then_inc(self.ms_ready, t.sent("ms_ready"))
        dve.wait_ge(self.ms_ready, t.now("ms_ready"))

    def pool_stat(self, t, r, n):
        pool = t.eng
        pool.wait_ge(self.ms_ready, t.due("ms_ready"))
        self.nc.gpsimd.tensor_tensor(
            r, r, self.mhalf[:, 0:n], ALU.pow).then_inc(self.rstd_ready, t.sent("rstd_ready"))

    def dve_parts(self, t, y, hi, lo):
        dve = t.eng
        v = self.nc.vector
        v.tensor_copy(hi, y).then_inc(self.dve_seq, t.sent("dve_seq"))
        dve.wait_ge(self.dve_seq, t.now("dve_seq"))
        v.tensor_tensor(lo, y, hi.bitcast(F32), ALU.subtract).then_inc(self.h_ready, t.sent("h_ready"))

    def pe_transpose(self, out, in_):
        return self.nc.tensor.transpose(out, in_, self.ident[0:in_.shape[0], 0:in_.shape[0]])

    F_G, F_Y, F_CS, F_DN, F_VH, F_SQ, F_BS, F_WS, F_R = 8192, 9216, 13312, 13568, 14592, 16640, 18688, 19200, 19712

    def f_tile(self, t):
        return self.a(A_OUT + 512 * t, 512)

    def f_consts(self, t):
        io = self.io
        self.load_consts(t, [(self.a(self.F_CS, 256), io["dft_ch"]), (self.a(self.F_DN, 1024), io["dft_tok"]),
                             (self.a(self.F_WS, 512), io["w_s"]),
                             (self.a(self.F_BS, 512), io["b_s"].partition_broadcast(P))])

    def pe_fourier(self, t):
        pe = t.eng
        nc = self.nc
        pe.wait_ge(self.cst_ready, t.due("cst_ready", 4 * 16))
        pe.wait_ge(self.bank_free, t.now("bank_free") + 4)
        cs = self.a(self.F_CS, 256)
        for n in range(4):
            for half in range(2):
                k = 2 * n + half
                if k >= 2:
                    pe.wait_ge(self.yev_ready, t.due("yev_ready"))
                for gg in range(2):
                    g = 2 * half + gg
                    ins = nc.tensor.matmul(self.X[k % 2][:, gg * 256:gg * 256 + 256],
                                           self.a(A_OUT + 512 * g + n * P, P), cs, start=True, stop=True)
                ins.then_inc(self.y_done, t.sent("y_done"))
        pe.wait_ge(self.yev_ready, t.due("yev_ready", 2))
        h0 = self.h_total["in_ab"]
        for k in range(8):
            s, g = k // 4, k % 4
            if k >= 2:
                pe.wait_ge(self.h_ready, t.at("h_ready", h0 + k - 1))
            for tt in range(TT):
                y = self.F_Y + ((2 * s + tt) * 4 + g) * 256
                for part in range(2):
                    ins = nc.tensor.matmul(self.X[2 + k % 2][:, 0:256], self.a(y + part * P, P),
                                           self.a(self.F_DN + (2 * tt + part) * 256, 256),
                                           start=tt == 0 and part == 0, stop=tt == 1 and part == 1)
            ins.then_inc(self.fo_done, t.sent("fo_done"))
        pe.wait_ge(self.sq_ready, t.due("sq_ready", 4))
        for n in range(4):
            for g in range(4):
                ins = nc.tensor.matmul(self.X[0][:, 4 * n + g:4 * n + g + 1],
                                       self.a(self.F_SQ + 512 * g + n * P, P), self.ones[:, 0:1], start=True,
                                       stop=True)
        ins.then_inc(self.stat_ready, t.sent("stat_ready"))
        pe.wait_ge(self.ms_ready, t.at("ms_ready", 5))
        t.add("rstd_ready")
        for n in range(4):
            if n >= 2:
                pe.wait_ge(self.vt_ready, t.due("vt_ready"))
            for g in range(4):
                ins = self.pe_transpose(self.X[n % 2][:, g * P:g * P + P], self.a(A_OUT + 512 * (8 + g) + n * P, P))
            ins.then_inc(self.vt_done, t.sent("vt_done"))
        pe.wait_ge(self.vt_ready, t.due("vt_ready", 2))
        pe.wait_ge(self.h_ready, t.at("h_ready", h0 + 8))
        for g in range(4):
            if g >= 2:
                pe.wait_ge(self.h_ready, t.at("h_ready", h0 + 8 + g - 1))
            for n in range(4):
                ins = nc.tensor.matmul(self.X[2 + g % 2][:, n * P:n * P + P],
                                       self.a(self.F_VH + 512 * n + g * P, P), self.a(self.F_WS + g * P, P),
                                       start=True, stop=True)
            ins.then_inc(self.mix_done, t.sent("mix_done"))

    def act_fourier(self, t):
        act = t.eng
        nc = self.nc
        for k in range(8):
            act.wait_ge(self.y_done, t.due("y_done"))
            nc.scalar.activation(
                self.a(self.F_Y + 512 * k, 512), self.X[k % 2][:], ACT.Copy) \
                .then_inc(self.yev_ready, t.sent("yev_ready"))
        act.wait_ge(self.bank_free, t.at("bank_free", self.evacuated["in_ab"]))

        def tanh(k):
            act.wait_ge(self.gelu_b, t.due("gelu_b"))
            nc.scalar.activation(
                self.a(self.F_G + 512 * (k % 2), 512), self.a(self.F_G + 512 * (k % 2), 512), ACT.Tanh) \
                .then_inc(self.gelu_c, t.sent("gelu_c"))

        for k, tile in enumerate(self.GELU):
            if k >= 2:
                act.wait_ge(self.gelu_d, t.due("gelu_d"))
            nc.scalar.activation(
                self.a(self.F_G + 512 * (k % 2), 512), self.f_tile(tile), ACT.Square) \
                .then_inc(self.gelu_a, t.sent("gelu_a"))
            if k >= 1:
                tanh(k - 1)
            if 2 <= k < 6:
                nc.scalar.activation(
                    self.a(self.F_SQ + 512 * (k - 2), 512), self.f_tile(8 + k - 2), ACT.Square) \
                    .then_inc(self.sq_ready, t.sent("sq_ready"))
        tanh(7)
        act.wait_ge(self.gelu_d, t.due("gelu_d", 2))
        t.add("vt_done", 4)

    GELU = (8, 9, 10, 11, 4, 5, 6, 7)

    def dve_fourier(self, t):
        dve = t.eng
        v = self.nc.vector

        def poly(k):
            s, z = self.a(self.F_G + 512 * (k % 2), 512), self.f_tile(self.GELU[k])
            dve.wait_ge(self.gelu_a, t.due("gelu_a"))
            v.tensor_scalar(
                s, s, 0.044715 * 0.7978845608028654, 0.7978845608028654, ALU.mult, ALU.add) \
                .then_inc(self.dve_seq, t.sent("dve_seq"))
            dve.wait_ge(self.dve_seq, t.now("dve_seq"))
            v.tensor_tensor(s, s, z, ALU.mult).then_inc(self.gelu_b, t.sent("gelu_b"))

        def fin(k):
            s, z = self.a(self.F_G + 512 * (k % 2), 512), self.f_tile(self.GELU[k])
            dve.wait_ge(self.gelu_c, t.due("gelu_c"))
            v.scalar_tensor_tensor(z, s, 1.0, z, ALU.add, ALU.mult).then_inc(self.dve_seq, t.sent("dve_seq"))
            dve.wait_ge(self.dve_seq, t.now("dve_seq"))
            v.tensor_scalar(z, z, 0.5, None, ALU.mult).then_inc(self.gelu_d, t.sent("gelu_d"))

        for k in range(8):
            poly(k)
            if k >= 1:
                fin(k - 1)
        fin(7)
        for k in range(8):
            s, g = k // 4, k % 4
            dve.wait_ge(self.fo_done, t.due("fo_done"))
            hi, lo = self.norm_dst(True, s, g)
            self.dve_parts(t, self.X[2 + k % 2][:, 0:256], hi, lo)
        r = self.a(self.F_R, 16)
        self.dve_stat(t, self.X[0][:, 0:16], r, P)
        dve.wait_ge(self.rstd_ready, t.due("rstd_ready"))
        for n in range(4):
            dve.wait_ge(self.vt_done, t.due("vt_done"))
            v.tensor_tensor(
                self.a(self.F_VH + 512 * n, 512).rearrange("p (g d) -> p g d", g=4),
                self.X[n % 2][:].rearrange("p (g d) -> p g d", g=4),
                self.a(self.F_R + 4 * n, 4).unsqueeze(2).broadcast_to([P, 4, P]), ALU.mult) \
                .then_inc(self.vt_ready, t.sent("vt_ready"))
        dve.wait_ge(self.cst_ready, t.due("cst_ready", 4 * 16))
        dve.wait_ge(self.gelu_d, t.now("gelu_d"))
        for g in range(4):
            dve.wait_ge(self.mix_done, t.due("mix_done"))
            y = self.a(self.F_G + 512 * (g % 2), 512)
            bs = self.a(self.F_BS + g * P, P).unsqueeze(1).broadcast_to([P, 4, P])
            if g >= 2:
                dve.wait_ge(self.h_ready, t.now("h_ready"))
            v.scalar_tensor_tensor(
                y.rearrange("p (n d) -> p n d", n=4), self.X[2 + g % 2][:].rearrange("p (n d) -> p n d", n=4),
                self.vec[:, V_GV + g:V_GV + g + 1], bs, ALU.mult, ALU.add).then_inc(self.dve_seq, t.sent("dve_seq"))
            dve.wait_ge(self.dve_seq, t.now("dve_seq"))
            v.tensor_tensor(y, y, self.f_tile(4 + g), ALU.mult).then_inc(self.dve_seq, t.sent("dve_seq"))
            dve.wait_ge(self.dve_seq, t.now("dve_seq"))
            c = (4 + g) * 1024
            self.dve_parts(t, y, self.h[:, c:c + 512], self.h[:, c + 512:c + 1024])
        dve.wait_ge(self.h_ready, t.now("h_ready"))

    WHERE = {"gqa": dict(q=2048, k=4096, v=10752, vw=256, p=11776, pt=12800, r=16000, sm=16032),
             "moba": dict(q=2048, k=4096, v=12288, vw=1024, p=8192, pt=9216, r=15616, sm=15680),
             "diff": dict(q=2048, k=4096, v=12288, vw=1024, p=8192, pt=9216, r=15616, sm=15680)}
    BIAS = 16384
    O_TILES = 10240

    def s_bank(self, n, a):
        return (self.X[n % 2], self.acc[1 + n % 2])[a]

    def att(self, kind, n):
        i, qt = n // 2, n % 2
        if kind == "gqa":
            return i, qt, 512, 1, [0, P, 2 * P, 3 * P]
        nk = P * (qt + 1)
        return i, qt, nk, 2, [a * 256 + b * P for a in range(2 if kind == "moba" else 1) for b in range(qt + 1)]

    def pe_attention(self, t, kind):
        pe = t.eng
        nc, w = self.nc, self.WHERE[kind]
        evac = "o_evac" if kind == "diff" else "h_ready"
        base = t.count.get(evac, 0)

        def scores(n):
            i, qt, nk, na, _ = self.att(kind, n)
            if n >= 2:
                pe.wait_ge(self.p_ready, t.due("p_ready"))
            for a in range(na):
                p0, p1 = (0, P) if na == 1 else (64 * a, 64 * a + 64)
                kc = w["k"] + (512 * (i // 4) if kind == "gqa" else 256 * i)
                ins = nc.tensor.matmul(self.s_bank(n, a)[:, 0:nk],
                                       self.a(w["q"] + 256 * i + qt * P, P, p0, p1), self.a(kc, nk, p0, p1),
                                       start=True, stop=True)
            ins.then_inc(self.s_done, t.sent("s_done"))

        def turn(n):
            if n >= 1:
                pe.wait_ge(self.pt_ready, t.due("pt_ready"))
            pe.wait_ge(self.pn_ready, t.due("pn_ready"))
            for b, c in enumerate(self.att(kind, n)[4]):
                ins = self.pe_transpose(self.X[2][:, b * P:b * P + P], self.a(w["p"] + 512 * (n % 2) + c, P))
            ins.then_inc(self.t_done, t.sent("t_done"))

        def values(n):
            i, qt, nk, na, blocks = self.att(kind, n)
            if n >= 2:
                pe.wait_ge(self.o_evac if kind == "diff" else self.h_ready, t.at(evac, base + n - 1))
            nb = len(blocks) // (2 if kind == "moba" else 1)
            for a in range(2 if kind == "moba" else 1):
                p0, p1 = (64 * a, 64 * a + 64) if kind == "moba" else (0, P)
                vc = {"gqa": P * (i // 4), "moba": 64 * (2 * i + a), "diff": P * i}[kind]
                for b in range(nb):
                    ins = nc.tensor.matmul((self.X[3], self.acc[0])[n % 2][p0:p1, 0:P],
                                           self.a(w["v"] + w["vw"] * b + vc, p1 - p0),
                                           self.a(w["pt"] + 512 * (n % 2) + (a * nb + b) * P, P),
                                           start=b == 0, stop=b == nb - 1)
            ins.then_inc(self.pv_done, t.sent("pv_done"))

        scores(0)
        for n in range(16):
            if n < 15:
                scores(n + 1)
            turn(n)
            if n >= 1:
                values(n - 1)
        pe.wait_ge(self.pt_ready, t.due("pt_ready"))
        values(15)
        pe.wait_ge(self.p_ready, t.due("p_ready", 2))
        if kind == "diff":
            t.count[evac] = base + 16

    def act_attention(self, t, kind):
        act = t.eng
        nc, w = self.nc, self.WHERE[kind]

        def exps(n):
            i, qt, nk, na, _ = self.att(kind, n)
            sm = w["sm"] + 8 * (n % 2)
            p = w["p"] + 512 * (n % 2)
            act.wait_ge(self.nm_ready, t.due("nm_ready"))
            for a in range(na):
                dst = self.a(p + 256 * a, nk)
                src, scale = (self.X[n % 2][:], self.a(w["r"] + 8 * qt + i, 1)) if kind == "gqa" else (dst, 1.0)
                ins = nc.scalar.activation(dst, src, ACT.Exp, bias=self.a(sm + a, 1), scale=scale,
                                           accum_out=self.a(sm + 2 + a, 1))
                if a == na - 1:
                    ins.then_inc(self.p_ready, t.sent("p_ready"))
                else:
                    ins.then_inc(self.act_seq, t.sent("act_seq"))

        def copy(n):
            width = P * len(self.att(kind, n)[4])
            act.wait_ge(self.t_done, t.due("t_done"))
            if n >= 2:
                act.wait_ge(self.pv_done, t.due("pv_done"))
            nc.scalar.activation(
                self.a(w["pt"] + 512 * (n % 2), width), self.X[2][:, 0:width], ACT.Copy) \
                .then_inc(self.pt_ready, t.sent("pt_ready"))

        exps(0)
        for n in range(16):
            if n < 15:
                exps(n + 1)
            copy(n)
        act.wait_ge(self.pv_done, t.due("pv_done", 2))

    def dve_attention(self, t, kind):
        dve = t.eng
        v, w = self.nc.vector, self.WHERE[kind]

        def front(n):
            i, qt, nk, na, _ = self.att(kind, n)
            sm, p = w["sm"] + 8 * (n % 2), w["p"] + 512 * (n % 2)
            dve.wait_ge(self.s_done, t.due("s_done"))
            if kind == "gqa":
                v.reduce_max(self.a(sm + 4, 1), self.X[n % 2][:], AX).then_inc(self.dve_seq, t.sent("dve_seq"))
                dve.wait_ge(self.dve_seq, t.now("dve_seq"))
                v.scalar_tensor_tensor(
                    self.a(sm, 1), self.a(sm + 4, 1), -1.0, self.a(w["r"] + 8 * qt + i, 1), ALU.mult, ALU.mult) \
                    .then_inc(self.nm_ready, t.sent("nm_ready"))
                return
            if n >= 2:
                dve.wait_ge(self.t_done, t.due("t_done"))
            for a in range(2):
                h = 2 * i + a
                bias = self.a(self.BIAS + (P * h if qt == 0 else 2048 + 256 * h), nk)
                v.scalar_tensor_tensor(
                    self.a(p + 256 * a, nk), self.s_bank(n, a)[:, 0:nk], self.a(w["r"] + 32 * qt + h, 1), bias,
                    ALU.mult, ALU.add).then_inc(self.dve_seq, t.sent("dve_seq"))
            dve.wait_ge(self.dve_seq, t.now("dve_seq"))
            v.reduce_max(
                self.a(sm + 4, 2), self.a(p, 512).rearrange("p (a k) -> p a k", a=2)[:, :, 0:nk], AX) \
                .then_inc(self.dve_seq, t.sent("dve_seq"))
            dve.wait_ge(self.dve_seq, t.now("dve_seq"))
            v.tensor_scalar(
                self.a(sm, 2), self.a(sm + 4, 2), -1.0, None, ALU.mult).then_inc(self.nm_ready, t.sent("nm_ready"))

        def normalise(n):
            i, qt, nk, na, _ = self.att(kind, n)
            sm, p = w["sm"] + 8 * (n % 2), w["p"] + 512 * (n % 2)
            dve.wait_ge(self.p_ready, t.due("p_ready"))
            v.reciprocal(self.a(sm + 6, na), self.a(sm + 2, na)).then_inc(self.dve_seq, t.sent("dve_seq"))
            dve.wait_ge(self.dve_seq, t.now("dve_seq"))
            if kind == "gqa":
                v.tensor_scalar(
                    self.a(p, nk), self.a(p, nk), self.a(sm + 6, 1), None, ALU.mult) \
                    .then_inc(self.pn_ready, t.sent("pn_ready"))
            elif kind == "moba":
                v.tensor_scalar(
                    self.a(p, nk), self.a(p, nk), self.a(sm + 6, 1), None, ALU.mult) \
                    .then_inc(self.dve_seq, t.sent("dve_seq"))
                dve.wait_ge(self.dve_seq, t.now("dve_seq"))
                v.tensor_scalar(
                    self.a(p + 256, nk), self.a(p + 256, nk), self.a(sm + 7, 1), None, ALU.mult) \
                    .then_inc(self.pn_ready, t.sent("pn_ready"))
            else:
                v.tensor_tensor(
                    self.a(sm + 7, 1), self.a(sm + 7, 1), self.a(self.D_NL, 1), ALU.mult) \
                    .then_inc(self.dve_seq, t.sent("dve_seq"))
                v.tensor_scalar(
                    self.a(p, nk), self.a(p, nk), self.a(sm + 6, 1), None, ALU.mult) \
                    .then_inc(self.dve_seq, t.sent("dve_seq"))
                dve.wait_ge(self.dve_seq, t.now("dve_seq"))
                v.scalar_tensor_tensor(
                    self.a(p, nk), self.a(p + 256, nk), self.a(sm + 7, 1), self.a(p, nk), ALU.mult, ALU.add) \
                    .then_inc(self.pn_ready, t.sent("pn_ready"))

        def take(n):
            i, qt = n // 2, n % 2
            dve.wait_ge(self.pv_done, t.due("pv_done"))
            o = (self.X[3], self.acc[0])[n % 2][:, 0:P]
            if kind == "diff":
                v.tensor_copy(self.a(self.O_TILES + 256 * i + P * qt, P), o).then_inc(self.o_evac, t.sent("o_evac"))
                return
            c = 512 * i + P * qt
            self.dve_parts(t, o, self.h[:, c:c + P], self.h[:, c + 256:c + 256 + P])

        front(0)
        for n in range(16):
            if n < 15:
                front(n + 1)
            normalise(n)
            if n >= 1:
                take(n - 1)
        take(15)
        dve.wait_ge(self.t_done, t.due("t_done", 2 if kind != "gqa" else 16))
        dve.wait_ge(self.h_ready, t.now("h_ready"))
        dve.wait_ge(self.pn_ready, t.now("pn_ready"))

    G_SQ, G_QG, G_T, G_COS, G_SIN, G_ROT, G_SEL, G_RT, G_R = 6144, 9216, 9728, 13824, 14080, 14336, 14464, 15488, 16000

    def g_consts(self, t):
        io = self.io
        self.load_consts(t, [(self.a(self.G_COS, 640), io["rope"]), (self.a(self.G_SEL, 1024, 0, 8), io["sel_head"])])

    def pe_gqa(self, t):
        pe = t.eng
        nc = self.nc
        pe.wait_ge(self.cst_ready, t.due("cst_ready", 2 * 16))
        pe.wait_ge(self.bank_free, t.now("bank_free") + 4)
        pe.wait_ge(self.sq_ready, t.due("sq_ready", 10))
        for tt in range(TT):
            for h in range(8):
                ins = nc.tensor.matmul(self.X[0][:, 8 * tt + h:8 * tt + h + 1],
                                       self.a(self.G_SQ + 256 * h + tt * P, P), self.ones[:, 0:1], start=True,
                                       stop=True)
        for n in range(4):
            for j in range(2):
                ins = nc.tensor.matmul(self.X[0][:, 16 + 2 * n + j:17 + 2 * n + j],
                                       self.a(self.G_SQ + 2048 + 512 * j + n * P, P), self.ones[:, 0:1], start=True,
                                       stop=True)
        ins.then_inc(self.stat_ready, t.sent("stat_ready"))
        for n in range(4):
            for j in range(2):
                c = (n % 2) * 256 + j * P
                ins = self.pe_transpose(self.X[1 + n // 2][:, c:c + P], self.a(A_OUT + 3072 + 512 * j + n * P, P))
            if n % 2:
                ins.then_inc(self.vt_done, t.sent("vt_done"))
        pe.wait_ge(self.rstd_ready, t.due("rstd_ready"))
        for n in range(4):
            ins = self.pe_transpose(self.X[3][0:2, n * P:n * P + P], self.a(self.G_R + 16 + 2 * n, 2))
        ins.then_inc(self.rt_done, t.sent("rt_done"))
        pe.wait_ge(self.vt_ready, t.due("vt_ready", 2))
        for k in range(10):
            pe.wait_ge(self.qg_ready, t.due("qg_ready"))
            if k >= 2:
                pe.wait_ge(self.rope_ready, t.due("rope_ready"))
            ins = nc.tensor.matmul(self.X[k % 2][:, 0:256], self.a(self.G_ROT, P),
                                   self.a(self.G_QG + 256 * (k % 2), 256), start=True, stop=True)
            ins.then_inc(self.rot_done, t.sent("rot_done"))
        pe.wait_ge(self.rt_ready, t.due("rt_ready"))
        for j in range(2):
            ins = nc.tensor.matmul(self.X[2 + j][:], self.a(self.G_SEL + j * P, P, 0, 2), self.a(self.G_RT, 512, 0, 2),
                                   start=True, stop=True)
            ins.then_inc(self.hb_done, t.sent("hb_done"))
        pe.wait_ge(self.rope_ready, t.due("rope_ready", 2))
        pe.wait_ge(self.rk_ready, t.due("rk_ready", 2))

    def g_src(self, k):
        return self.a(A_OUT + 256 * k, 256) if k < 8 else self.a(A_OUT + 2048 + 512 * (k - 8), 256)

    def act_gqa(self, t):
        act = t.eng
        nc = self.nc
        act.wait_ge(self.bank_free, t.at("bank_free", self.evacuated["kv"]))
        for h in range(8):
            nc.scalar.activation(
                self.a(self.G_SQ + 256 * h, 256), self.g_src(h), ACT.Square) \
                .then_inc(self.sq_ready, t.sent("sq_ready"))
        for j in range(2):
            nc.scalar.activation(
                self.a(self.G_SQ + 2048 + 512 * j, 512), self.a(A_OUT + 2048 + 512 * j, 512), ACT.Square) \
                .then_inc(self.sq_ready, t.sent("sq_ready"))
        act.wait_ge(self.sq_ready, t.now("sq_ready"))
        for b in range(2):
            act.wait_ge(self.vt_done, t.due("vt_done"))
            nc.scalar.activation(
                self.a(self.WHERE["gqa"]["v"] + 512 * b, 512), self.X[1 + b][:], ACT.Copy) \
                .then_inc(self.vt_ready, t.sent("vt_ready"))
        for j in range(2):
            kc = self.a(A_OUT + 2048 + 512 * j + 256, 256)
            nc.scalar.activation(
                kc, kc, ACT.Copy, scale=self.vec[:, V_GK:V_GK + 1]).then_inc(self.act_seq, t.sent("act_seq"))
            act.wait_ge(self.act_seq, t.now("act_seq"))
        for k in range(10):
            if k >= 2:
                act.wait_ge(self.rope_ready, t.due("rope_ready"))
            gain = V_GQ if k < 8 else V_GK
            nc.scalar.activation(
                self.a(self.G_QG + 256 * (k % 2), 256), self.g_src(k), ACT.Copy, scale=self.vec[:, gain:gain + 1]) \
                .then_inc(self.qg_ready, t.sent("qg_ready"))
        act.wait_ge(self.rope_ready, t.due("rope_ready", 2))

    def dve_gqa(self, t):
        dve = t.eng
        v = self.nc.vector
        self.dve_stat(t, self.X[0][:, 0:24], self.a(self.G_R, 24), P)
        dve.wait_ge(self.rstd_ready, t.due("rstd_ready"))
        dve.wait_ge(self.rt_done, t.due("rt_done"))
        v.tensor_copy(self.a(self.G_RT, 512, 0, 2), self.X[3][0:2, :]).then_inc(self.rt_ready, t.sent("rt_ready"))
        v.tensor_scalar(
            self.a(self.G_R, 16), self.a(self.G_R, 16), P ** -0.5, None, ALU.mult) \
            .then_inc(self.dve_seq, t.sent("dve_seq"))
        dve.wait_ge(self.dve_seq, t.now("dve_seq"))
        dve.wait_ge(self.cst_ready, t.due("cst_ready", 2 * 16))
        for k in range(10):
            dve.wait_ge(self.rot_done, t.due("rot_done"))
            c = self.a(self.G_T + 256 * (k % 2), 256)
            dst = self.g_src(k)
            v.tensor_tensor(
                c, self.a(self.G_QG + 256 * (k % 2), 256), self.a(self.G_COS, 256), ALU.mult) \
                .then_inc(self.dve_seq, t.sent("dve_seq"))
            v.tensor_tensor(
                dst, self.X[k % 2][:, 0:256], self.a(self.G_SIN, 256), ALU.mult) \
                .then_inc(self.dve_seq, t.sent("dve_seq"))
            dve.wait_ge(self.dve_seq, t.now("dve_seq"))
            v.tensor_tensor(dst, dst, c, ALU.add).then_inc(self.rope_ready, t.sent("rope_ready"))
            dve.wait_ge(self.rope_ready, t.now("rope_ready"))
        t.add("vt_done", 2)
        for j in range(2):
            dve.wait_ge(self.hb_done, t.due("hb_done"))
            k = self.a(A_OUT + 2048 + 512 * j, 512)
            v.tensor_tensor(k, k, self.X[2 + j][:], ALU.mult).then_inc(self.rk_ready, t.sent("rk_ready"))
        dve.wait_ge(self.rk_ready, t.now("rk_ready"))

    M_SQ, M_SEL, M_RT, M_R, M_SM, D_LAM, D_NL, M_GC, M_HALF, D_SEL = (
        8192, 14336, 15360, 15616, 15680, 15704, 15700, 15698, 15696, 0)

    def m_consts(self, t, kind):
        io = self.io
        parts = [(self.a(self.M_SEL, 1024, 0, 16), io["sel_pair"]), (self.a(self.M_HALF, 2), io["halves"])]
        if kind == "moba":
            for qt in range(TT):
                nk = P * (qt + 1)
                row = 2 * SEQ - 1
                window = bass.AP(self.dist_bias, SEQ - 1 - P * qt, [[16 * row - 1, P], [row, 16], [1, nk]])
                dst = self.a(self.BIAS + (0 if qt == 0 else 16 * P), 16 * nk).rearrange("p (h j) -> p h j", h=16)
                parts.append((dst, window))
        else:
            parts += [(self.a(self.D_LAM, 256), io["diff_lambda"].partition_broadcast(P)),
                      (self.a(self.D_SEL, 1024, 0, 8), io["sel_head"])]
        self.load_consts(t, parts)

    def pe_heads(self, t, kind):
        pe = t.eng
        nc = self.nc
        pe.wait_ge(self.cst_ready, t.due("cst_ready", 4 * 16))
        pe.wait_ge(self.bank_free, t.now("bank_free") + 4)
        pe.wait_ge(self.sq_ready, t.due("sq_ready", 16))
        for tt in range(TT):
            for c in range(16):
                ins = nc.tensor.matmul(self.X[0][:, 32 * tt + 2 * c:32 * tt + 2 * c + 2],
                                       self.a(self.M_SQ + 256 * c + tt * P, P), self.a(self.M_HALF, 2), start=True,
                                       stop=True)
        ins.then_inc(self.stat_ready, t.sent("stat_ready"))
        for b in range(4):
            if b >= 2:
                pe.wait_ge(self.vt_ready, t.due("vt_ready"))
            for c in range(4):
                tile, tt = 4 * (b % 2) + c, b // 2
                ins = self.pe_transpose(self.X[1 + b % 2][:, c * P:c * P + P],
                                        self.a(A_OUT + 4096 + 256 * tile + tt * P, P))
            ins.then_inc(self.vt_done, t.sent("vt_done"))
        pe.wait_ge(self.vt_ready, t.due("vt_ready", 2))
        pe.wait_ge(self.rstd_ready, t.due("rstd_ready"))
        for tt in range(TT):
            ins = self.pe_transpose(self.X[3][0:16, tt * P:tt * P + P], self.a(self.M_R + 32 * tt + 16, 16))
        ins.then_inc(self.rt_done, t.sent("rt_done"))
        pe.wait_ge(self.rt_ready, t.due("rt_ready"))
        for k in range(8):
            if k >= 2:
                pe.wait_ge(self.rk_ready, t.due("rk_ready"))
            ins = nc.tensor.matmul(self.X[k % 2][:, 0:256], self.a(self.M_SEL + k * P, P, 0, 16),
                                   self.a(self.M_RT, 256, 0, 16), start=True, stop=True)
            ins.then_inc(self.hb_done, t.sent("hb_done"))
        pe.wait_ge(self.rk_ready, t.due("rk_ready", 2))

    def act_heads(self, t, kind):
        act = t.eng
        nc = self.nc
        act.wait_ge(self.bank_free, t.at("bank_free", self.evacuated[kind + "_in"]))
        for c in range(16):
            nc.scalar.activation(
                self.a(self.M_SQ + 256 * c, 256), self.a(A_OUT + 256 * c, 256), ACT.Square) \
                .then_inc(self.sq_ready, t.sent("sq_ready"))
        for b in range(4):
            act.wait_ge(self.vt_done, t.due("vt_done"))
            nc.scalar.activation(
                self.a(self.WHERE[kind]["v"] + 1024 * (b // 2) + 512 * (b % 2), 512), self.X[1 + b % 2][:],
                ACT.Copy).then_inc(self.vt_ready, t.sent("vt_ready"))
        if kind == "diff":
            act.wait_ge(self.lam_a, t.due("lam_a"))
            nc.scalar.activation(
                self.a(self.D_NL, 2), self.a(self.D_NL, 2), ACT.Exp).then_inc(self.lam_ready, t.sent("lam_ready"))

    def dve_heads(self, t, kind):
        dve = t.eng
        v = self.nc.vector
        gq, gk = (V_MQ, V_MK) if kind == "moba" else (V_DQ, V_DK)
        gc = self.a(self.M_GC, 1)
        t.add("vt_done", 4)
        v.scalar_tensor_tensor(
            gc, self.vec[:, gq:gq + 1], 64.0 ** -0.5, self.vec[:, gk:gk + 1], ALU.mult, ALU.mult) \
            .then_inc(self.dve_seq, t.sent("dve_seq"))
        dve.wait_ge(self.dve_seq, t.now("dve_seq"))
        if kind == "diff":
            dve.wait_ge(self.cst_ready, t.due("cst_ready", 8 * 16))
            lam = self.a(self.D_LAM, 256).rearrange("p (a b d) -> p a b d", a=2, b=2)
            v.tensor_tensor(
                lam[:, :, 0, :], lam[:, :, 0, :], lam[:, :, 1, :], ALU.mult).then_inc(self.dve_seq, t.sent("dve_seq"))
            dve.wait_ge(self.dve_seq, t.now("dve_seq"))
            v.reduce_sum(self.a(self.D_NL, 2), lam[:, :, 0, :], AX).then_inc(self.lam_a, t.sent("lam_a"))
            dve.wait_ge(self.lam_ready, t.due("lam_ready"))
            nl = self.a(self.D_NL, 1)
            v.scalar_tensor_tensor(
                nl, nl, -1.0, self.a(self.D_NL + 1, 1), ALU.mult, ALU.add).then_inc(self.dve_seq, t.sent("dve_seq"))
            dve.wait_ge(self.dve_seq, t.now("dve_seq"))
            v.tensor_scalar(nl, nl, LAMBDA_INIT, None, ALU.subtract).then_inc(self.dve_seq, t.sent("dve_seq"))
            dve.wait_ge(self.dve_seq, t.now("dve_seq"))
        self.dve_stat(t, self.X[0][:, 0:64], self.a(self.M_R, 64), 64)
        dve.wait_ge(self.rstd_ready, t.due("rstd_ready"))
        dve.wait_ge(self.rt_done, t.due("rt_done"))
        v.tensor_copy(
            self.a(self.M_RT, 256, 0, 16), self.X[3][0:16, 0:256]).then_inc(self.rt_ready, t.sent("rt_ready"))
        for c in range(8):
            dve.wait_ge(self.hb_done, t.due("hb_done"))
            k = self.a(A_OUT + 2048 + 256 * c, 256)
            v.scalar_tensor_tensor(
                k, k, gc, self.X[c % 2][:, 0:256], ALU.mult, ALU.mult).then_inc(self.rk_ready, t.sent("rk_ready"))
        dve.wait_ge(self.rk_ready, t.now("rk_ready"))

    def act_sub(self, t):
        act = t.eng
        act.wait_ge(self.o_evac, t.due("o_evac", 16))
        for c in range(8):
            self.nc.scalar.activation(
                self.a(A_OUT + 256 * c, 256), self.a(self.O_TILES + 256 * c, 256), ACT.Square) \
                .then_inc(self.sq_ready, t.sent("sq_ready"))

    def pe_sub(self, t):
        pe = t.eng
        nc = self.nc
        pe.wait_ge(self.sq_ready, t.due("sq_ready", 8))
        for tt in range(TT):
            for c in range(8):
                ins = nc.tensor.matmul(self.X[0][:, 8 * tt + c:8 * tt + c + 1], self.a(A_OUT + 256 * c + tt * P, P),
                                       self.ones[:, 0:1], start=True, stop=True)
        ins.then_inc(self.stat_ready, t.sent("stat_ready"))
        pe.wait_ge(self.rstd_ready, t.due("rstd_ready"))
        for tt in range(TT):
            ins = self.pe_transpose(self.X[3][0:8, tt * P:tt * P + P], self.a(self.M_R + 8 * tt, 8))
        ins.then_inc(self.rt_done, t.sent("rt_done"))
        pe.wait_ge(self.rt_ready, t.due("rt_ready"))
        h0 = self.h_total["diff_in"]
        for k in range(8):
            if k >= 2:
                pe.wait_ge(self.h_ready, t.at("h_ready", h0 + k - 1))
            ins = nc.tensor.matmul(self.X[k % 2][:, 0:256], self.a(self.D_SEL + k * P, P, 0, 8),
                                   self.a(self.M_RT, 256, 0, 8), start=True, stop=True)
            ins.then_inc(self.hb_done, t.sent("hb_done"))

    def dve_sub(self, t):
        dve = t.eng
        v = self.nc.vector
        gc = self.a(self.M_GC, 1)
        v.tensor_scalar(
            gc, self.vec[:, V_SUB:V_SUB + 1], 1.0 - LAMBDA_INIT, None, ALU.mult) \
            .then_inc(self.dve_seq, t.sent("dve_seq"))
        dve.wait_ge(self.dve_seq, t.now("dve_seq"))
        self.dve_stat(t, self.X[0][:, 0:16], self.a(self.M_R, 16), P)
        dve.wait_ge(self.rstd_ready, t.due("rstd_ready"))
        dve.wait_ge(self.rt_done, t.due("rt_done"))
        v.tensor_copy(self.a(self.M_RT, 256, 0, 8), self.X[3][0:8, 0:256]).then_inc(self.rt_ready, t.sent("rt_ready"))
        dve.wait_ge(self.o_evac, t.now("o_evac"))
        for c in range(8):
            dve.wait_ge(self.hb_done, t.due("hb_done"))
            o = self.a(self.O_TILES + 256 * c, 256)
            v.scalar_tensor_tensor(
                o, o, gc, self.X[c % 2][:, 0:256], ALU.mult, ALU.mult).then_inc(self.dve_seq, t.sent("dve_seq"))
            dve.wait_ge(self.dve_seq, t.now("dve_seq"))
            hi, lo = self.norm_dst(False, 0, c)
            self.dve_parts(t, o, hi, lo)
        dve.wait_ge(self.h_ready, t.now("h_ready"))

    R_COS, R_DEC, R_V, R_TD, R_TP, R_ST, R_SQ, R_SEL, R_RT, R_R = (
        0, 512, 14336, 18432, 20480, 6144, 6912, 7936, 8960, 9216)
    R_O = 18432

    def r_consts(self, t):
        io = self.io
        self.load_consts(t, [(self.a(self.R_COS, 512), io["rotary"]), (self.a(self.R_DEC, 1536), io["decay"])])

    def dve_rotary(self, t, base, tmp):
        dve, v = t.eng, self.nc.vector
        x = self.a(base, 2048).rearrange("p (h s n) -> p h s n", h=4, s=2)
        x1, x2 = x[:, :, 0, :], x[:, :, 1, :]
        ta, tb = (self.a(tmp + 1024 * k, 1024).rearrange("p (h n) -> p h n", h=4) for k in range(2))
        cos, sin = (self.a(self.R_COS + 256 * k, 256).unsqueeze(1).broadcast_to([P, 4, 256]) for k in range(2))
        v.tensor_tensor(ta, x1, sin, ALU.mult).then_inc(self.dve_seq, t.sent("dve_seq"))
        v.tensor_tensor(tb, x2, sin, ALU.mult).then_inc(self.dve_seq, t.sent("dve_seq"))
        dve.wait_ge(self.dve_seq, t.now("dve_seq"))
        v.tensor_tensor(x1, x1, cos, ALU.mult).then_inc(self.dve_seq, t.sent("dve_seq"))
        v.tensor_tensor(x2, x2, cos, ALU.mult).then_inc(self.dve_seq, t.sent("dve_seq"))
        dve.wait_ge(self.dve_seq, t.now("dve_seq"))
        v.tensor_tensor(x1, x1, tb, ALU.subtract).then_inc(self.dve_seq, t.sent("dve_seq"))
        dve.wait_ge(self.dve_seq, t.now("dve_seq"))
        v.tensor_tensor(x2, x2, ta, ALU.add).then_inc(self.rope_ready, t.sent("rope_ready"))
        dve.wait_ge(self.rope_ready, t.now("rope_ready"))

    def pool_rotary(self, t, base, tmp):
        pool, g = t.eng, self.nc.gpsimd
        x = self.a(base, 2048).rearrange("p (h s n) -> p h s n", h=4, s=2)
        x1, x2 = x[:, :, 0, :], x[:, :, 1, :]
        ta, tb = (self.a(tmp + 1024 * k, 1024).rearrange("p (h n) -> p h n", h=4) for k in range(2))
        cos, sin = (self.a(self.R_COS + 256 * k, 256).unsqueeze(1).broadcast_to([P, 4, 256]) for k in range(2))
        g.tensor_tensor(ta, x1, sin, ALU.mult).then_inc(self.pool_seq, t.sent("pool_seq"))
        g.tensor_tensor(tb, x2, sin, ALU.mult).then_inc(self.pool_seq, t.sent("pool_seq"))
        pool.wait_ge(self.pool_seq, t.now("pool_seq"))
        g.tensor_tensor(x1, x1, cos, ALU.mult).then_inc(self.pool_seq, t.sent("pool_seq"))
        g.tensor_tensor(x2, x2, cos, ALU.mult).then_inc(self.pool_seq, t.sent("pool_seq"))
        pool.wait_ge(self.pool_seq, t.now("pool_seq"))
        g.tensor_tensor(x1, x1, tb, ALU.subtract).then_inc(self.pool_seq, t.sent("pool_seq"))
        pool.wait_ge(self.pool_seq, t.now("pool_seq"))
        g.tensor_tensor(x2, x2, ta, ALU.add).then_inc(self.kr_ready, t.sent("kr_ready"))
        pool.wait_ge(self.kr_ready, t.now("kr_ready"))

    def pe_retention(self, t, j):
        pe = t.eng
        nc = self.nc
        pe.wait_ge(self.cst_ready, t.due("cst_ready", 2 * 16))
        pe.wait_ge(self.bank_free, t.now("bank_free") + 4)
        for b in range(8):
            if b >= 2:
                pe.wait_ge(self.vt_ready, t.due("vt_ready"))
            for c in range(4):
                tile, tt = 4 * (b % 4) + c, b // 4
                ins = self.pe_transpose(self.X[1 + b % 2][:, c * P:c * P + P],
                                        self.a(A_OUT + 4096 + 256 * tile + tt * P, P))
            ins.then_inc(self.vt_done, t.sent("vt_done"))
        pe.wait_ge(self.vt_ready, t.due("vt_ready", 2))
        pe.wait_ge(self.rope_ready, t.due("rope_ready"))
        pe.wait_ge(self.kr_ready, t.due("kr_ready"))
        q, k = A_OUT, A_OUT + 2048

        def scores(h):
            bank = self.acc[1 + h % 2]
            for jt, n in ((0, 256), (1, P)):
                for c in range(2):
                    tile = 256 * (2 * h + c)
                    ins = nc.tensor.matmul(bank[:, jt * 256:jt * 256 + n], self.a(k + tile + jt * P, P),
                                           self.a(q + tile + jt * P, n), start=c == 0, stop=c == 1)
            ins.then_inc(self.st_done, t.sent("st_done"))

        def values(h):
            pe.wait_ge(self.st_ready, t.due("st_ready"))
            if h >= 1:
                pe.wait_ge(self.o_evac, t.due("o_evac"))
            for c in range(4):
                o = self.X[1 + c // 2]
                at = (c % 2) * 256
                v = self.R_V + 512 * h + P * c
                st = self.R_ST + 384 * (h % 2)
                nc.tensor.matmul(o[:, at:at + P], self.a(v, P), self.a(st, P), start=True, stop=True)
                nc.tensor.matmul(o[:, at + P:at + 256], self.a(v, P), self.a(st + P, P), start=True, stop=False)
                ins = nc.tensor.matmul(o[:, at + P:at + 256], self.a(v + 2048, P), self.a(st + 256, P), start=False,
                                       stop=True)
            ins.then_inc(self.od_done, t.sent("od_done"))

        def stats(h):
            pe.wait_ge(self.sq_ready, t.due("sq_ready"))
            if h == 3:
                pe.wait_ge(self.o_evac, t.due("o_evac"))
            for tt in range(TT):
                for c in range(4):
                    ins = nc.tensor.matmul(self.acc[0][:, 4 * tt + h:4 * tt + h + 1],
                                           self.a(self.R_SQ + 256 * c + tt * P, P), self.ones[:, 0:1],
                                           start=c == 0, stop=c == 3)
            ins.then_inc(self.ost_ready, t.sent("ost_ready"))

        scores(0)
        scores(1)
        for h in range(4):
            values(h)
            if h >= 1:
                stats(h - 1)
            if h + 2 < 4:
                scores(h + 2)
        stats(3)
        pe.wait_ge(self.rstd_ready, t.due("rstd_ready"))
        for tt in range(TT):
            ins = self.pe_transpose(self.X[3][0:4, tt * P:tt * P + P], self.a(self.R_R + 4 * tt, 4))
        ins.then_inc(self.rt_done, t.sent("rt_done"))
        pe.wait_ge(self.rt_ready, t.due("rt_ready"))
        pe.wait_ge(self.cst_ready, t.due("cst_ready", 16))
        for h in range(4):
            ins = nc.tensor.matmul(self.X[h][:, 0:256],
                                   self.a(self.R_SEL + h * P, P, 0, 4), self.a(self.R_RT, 256, 0, 4), start=True,
                                   stop=True)
            ins.then_inc(self.hb_done, t.sent("hb_done"))

    def act_retention(self, t, j):
        act = t.eng
        nc = self.nc
        act.wait_ge(self.bank_free, t.at("bank_free", self.evacuated[f"ret_in{j}"]))
        for b in range(8):
            act.wait_ge(self.vt_done, t.due("vt_done"))
            nc.scalar.activation(
                self.a(self.R_V + 2048 * (b // 4) + 512 * (b % 4), 512), self.X[1 + b % 2][:], ACT.Copy) \
                .then_inc(self.vt_ready, t.sent("vt_ready"))
            if b % 2:
                k = b // 2
                if k:
                    act.wait_ge(self.silu_a, t.due("silu_a"))
                nc.scalar.activation(
                    self.tmp[:], self.a(A_OUT + 8192 + 1024 * k, 1024), ACT.Tanh, scale=0.5) \
                    .then_inc(self.th_ready, t.sent("th_ready"))
        act.wait_ge(self.silu_a, t.due("silu_a"))
        self.load_consts(t, [(self.a(self.R_SEL, 1024, 0, 8), self.io["sel_head"])])
        for h in range(4):
            act.wait_ge(self.o_evac, t.due("o_evac"))
            if h:
                act.wait_ge(self.ost_ready, t.due("ost_ready"))
            nc.scalar.activation(
                self.a(self.R_SQ, 1024), self.a(self.R_O + 1024 * h, 1024), ACT.Square) \
                .then_inc(self.sq_ready, t.sent("sq_ready"))
        act.wait_ge(self.ost_ready, t.due("ost_ready"))

    def pool_retention(self, t, j):
        pool = t.eng
        g = self.nc.gpsimd
        pool.wait_ge(self.bank_free, t.at("bank_free", self.evacuated[f"ret_in{j}"]))
        pool.wait_ge(self.cst_ready, t.due("cst_ready", 2 * 16))
        self.pool_rotary(t, A_OUT + 2048, self.R_TP)
        t.add("cst_ready", 16)
        for h in range(4):
            pool.wait_ge(self.ost_ready, t.due("ost_ready"))
            o = self.a(self.R_O + 1024 * h, 1024)
            g.tensor_tensor(
                o, o, self.a(A_OUT + 8192 + 1024 * h, 1024), ALU.mult).then_inc(self.og_ready, t.sent("og_ready"))
        self.pool_stat(t, self.a(self.R_R, 8), 8)

    def dve_retention(self, t, j):
        dve = t.eng
        v = self.nc.vector
        dve.wait_ge(self.cst_ready, t.due("cst_ready", 2 * 16))
        self.dve_rotary(t, A_OUT, self.R_TD)
        for k in range(4):
            dve.wait_ge(self.th_ready, t.due("th_ready"))
            g = self.a(A_OUT + 8192 + 1024 * k, 1024)
            v.scalar_tensor_tensor(g, self.tmp[:], 1.0, g, ALU.add, ALU.mult).then_inc(self.silu_a, t.sent("silu_a"))
        dve.wait_ge(self.silu_a, t.now("silu_a"))
        dve.wait_ge(self.vt_done, t.due("vt_done", 8))
        dve.wait_ge(self.kr_ready, t.due("kr_ready"))

        def decay(h):
            dve.wait_ge(self.st_done, t.due("st_done"))
            v.tensor_tensor(
                self.a(self.R_ST + 384 * (h % 2), 384), self.acc[1 + h % 2][:, 0:384],
                self.a(self.R_DEC + 384 * h, 384), ALU.mult).then_inc(self.st_ready, t.sent("st_ready"))

        def take(h):
            dve.wait_ge(self.od_done, t.due("od_done"))
            v.tensor_copy(self.a(self.R_O + 1024 * h, 512), self.X[1][:]).then_inc(self.dve_seq, t.sent("dve_seq"))
            dve.wait_ge(self.dve_seq, t.now("dve_seq"))
            v.tensor_copy(
                self.a(self.R_O + 1024 * h + 512, 512), self.X[2][:]).then_inc(self.o_evac, t.sent("o_evac"))

        decay(0)
        decay(1)
        for h in range(4):
            take(h)
            if h + 2 < 4:
                decay(h + 2)
        self.dve_stat(t, self.acc[0][:, 0:8], self.a(self.R_R, 8), 512, "ost_ready", 4)
        dve.wait_ge(self.rstd_ready, t.due("rstd_ready"))
        dve.wait_ge(self.rt_done, t.due("rt_done"))
        v.tensor_scalar(
            self.a(self.R_RT, 256, 0, 4), self.X[3][0:4, 0:256], 0.5, None, ALU.mult) \
            .then_inc(self.rt_ready, t.sent("rt_ready"))
        t.add("cst_ready", 16)
        for h in range(4):
            dve.wait_ge(self.hb_done, t.due("hb_done"))
            dve.wait_ge(self.og_ready, t.due("og_ready"))
            o = self.a(self.R_O + 1024 * h, 1024).rearrange("p (c n) -> p c n", c=4)
            bc = self.X[h][:, 0:256].unsqueeze(1).broadcast_to([P, 4, 256])
            v.tensor_tensor(o, o, bc, ALU.mult).then_inc(self.dve_seq, t.sent("dve_seq"))
            dve.wait_ge(self.dve_seq, t.now("dve_seq"))
            parts = self.h[:, 2048 * h:2048 * h + 2048].rearrange("p (c s n) -> p c s n", c=4, s=2)
            hi, lo = parts[:, :, 0, :], parts[:, :, 1, :]
            v.tensor_copy(hi, o).then_inc(self.dve_seq, t.sent("dve_seq"))
            dve.wait_ge(self.dve_seq, t.now("dve_seq"))
            v.tensor_tensor(lo, o, hi.bitcast(F32), ALU.subtract).then_inc(self.h_ready, t.sent("h_ready", 4))
        dve.wait_ge(self.h_ready, t.now("h_ready"))

    def tensor_program(self, pe):
        t = Track(pe)
        self.pe_start(t)
        self.pe_mod(t, 0)
        self.pe_mod(t, 1)
        for l in range(2):
            for m, name in ((0, "1"), (3, "mix"), (6, "2")):
                wide = not (l == 1 and m == 6)
                self.pe_norm(t, ("mod", l, m), 0, wide)
                if wide:
                    self.pe_norm(t, ("mod", l, m), 1, wide)
                if name != "mix":
                    self.pe_gemm(t, f"gu{name}_{l}")
                    self.pe_gemm(t, f"down{name}_{l}")
                elif l == 0:
                    self.pe_gemm(t, "in_ab")
                    self.pe_fourier(t)
                    self.pe_gemm(t, "out_ab")
                else:
                    self.pe_gemm(t, "q")
                    self.pe_gemm(t, "kv")
                    self.pe_gqa(t)
                    self.pe_attention(t, "gqa")
                    self.pe_gemm(t, "o")
        self.pe_norm(t, ("final", V_FINAL), 0, False)
        for i in range(4):
            self.pe_norm(t, ("gain", V_N1 + 8 * i), 0, False)
            if i % 3 == 0:
                self.pe_gemm(t, f"ret_in{i // 3}")
                self.pe_retention(t, i // 3)
                self.pe_gemm(t, f"ret_out{i // 3}")
            else:
                kind = ("moba", "diff")[i - 1]
                self.pe_gemm(t, kind + "_in")
                self.pe_heads(t, kind)
                self.pe_attention(t, kind)
                if kind == "diff":
                    self.pe_sub(t)
                self.pe_gemm(t, kind + "_out")
            self.pe_norm(t, ("gain", V_N2 + 8 * i), 0, False)
            self.pe_gemm(t, f"up{i}")
            self.pe_gemm(t, f"down{i}")

    def scalar_program(self, act):
        t = Track(act)
        self.act_start(t)
        self.act_gemm(t, "mod0")
        self.act_gemm(t, "mod1")
        for l in range(2):
            for m, name in ((0, "1"), (3, "mix"), (6, "2")):
                wide = not (l == 1 and m == 6)
                self.act_norm(t, ("mod", l, m), 0, wide)
                if wide:
                    self.act_norm(t, ("mod", l, m), 1, wide)
                if name != "mix":
                    self.act_gemm(t, f"gu{name}_{l}")
                    self.act_gemm(t, f"down{name}_{l}")
                elif l == 0:
                    self.f_consts(t)
                    self.act_gemm(t, "in_ab")
                    self.act_fourier(t)
                    self.act_gemm(t, "out_ab")
                else:
                    self.g_consts(t)
                    self.act_gemm(t, "q")
                    self.act_gemm(t, "kv")
                    self.act_gqa(t)
                    self.act_attention(t, "gqa")
                    self.act_gemm(t, "o")
        self.act_norm(t, ("final", V_FINAL), 0, False)
        for i in range(4):
            self.act_norm(t, ("gain", V_N1 + 8 * i), 0, False)
            if i % 3 == 0:
                self.r_consts(t)
                self.act_gemm(t, f"ret_in{i // 3}")
                self.act_retention(t, i // 3)
                self.act_gemm(t, f"ret_out{i // 3}")
            else:
                kind = ("moba", "diff")[i - 1]
                self.m_consts(t, kind)
                self.act_gemm(t, kind + "_in")
                self.act_heads(t, kind)
                self.act_attention(t, kind)
                if kind == "diff":
                    self.act_sub(t)
                self.act_gemm(t, kind + "_out")
            self.act_norm(t, ("gain", V_N2 + 8 * i), 0, False)
            self.act_gemm(t, f"up{i}")
            self.act_gemm(t, f"down{i}")

    def vector_program(self, dve):
        t = Track(dve)
        self.dve_start(t)
        self.dve_gemm(t, "mod0")
        self.dve_mod(t, 0)
        self.dve_gemm(t, "mod1")
        self.dve_mod(t, 1)
        for l in range(2):
            for m, name in ((0, "1"), (3, "mix"), (6, "2")):
                wide = not (l == 1 and m == 6)
                self.dve_norm(t, ("mod", l, m), 0, wide)
                if wide:
                    self.dve_norm(t, ("mod", l, m), 1, wide)
                if name != "mix":
                    self.dve_gemm(t, f"gu{name}_{l}")
                    self.dve_gemm(t, f"down{name}_{l}")
                elif l == 0:
                    self.dve_gemm(t, "in_ab")
                    self.dve_fourier(t)
                    self.dve_gemm(t, "out_ab")
                else:
                    self.dve_gemm(t, "q")
                    self.dve_gemm(t, "kv")
                    self.dve_gqa(t)
                    self.dve_attention(t, "gqa")
                    self.dve_gemm(t, "o")
        self.dve_norm(t, ("final", V_FINAL), 0, False)
        for i in range(4):
            self.dve_norm(t, ("gain", V_N1 + 8 * i), 0, False)
            if i % 3 == 0:
                self.dve_gemm(t, f"ret_in{i // 3}")
                self.dve_retention(t, i // 3)
                self.dve_gemm(t, f"ret_out{i // 3}")
            else:
                kind = ("moba", "diff")[i - 1]
                self.dve_gemm(t, kind + "_in")
                self.dve_heads(t, kind)
                self.dve_attention(t, kind)
                if kind == "diff":
                    self.dve_sub(t)
                self.dve_gemm(t, kind + "_out")
            self.dve_norm(t, ("gain", V_N2 + 8 * i), 0, False)
            self.dve_gemm(t, f"up{i}")
            self.dve_gemm(t, f"down{i}")

    def pool_program(self, pool):
        t = Track(pool)
        self.pool_start(t)
        for l in range(2):
            for m in (0, 3, 6):
                self.pool_norm(t)
                if not (l == 1 and m == 6):
                    self.pool_norm(t)
                if m == 3:
                    self.pool_stat(t, self.a(self.F_R, 16) if l == 0 else self.a(self.G_R, 24), 16 if l == 0 else 24)
        t.add("cst_ready", 6 * 16)
        self.pool_norm(t)
        for i in range(4):
            self.pool_norm(t)
            if i % 3 == 0:
                self.pool_retention(t, i // 3)
            else:
                self.pool_stat(t, self.a(self.M_R, 64), 64)
                if i == 2:
                    self.pool_stat(t, self.a(self.M_R, 16), 16)
                t.add("cst_ready", 4 * 16)
            self.pool_norm(t)


def build(nc, io):
    prog = Program(nc, io)
    with ExitStack() as ctx:
        prog.allocate(ctx)
        block = ctx.enter_context(nc.Block())

        @block.sync
        def _(sp):
            prog.sync_program(sp)

        @block.gpsimd
        def _(pool):
            prog.pool_program(pool)

        @block.scalar
        def _(act):
            prog.scalar_program(act)

        @block.vector
        def _(dve):
            prog.vector_program(dve)

        @block.tensor
        def _(pe):
            prog.tensor_program(pe)


def _units(np, w, order=None, kpad=None, nb=16):
    k, m = w.shape
    if kpad:
        full = np.zeros((kpad, m), w.dtype)
        full[:k] = w
        w, k = full, kpad
    b = w.reshape(k // 128, 128, m // 128, 128).transpose(2, 0, 1, 3)
    if order is not None:
        b = b[order]
    b = b.reshape(-1, nb, 128, 128).transpose(0, 2, 1, 3)
    return np.ascontiguousarray(b.reshape(b.shape[0], 128, nb * 128))


def _gate_up(np, w):
    ff = w.shape[1] // 2
    full = np.zeros((w.shape[0], 2 * FF_T * 128), w.dtype)
    full[:, :ff] = w[:, :ff]
    full[:, FF_T * 128:FF_T * 128 + ff] = w[:, ff:]
    order = [t + s * FF_T for t in range(FF_T) for s in range(2)]
    return _units(np, full, order=order)


def _col(np, v):
    return v.reshape(-1, 128).T


def _tables(np):
    f = np.float32
    n, c = np.arange(SEQ), np.arange(128)
    scale = 1.0 / np.sqrt(SEQ * 128.0)
    ch = 2 * np.pi * np.outer(c, c) / 128
    tok = 2 * np.pi * np.outer(n, n) / SEQ
    dft_ch = np.concatenate([np.cos(ch), np.sin(ch)], 1) * scale
    dft_tok = np.concatenate([x[tt * 128:tt * 128 + 128] for tt in range(2) for x in (np.cos(tok), -np.sin(tok))], 1)
    inv = f(10000.0) ** (-np.arange(0, 64, 2, dtype=f) / f(64))
    pos = np.stack([n // 64, n % 64]).astype(f)
    ang = np.concatenate([np.concatenate([inv[:, None] * pos[a]] * 2, 0) for a in range(2)], 0).astype(f)
    rot = np.zeros((128, 128))
    for a in (0, 64):
        for i in range(32):
            rot[a + i, a + 32 + i] = -1.0
            rot[a + 32 + i, a + i] = 1.0
    rope = np.concatenate([np.cos(ang.astype(np.float64)), np.sin(ang.astype(np.float64)), rot.T], 1)
    inv = f(10000.0) ** (-np.arange(0, 256, 2, dtype=f) / f(256))
    ang = (inv[:, None] * n.astype(f)[None, :]).astype(f).astype(np.float64)
    rotary = np.concatenate([np.cos(ang), np.sin(ang)], 1)
    decay = []
    for h in range(4):
        gamma = 1.0 - 2.0 ** (-5.0 - h)
        for jt in range(2):
            j, i = jt * 128 + c[:, None], np.arange(jt * 128, 256)[None, :]
            decay.append(np.where(i >= j, gamma ** np.maximum(i - j, 0), 0.0) / 16.0)
    dist = np.arange(-255, 256)
    nn = np.maximum(dist, 0)
    large = 16 + (np.log(np.maximum(nn, 1).astype(f) / f(16)) / f(np.log(64.0)) * f(16)).astype(np.int32)
    bucket = np.where(nn < 16, nn, np.minimum(large, 31))
    onehot = np.zeros((33, 511))
    onehot[bucket, np.arange(511)] = 1.0
    onehot[:32, dist < 0] = 0.0
    onehot[32, dist < 0] = 1.0
    onehot = onehot[:, ::-1]
    sel_head = np.zeros((8, 8, 128))
    for t in range(8):
        sel_head[t, t] = 1.0
    sel_pair = np.zeros((16, 8, 128))
    for t in range(8):
        sel_pair[2 * t, t, :64] = 1.0
        sel_pair[2 * t + 1, t, 64:] = 1.0
    halves = np.zeros((128, 2))
    halves[:64, 0] = 1.0
    halves[64:, 1] = 1.0
    out = dict(dft_ch=dft_ch, dft_tok=dft_tok, rope=rope, rotary=rotary, decay=np.concatenate(decay, 1),
               bucket=onehot, sel_head=sel_head.reshape(8, 1024), sel_pair=sel_pair.reshape(16, 1024),
               halves=halves, ones=np.ones((128, 128)), ident=np.eye(128))
    return {k: np.ascontiguousarray(v, f) for k, v in out.items()}


def _layout(np, i):
    a = {k: np.asarray(v) for k, v in i.items()}
    out = _tables(np)
    for name in ("x", "ctx"):
        out[name] = np.ascontiguousarray(a[name][0].T.reshape(8, 128, 256).transpose(1, 0, 2).reshape(128, 2048))
    c2 = np.stack([_col(np, a["c"][0]), _col(np, a["c_ctx"])], 2).reshape(128, 16)
    twice = [np.concatenate([a[n][0], a[n][0]])[:, None] for n in
             ("moba_q_norm_2", "moba_k_norm_2", "diff_q_norm_2", "diff_k_norm_2")]
    out["vectors"] = np.ascontiguousarray(np.concatenate(
        [_col(np, a[n][l]) for n in ("g_ffn1", "g_mix", "g_ffn2") for l in range(2)] + [_col(np, a["g_final"])]
        + [_col(np, a[n][l]) for n in ("norm1_2", "norm2_2") for l in range(4)]
        + [a["g_v"][0].T, a["g_q"][0][:, None], a["g_k"][0][:, None]] + twice + [a["diff_subln_2"][0][:, None], c2]
        + [_col(np, a["b_mod"][l]) for l in range(2)]
        + [np.tile(np.eye(2, dtype=np.float32), (64, 1))], 1))
    out["w_s"] = np.ascontiguousarray(a["w_s"][0].transpose(2, 0, 1).reshape(128, 512))
    out["b_s"] = a["b_s"][0].reshape(512)
    out["rel_bias"] = a["rel_bias_2"]
    out["diff_lambda"] = a["diff_lambda_2"][0].reshape(256)
    for l in range(2):
        out[f"mod{l}"] = np.ascontiguousarray(a["w_mod"][l].reshape(2, 4, 128, 18, 512).transpose(3, 0, 2, 1, 4)
                                              .reshape(36, 128, 2048))
        for n in "12":
            out[f"gu{n}_{l}"] = _gate_up(np, a[f"w_ffn{n}_gu"][l])
            out[f"down{n}_{l}"] = _units(np, a[f"w_ffn{n}_down"][l], kpad=FF_T * 128, nb=11)
    out["in_ab"], out["out_ab"] = _units(np, a["w_in_ab"][0]), _units(np, a["w_out_ab"][0])
    out["q"], out["kv"] = _units(np, a["w_qkv"][0][:, :1024]), _units(np, a["w_qkv"][0][:, 1024:])
    out["o"] = _units(np, a["w_o"][0])
    for j in range(2):
        out[f"ret_in{j}"], out[f"ret_out{j}"] = _units(np, a["ret_w_in_2"][j]), _units(np, a["ret_w_out_2"][j])
    for kind in ("moba", "diff"):
        out[kind + "_in"], out[kind + "_out"] = _units(np, a[kind + "_w_in_2"][0]), _units(np, a[kind + "_w_out_2"][0])
    for i in range(4):
        out[f"up{i}"], out[f"down{i}"] = _units(np, a["w_up_2"][i]), _units(np, a["w_down_2"][i])
    return out


def kernel(**inputs):
    import numpy as np
    import concourse.bacc as bacc
    from concourse.bass_utils import run_bass_kernel_spmd

    nc = bacc.Bacc("TRN2", target_bir_lowering=False, num_devices=1)
    arrays = _layout(np, inputs)
    io = {name: nc.dram_tensor(f"in_{name}", a.shape, F32, kind="ExternalInput").ap() for name, a in arrays.items()}
    io["out"] = nc.dram_tensor("out_x", (128, 2048), F32, kind="ExternalOutput").ap()
    build(nc, io)
    r = run_bass_kernel_spmd(nc, [{f"in_{name}": a for name, a in arrays.items()}], core_ids=[0])
    y = r.results[0]["out_x"]
    return np.ascontiguousarray(y.reshape(128, 8, 256).transpose(2, 1, 0).reshape(1, 256, 1024))
```

```python
import concourse.bass as bass
from concourse import mybir
from contextlib import ExitStack, contextmanager

F32 = mybir.dt.float32
F32R = mybir.dt.float32r
ALU = mybir.AluOpType
ACT = mybir.ActivationFunctionType
AX = mybir.AxisListType.X

P = 128
D = 1024
KT = D // P
SEQ = 256
TT = SEQ // P
FF_T = 22
FF2_T = 32
N_MOD = 9
EPS = 1e-6
RING = 4
UNIT = 2048
LAMBDA_INIT = 0.8 - 0.6 * 2.718281828459045 ** (-0.3 * 2)

V_FFN1, V_MIX, V_FFN2, V_FINAL, V_N1, V_N2 = 0, 16, 32, 48, 56, 88
V_GV, V_GQ, V_GK, V_MQ, V_MK, V_DQ, V_DK, V_SUB = 120, 124, 125, 126, 127, 128, 129, 130
V_C, V_BMOD, V_PAIR, V_N = 131, 147, 147 + 2 * 72, 147 + 2 * 72 + 2

N_SUM = 512
G_ROWS = 20 * 1024

A_OUT = 2048


class Track:

    def __init__(self, eng):
        self.eng = eng
        self.count, self.per, self.reg = {}, {}, None

    def value(self, name):
        v = self.count.get(name, 0)
        if self.reg is not None and self.per.get(name, 0):
            return self.reg * self.per[name] + v
        return v

    def add(self, name, n=1):
        self.count[name] = self.count.get(name, 0) + n

    def due(self, name, n=1):
        self.add(name, n)
        return self.now(name)

    def at(self, name, total):
        self.count[name] = total
        return self.now(name)

    def now(self, name):
        assert self.count.get(name, 0) > 0, name
        return self.value(name)

    def begun(self, name):
        return self.count.get(name, 0) > 0

    def sent(self, name, n=1):
        self.add(name, n)
        return n

    @contextmanager
    def loop(self, n, per):
        before = dict(self.count)
        assert self.reg is None
        with self.eng.Fori(0, n) as i:
            self.reg, self.per = i, per
            yield i
            self.reg = None
        made = {k: v - before.get(k, 0) for k, v in self.count.items() if v != before.get(k, 0)}
        assert made == {k: v for k, v in per.items() if v}, (made, per)
        for k, v in made.items():
            self.count[k] += v * (n - 1)


class Gemm:

    def __init__(self, name, kt, tiles, mode, kind, src, **kw):
        self.name, self.kt, self.tiles, self.mode, self.kind, self.src = name, kt, tiles, mode, kind, src
        self.kw = kw
        if kind == "mod":
            self.nb, self.units, self.parts, self.group = 16, tiles // 2, 1, 4
        elif kt == 8:
            self.nb, self.units, self.parts, self.group = 16, tiles // 2, 2, 4
        elif kt == 16:
            self.nb, self.units, self.parts, self.group = 16, tiles, 1, 4
        else:
            self.nb, self.units, self.parts, self.group = kt // 2, tiles * 2, 1, 8
        self.half = (self.nb + 1) // 2
        self.first_guest, self.guests = kw.get("guests", (0, 0))

    def pos(self, k):
        return self.s0 + (2 * k if k < self.guests else self.guests + k)


def gemm_list():
    out = []

    def add(*a, **kw):
        out.append(Gemm(*a, **kw))
        return out[-1]

    add("mod0", 8, 72, "mod", "mod", "act")
    add("gu1_0", 8, 44, "wide", "glu", "h", guests=(0, 20))
    add("down1_0", 22, 8, "wide", "res", "act", gate=(0, 2))
    add("in_ab", 8, 12, "wide", "plain", "h", at=A_OUT, w=512)
    add("out_ab", 8, 8, "wide", "res", "h", gate=(0, 5))
    add("gu2_0", 8, 44, "wide", "glu", "h", guests=(20, 16))
    add("down2_0", 22, 8, "wide", "res", "act", gate=(0, 8))
    add("gu1_1", 8, 44, "wide", "glu", "h")
    add("down1_1", 22, 8, "wide", "res", "act", gate=(1, 2))
    add("q", 8, 8, "xonly", "plain", "h", at=A_OUT, w=256)
    add("kv", 8, 4, "wide", "plain", "h", at=A_OUT + 2048, w=512)
    add("o", 8, 8, "cat", "res", "h", gate=(1, 5))
    add("gu2_1", 8, 44, "cat", "glu", "h")
    add("down2_1", 22, 8, "cat", "res", "act", gate=(1, 8))
    for i in range(4):
        if i % 3 == 0:
            add(f"ret_in{i // 3}", 8, 48, "cat", "plain", "h", at=A_OUT, w=256)
            add(f"ret_out{i // 3}", 16, 8, "cat", "res", "h", gate=None)
        elif i == 1:
            add("moba_in", 8, 24, "cat", "plain", "h", at=A_OUT, w=256)
            add("moba_out", 8, 8, "cat", "res", "h", gate=None)
        else:
            add("diff_in", 8, 24, "cat", "plain", "h", at=A_OUT, w=256)
            add("diff_out", 8, 8, "cat", "res", "h", gate=None)
        add(f"up{i}", 8, 32, "cat", "relu2", "h")
        add(f"down{i}", 32, 8, "cat", "res", "act", gate=None)
    s = 0
    for g in out:
        g.s0 = s
        s += g.units + g.guests
    return out


class Program:
    def __init__(self, nc, io):
        self.nc, self.io = nc, io
        self.gemms = gemm_list()
        self.by_name = {g.name: g for g in self.gemms}
        mixer = {"out_ab": 12, "o": 16, "ret_out0": 16, "ret_out1": 16, "moba_out": 16, "diff_out": 8}
        h, a, tiles = 0, 1, 0
        self.h_total, self.act_total, self.evacuated = {}, {}, {}
        for g in self.gemms:
            if g.kind == "mod":
                continue
            if g.src == "h":
                h += mixer.get(g.name, 0 if g.name == "kv" else 8)
                self.h_total[g.name] = h
            else:
                a += g.kt
                self.act_total[g.name] = a
            tiles += g.tiles
            self.evacuated[g.name] = 4 + tiles
        self.x_tiles = sum(g.tiles for g in self.gemms if g.kind == "res")
        self.split = [h for g in self.gemms for k in range(g.units)
                      for h in ((g, self.gemms[0]) if k < g.guests else (g,))]

    def allocate(self, ctx):
        nc = self.nc

        def sb(name, cols, dt=F32):
            return ctx.enter_context(nc.sbuf_tensor(name, [P, cols], dt))

        here = -(-nc.sbuf_base // 32) * 32
        self.ar = sb("arena", 22528)
        self.act = nc.alloc_sbuf_tensor_at("act_parts", [P, 22528], F32R, offset=here)
        self.h = sb("h_parts", 8192, F32R)
        self.raw = [sb(f"raw{k}", UNIT) for k in range(RING)]
        self.wh = [sb(f"w_hi{k}", UNIT, F32R) for k in range(2)]
        self.wl = [sb(f"w_lo{k}", UNIT, F32R) for k in range(2)]
        self.x = sb("x_stream", KT * SEQ)
        self.ctx_ = sb("ctx_stream", KT * SEQ)
        self.ones = sb("ones", P)
        self.ident = sb("ident", P)
        self.mods = [sb(f"mods{l}", 144) for l in range(2)]
        self.vec = sb("vectors", V_N)
        self.tmp = sb("tmp", 1024)
        self.c_parts = sb("c_parts", 4 * KT, F32R)
        self.dist_bias = nc.dram_tensor("dist_bias", (P, 16, 2 * SEQ - 1), F32)
        self.mhalf = sb("minus_half", 64)
        self.ms = sb("mean_square", 4)
        self.rstd = sb("rstd", 4)
        ps = [ctx.enter_context(nc.psum_tensor(f"ps{k}", [P, 512], F32)) for k in range(8)]
        self.acc, self.X = ps[:4], ps[4:]
        self.loaded = ctx.enter_context(nc.semaphore("loaded"))
        self.mod_done = ctx.enter_context(nc.semaphore("mod_done"))
        self.square_ready = ctx.enter_context(nc.semaphore("square_ready"))
        self.diag_ready = ctx.enter_context(nc.semaphore("diag_ready"))
        self.bc_ready = ctx.enter_context(nc.semaphore("bc_ready"))
        self.sum_ready = ctx.enter_context(nc.semaphore("sum_ready"))
        self.a_ready = ctx.enter_context(nc.semaphore("a_ready"))
        self.act_hi_ready = ctx.enter_context(nc.semaphore("act_hi_ready"))
        self.hi_ready = ctx.enter_context(nc.semaphore("hi_ready"))
        self.rows_ready = ctx.enter_context(nc.semaphore("rows_ready"))
        self.table_ready = ctx.enter_context(nc.semaphore("table_ready"))
        self.table_done = ctx.enter_context(nc.semaphore("table_done"))
        self.table_taken = ctx.enter_context(nc.semaphore("table_taken"))
        self.table_kept = ctx.enter_context(nc.semaphore("table_kept"))
        self.wh_ready = ctx.enter_context(nc.semaphore("wh_ready"))
        self.wl_ready = ctx.enter_context(nc.semaphore("wl_ready"))
        self.acc_done = ctx.enter_context(nc.semaphore("acc_done"))
        self.bank_free = ctx.enter_context(nc.semaphore("bank_free"))
        self.lo_ready = ctx.enter_context(nc.semaphore("lo_ready"))
        self.th_ready = ctx.enter_context(nc.semaphore("th_ready"))
        self.glu_ready = ctx.enter_context(nc.semaphore("glu_ready"))
        self.x_ready = ctx.enter_context(nc.semaphore("x_ready"))
        self.h_ready = ctx.enter_context(nc.semaphore("h_ready"))
        self.sq_ready = ctx.enter_context(nc.semaphore("sq_ready"))
        self.stat_ready = ctx.enter_context(nc.semaphore("stat_ready"))
        self.ms_ready = ctx.enter_context(nc.semaphore("ms_ready"))
        self.rstd_ready = ctx.enter_context(nc.semaphore("rstd_ready"))
        self.xn_ready = ctx.enter_context(nc.semaphore("xn_ready"))
        self.y_ready = ctx.enter_context(nc.semaphore("y_ready"))
        self.dve_seq = ctx.enter_context(nc.semaphore("dve_seq"))
        self.act_seq = ctx.enter_context(nc.semaphore("act_seq"))
        self.pool_seq = ctx.enter_context(nc.semaphore("pool_seq"))
        self.mods_ready = ctx.enter_context(nc.semaphore("mods_ready"))
        self.csq_ready = ctx.enter_context(nc.semaphore("csq_ready"))
        self.csil_ready = ctx.enter_context(nc.semaphore("csil_ready"))
        self.cst_ready = ctx.enter_context(nc.semaphore("cst_ready"))
        self.gelu_a = ctx.enter_context(nc.semaphore("gelu_a"))
        self.gelu_b = ctx.enter_context(nc.semaphore("gelu_b"))
        self.gelu_c = ctx.enter_context(nc.semaphore("gelu_c"))
        self.gelu_d = ctx.enter_context(nc.semaphore("gelu_d"))
        self.y_done = ctx.enter_context(nc.semaphore("y_done"))
        self.yev_ready = ctx.enter_context(nc.semaphore("yev_ready"))
        self.fo_done = ctx.enter_context(nc.semaphore("fo_done"))
        self.vt_done = ctx.enter_context(nc.semaphore("vt_done"))
        self.vt_ready = ctx.enter_context(nc.semaphore("vt_ready"))
        self.mix_done = ctx.enter_context(nc.semaphore("mix_done"))
        self.qg_ready = ctx.enter_context(nc.semaphore("qg_ready"))
        self.rot_done = ctx.enter_context(nc.semaphore("rot_done"))
        self.rope_ready = ctx.enter_context(nc.semaphore("rope_ready"))
        self.rt_done = ctx.enter_context(nc.semaphore("rt_done"))
        self.rt_ready = ctx.enter_context(nc.semaphore("rt_ready"))
        self.hb_done = ctx.enter_context(nc.semaphore("hb_done"))
        self.s_done = ctx.enter_context(nc.semaphore("s_done"))
        self.nm_ready = ctx.enter_context(nc.semaphore("nm_ready"))
        self.p_ready = ctx.enter_context(nc.semaphore("p_ready"))
        self.pn_ready = ctx.enter_context(nc.semaphore("pn_ready"))
        self.t_done = ctx.enter_context(nc.semaphore("t_done"))
        self.pt_ready = ctx.enter_context(nc.semaphore("pt_ready"))
        self.pv_done = ctx.enter_context(nc.semaphore("pv_done"))
        self.o_evac = ctx.enter_context(nc.semaphore("o_evac"))
        self.rk_ready = ctx.enter_context(nc.semaphore("rk_ready"))
        self.st_done = ctx.enter_context(nc.semaphore("st_done"))
        self.st_ready = ctx.enter_context(nc.semaphore("st_ready"))
        self.od_done = ctx.enter_context(nc.semaphore("od_done"))
        self.silu_a = ctx.enter_context(nc.semaphore("silu_a"))
        self.g_ready = ctx.enter_context(nc.semaphore("g_ready"))
        self.lam_a = ctx.enter_context(nc.semaphore("lam_a"))
        self.lam_ready = ctx.enter_context(nc.semaphore("lam_ready"))
        self.stored = ctx.enter_context(nc.semaphore("stored"))
        self.rel_ready = ctx.enter_context(nc.semaphore("rel_ready"))
        self.og_ready = ctx.enter_context(nc.semaphore("og_ready"))
        self.kr_ready = ctx.enter_context(nc.semaphore("kr_ready"))
        self.ost_ready = ctx.enter_context(nc.semaphore("ost_ready"))
        self.raw_full = [ctx.enter_context(nc.semaphore(f"raw_full{k}")) for k in range(RING)]

    def sync_program(self, sp):
        t = Track(sp)
        io = self.io
        for dst, src in ((self.vec, io["vectors"]), (self.ones, io["ones"]), (self.ident, io["ident"]),
                         (self.x, io["x"]), (self.ctx_, io["ctx"])):
            sp.dma_start(dst[:], src).then_inc(self.loaded, t.sent("loaded", 16))

        def load(s, src):
            if s >= RING:
                sp.wait_ge(self.wl_ready, t.due("wl_ready", 2))
            slot = s % RING
            sp.dma_start(self.raw[slot][:, 0:self.split[s].nb * P], src) \
                .then_inc(self.raw_full[slot], t.sent(f"raw_full{slot}", 16))

        def at(w, unit):
            return w[bass.ds(unit, 1)].rearrange("o p n -> (o p) n")

        for g in self.gemms:
            w = io[g.name]
            if g.guests:
                with t.loop(g.guests // 4, {f"raw_full{k}": 32 for k in range(RING)} | {"wl_ready": 16}) as i:
                    for k in range(4):
                        load(g.pos(k), at(w, i * 4 + k))
                        load(g.pos(k) + 1, at(io["mod1"], i * 4 + (g.first_guest + k)))
                for k in range(g.guests, g.units):
                    load(g.pos(k), w[k])
                continue
            for k in range(min(RING, g.units)):
                load(g.pos(k), w[k])
            n = (g.units - RING) // RING
            if n > 0:
                per = {f"raw_full{k}": 16 for k in range(RING)}
                per["wl_ready"] = RING * 2
                with t.loop(n, per) as i:
                    for k in range(RING):
                        load(g.pos(RING + k), at(w, i * RING + (RING + k)))
            for k in range(RING + max(n, 0) * RING, g.units):
                load(g.pos(k), w[k])
        sp.wait_ge(self.x_ready, t.due("x_ready", self.x_tiles))
        sp.dma_start(io["out"], self.x[:]).then_inc(self.stored, t.sent("stored", 16))
        sp.wait_ge(self.stored, t.now("stored"))

    def act_split(self, t, s, halves=(0, 1)):
        act = t.eng
        if s >= len(self.split):
            return
        g, slot, w = self.split[s], s % RING, s % 2
        if 0 in halves:
            act.wait_ge(self.raw_full[slot], t.due(f"raw_full{slot}", 16))
        for half in halves:
            a, b = ((0, g.half), (g.half, g.nb))[half]
            self.nc.scalar.activation(
                self.wh[w][:, a * P:b * P], self.raw[slot][:, a * P:b * P], ACT.Copy) \
                .then_inc(self.wh_ready, t.sent("wh_ready"))

    def dve_split(self, t, s, halves=(0, 1)):
        dve = t.eng
        if s >= len(self.split):
            return
        g, slot, w = self.split[s], s % RING, s % 2
        for half in halves:
            a, b = ((0, g.half), (g.half, g.nb))[half]
            dve.wait_ge(self.wh_ready, t.due("wh_ready"))
            self.nc.vector.tensor_tensor(
                self.wl[w][:, a * P:b * P], self.raw[slot][:, a * P:b * P],
                self.wh[w][:, a * P:b * P].bitcast(F32), ALU.subtract).then_inc(self.wl_ready, t.sent("wl_ready"))

    def raw_per(self, g):
        return {f"raw_full{k}": 16 * g.group * (2 if g.guests else 1) // RING for k in range(RING)}

    def pe_gemm(self, t, name):
        pe = t.eng
        g = self.by_name[name]
        nc = self.nc
        src = self.act if g.src == "act" else self.h

        def block(bank, w, blk, kt, first, last):
            hi, lo = self.wh[w][:, blk * P:blk * P + P], self.wl[w][:, blk * P:blk * P + P]
            acc = self.acc[bank]
            if g.mode == "cat":
                prods = [(acc[:, 0:512], hi, src[:, kt * 512:kt * 512 + 512]),
                         (acc[:, 0:256], lo, src[:, kt * 512:kt * 512 + 256])]
            else:
                n = 256 if g.mode == "xonly" else 512
                a_hi, a_lo = src[:, kt * 1024:kt * 1024 + n], src[:, kt * 1024 + 512:kt * 1024 + 512 + n]
                prods = [(acc[:, 0:n], hi, a_hi), (acc[:, 0:n], lo, a_hi), (acc[:, 0:n], hi, a_lo)]
            if last:
                prods = prods[1:] + prods[:1]
            for j, (o, wgt, mov) in enumerate(prods):
                ins = nc.tensor.matmul(o, wgt, mov, start=first and j == 0, stop=last and j == len(prods) - 1)
            return ins

        signals, total = {"out_ab": (lambda kt: kt + 5, 12), "kv": (lambda kt: 0, 0), "o": (lambda kt: 16, 16),
                          "moba_out": (lambda kt: 16, 16), "ret_out0": (lambda kt: kt // 4 * 4 + 4, 16),
                          "ret_out1": (lambda kt: kt // 4 * 4 + 4, 16)}.get(name, (lambda kt: kt + 1, g.kt))

        def arrived(kt):
            if g.src == "h":
                pe.wait_ge(self.h_ready, t.at("h_ready", self.h_total[name] - total + signals(kt)))
            else:
                pe.wait_ge(self.glu_ready, t.at("glu_ready", self.act_total[name] - total + signals(kt)))

        def unit(k):
            w = g.pos(k) % 2
            if g.kt == 8:
                for j in range(2):
                    pe.wait_ge(self.bank_free, t.due("bank_free"))
                    pe.wait_ge(self.wl_ready, t.due("wl_ready"))
                    for kt in range(8):
                        if k % g.group == 0 and j == 0:
                            arrived(kt)
                        ins = block((2 * k + j) % 4, w, 8 * j + kt, kt, kt == 0, kt == 7)
                    ins.then_inc(self.acc_done, t.sent("acc_done"))
            else:
                per_tile = g.kt // g.nb
                tile, part = k // per_tile, k % per_tile
                if part == 0:
                    pe.wait_ge(self.bank_free, t.due("bank_free"))
                for a, b in ((0, g.half), (g.half, g.nb)):
                    pe.wait_ge(self.wl_ready, t.due("wl_ready"))
                    for blk in range(a, b):
                        kt = part * g.nb + blk
                        if k % g.group < per_tile:
                            arrived(kt)
                        ins = block(tile % 4, w, blk, kt, kt == 0, kt == g.kt - 1)
                ins.then_inc(self.acc_done, t.sent("acc_done"))

        n = g.guests // 4 if g.guests else g.units // g.group
        if n > 1:
            tiles = g.group * g.tiles // g.units
            per = {"bank_free": tiles, "wl_ready": 2 * g.group, "acc_done": g.parts * g.group}
            if g.guests:
                per.update({"wl_ready": 4 * g.group, "acc_done": (g.parts + 1) * g.group,
                            "rows_ready": 2, "mod_done": 1})
            t.at("h_ready" if g.src == "h" else "glu_ready",
                 self.h_total[name] if g.src == "h" else self.act_total[name])
            with t.loop(n, per) as i:
                for k in range(g.group):
                    unit(k)
                    if g.guests:
                        if k == 2:
                            self.pe_mod_columns(t, self.X[1], G_ROWS, 0, i)
                        self.pe_mod_unit(t, k, (g.pos(k) + 1) % 2, self.X[2 + k // 2])
                        if k == 3:
                            self.pe_mod_columns(t, self.X[1], G_ROWS, 1, i) \
                                .then_inc(self.mod_done, t.sent("mod_done"))
        else:
            n = 0
        for k in range(n * g.group, g.units):
            unit(k)

    def act_gemm(self, t, name):
        act = t.eng
        g = self.by_name[name]
        nc, tmp = self.nc, self.tmp
        if g.s0 == 0:
            self.act_split(t, 0)
            self.act_split(t, 1)

        def squares(end):
            n = 2 if g.kt == 8 else 1
            for j in range(n):
                if g.mode == "wide":
                    act.wait_ge(self.x_ready, t.due("x_ready"))
                    act.wait_ge(self.bank_free, t.due("bank_free"))
                elif j == 0:
                    act.wait_ge(self.x_ready, t.now("x_ready"))
                self.act_square(t, end - n + j, g.mode == "wide")

        def unit(k):
            rest = (0, 1)
            if g.kt == 8 and g.kind != "mod":
                act.wait_ge(self.acc_done, t.due("acc_done"))
                self.act_split(t, g.pos(k) + 2, (0,))
                rest = (1,)
                act.wait_ge(self.acc_done, t.due("acc_done"))
            else:
                act.wait_ge(self.acc_done, t.due("acc_done"))
            if g.kind == "mod" and k % 2:
                group = k // 2 % 2
                nc.scalar.activation(
                    self.ar[0:4, 512 * group:512 * group + 512], self.acc[group][0:4, :], ACT.Copy) \
                    .then_inc(self.rows_ready, t.sent("rows_ready"))
            early = g.kind == "res" and g.mode == "wide"
            if g.mode != "cat" and not early:
                self.act_split(t, g.pos(k) + 2, rest)
            per_tile = g.kt // g.nb if g.kt > 16 else 1
            if g.kind == "mod":
                return
            if k % per_tile != per_tile - 1:
                if g.mode == "cat" or early:
                    self.act_split(t, g.pos(k) + 2)
                if g.kind == "res" and k and not last_gemm:
                    squares(k // per_tile)
                return
            tile0 = 2 * k if g.kt == 8 else k // per_tile
            tiles = 2 if g.kt == 8 else 1
            if g.kind == "glu" and g.mode == "wide":
                act.wait_ge(self.glu_ready, t.now("glu_ready"))
                nc.scalar.activation(
                    tmp[:, 0:512], self.acc[tile0 % 4][:], ACT.Tanh, scale=0.5) \
                    .then_inc(self.th_ready, t.sent("th_ready"))
                t.add("glu_ready")
                return
            if early:
                if per_tile == 1 and tile0:
                    squares(tile0)
                if k == g.units - 1:
                    squares(g.tiles)
                self.act_split(t, g.pos(k) + 2, rest)
                return
            if g.mode != "cat":
                return
            used = {"plain": "bank_free", "res": "x_ready", "glu": "a_ready", "relu2": "a_ready"}[g.kind]
            if used == "a_ready":
                act.wait_ge(self.a_ready, t.now("a_ready"))
            elif used == "x_ready":
                act.wait_ge(self.x_ready, t.now("x_ready"))
            else:
                act.wait_ge(self.bank_free, t.now("bank_free"))
            if g.kind == "res" and per_tile == 1 and tile0 and not last_gemm:
                squares(tile0)
            for j in range(tiles):
                nc.scalar.activation(
                    tmp[:, j * 256:j * 256 + 256], self.acc[(tile0 + j) % 4][:, 256:512], ACT.Copy) \
                    .then_inc(self.lo_ready, t.sent("lo_ready"))
            t.add(used, 1 if used == "a_ready" else tiles)
            if g.kind != "glu":
                if g.kind == "res" and k == g.units - 1 and not last_gemm:
                    squares(g.tiles)
                self.act_split(t, g.pos(k) + 2, rest)
            else:
                act.wait_ge(self.g_ready, t.due("g_ready"))
                nc.scalar.activation(
                    tmp[:, 512:768], tmp[:, 0:256], ACT.Tanh, scale=0.5).then_inc(self.th_ready, t.sent("th_ready"))
                self.act_split(t, g.pos(k) + 2, (1,))

        def guest(k):
            act.wait_ge(self.acc_done, t.due("acc_done"))
            if k % 2:
                nc.scalar.activation(self.a(G_ROWS + 512 * (k // 2), 512, 0, 4), self.X[2 + k // 2][0:4, :], ACT.Copy) \
                    .then_inc(self.rows_ready, t.sent("rows_ready"))
            self.act_split(t, g.pos(k) + 3)

        n = g.guests // 4 if g.guests else (g.units - 2) // g.group
        last_gemm = g is self.gemms[-1]
        if n > 1 and g.kind != "res":
            per = self.raw_per(g)
            per["wh_ready"] = 2 * g.group
            per["acc_done"] = g.parts * g.group
            if g.guests:
                per.update({"wh_ready": 4 * g.group, "acc_done": (g.parts + 1) * g.group, "rows_ready": 2})
            if g.kind == "glu":
                per["glu_ready" if g.mode == "wide" else "a_ready"] = per["th_ready"] = g.group
            if g.kind == "mod":
                per["rows_ready"] = 2
            if g.mode == "cat":
                tiles = g.group * g.tiles // g.units
                per["lo_ready"] = tiles
                if g.kind == "glu":
                    per["g_ready"] = g.group
                elif g.kind == "plain":
                    per["bank_free"] = tiles
                else:
                    per["a_ready"] = g.group
            with t.loop(n, per):
                for k in range(g.group):
                    unit(k)
                    if g.guests:
                        guest(k)
        else:
            n = 0
        for k in range(n * g.group, g.units):
            unit(k)
        if g.kind != "mod" and (g.mode, g.kind) not in (("cat", "plain"), ("wide", "res")):
            t.add("bank_free", g.tiles)

    def dve_gemm(self, t, name):
        dve = t.eng
        g = self.by_name[name]
        nc, tmp, v = self.nc, self.tmp, self.nc.vector
        if g.s0 == 0:
            self.dve_split(t, 0)
            self.dve_split(t, 1)

        def cols(tensor, base, stride, k, n):
            if t.reg is None:
                return tensor[:, base + stride * k:base + stride * k + n]
            return tensor[:, bass.ds(t.reg * (stride * step) + (base + stride * k), n)]

        def unit(k):
            rest = (0, 1)
            if g.kt == 8 and g.kind != "mod":
                dve.wait_ge(self.acc_done, t.due("acc_done"))
                self.dve_split(t, g.pos(k) + 2, (0,))
                rest = (1,)
                dve.wait_ge(self.acc_done, t.due("acc_done"))
            else:
                dve.wait_ge(self.acc_done, t.due("acc_done"))
            per_tile = g.kt // g.nb if g.kt > 16 else 1
            end = k % per_tile == per_tile - 1
            late = g.mode == "cat" or g.kind == "res"
            if not late or not end:
                self.dve_split(t, g.pos(k) + 2, rest)
            if g.kind == "mod" or not end:
                return
            tile0 = 2 * k if g.kt == 8 else k // per_tile
            tiles = 2 if g.kt == 8 else 1
            banks = [self.acc[(tile0 + j) % 4] for j in range(tiles)]
            if g.kind == "glu":
                w = 512 if g.mode == "wide" else 256
                if g.mode == "wide":
                    gate, up, th, a = banks[0][:], banks[1][:], tmp[:, 0:512], tmp[:, 512:1024]
                else:
                    gate, up, th, a = tmp[:, 0:256], tmp[:, 256:512], tmp[:, 512:768], tmp[:, 768:1024]
                    dve.wait_ge(self.lo_ready, t.due("lo_ready"))
                    v.tensor_tensor(
                        gate, banks[0][:, 0:256], gate, ALU.add).then_inc(self.bank_free, t.sent("bank_free"))
                    dve.wait_ge(self.bank_free, t.now("bank_free"))
                    v.memset(self.ms[:, 0:1], 0.0).then_inc(self.g_ready, t.sent("g_ready"))
                    dve.wait_ge(self.lo_ready, t.due("lo_ready"))
                    v.tensor_tensor(up, banks[1][:, 0:256], up, ALU.add).then_inc(self.bank_free, t.sent("bank_free"))
                    dve.wait_ge(self.bank_free, t.now("bank_free"))
                dve.wait_ge(self.th_ready, t.due("th_ready"))
                if g.mode == "wide":
                    v.scalar_tensor_tensor(
                        th, th, 1.0, gate, ALU.add, ALU.mult).then_inc(self.bank_free, t.sent("bank_free"))
                    dve.wait_ge(self.bank_free, t.now("bank_free"))
                    v.scalar_tensor_tensor(
                        a, th, 0.5, up, ALU.mult, ALU.mult).then_inc(self.bank_free, t.sent("bank_free"))
                    dve.wait_ge(self.bank_free, t.now("bank_free"))
                else:
                    v.scalar_tensor_tensor(
                        th, th, 1.0, gate, ALU.add, ALU.mult).then_inc(self.dve_seq, t.sent("dve_seq"))
                    dve.wait_ge(self.dve_seq, t.now("dve_seq"))
                    dve.wait_ge(self.glu_ready, t.now("glu_ready"))
                    v.scalar_tensor_tensor(
                        a, th, 0.5, up, ALU.mult, ALU.mult).then_inc(self.a_ready, t.sent("a_ready"))
                    t.add("glu_ready")
                    self.dve_split(t, g.pos(k) + 2, (1,))
                    return
                stride = 2 * w
                hi, lo = cols(self.act, 0, stride, k, w), cols(self.act, w, stride, k, w)
                v.tensor_copy(hi, a).then_inc(self.dve_seq, t.sent("dve_seq"))
                dve.wait_ge(self.dve_seq, t.now("dve_seq"))
                v.tensor_tensor(lo, a, hi.bitcast(F32), ALU.subtract).then_inc(self.glu_ready, t.sent("glu_ready"))
                dve.wait_ge(self.glu_ready, t.now("glu_ready"))
                return
            for j in range(tiles):
                tile, bank = tile0 + j, banks[j]
                lo_sum = tmp[:, j * 256:j * 256 + 256]
                if g.mode == "cat":
                    dve.wait_ge(self.lo_ready, t.due("lo_ready"))
                if g.kind == "plain":
                    w = g.kw["w"]
                    dst = cols(self.ar, g.kw["at"], w, tile, w)
                    if g.mode == "cat":
                        v.tensor_tensor(
                            dst, bank[:, 0:256], lo_sum, ALU.add).then_inc(self.bank_free, t.sent("bank_free"))
                    else:
                        v.tensor_copy(dst, bank[:, 0:w]).then_inc(self.bank_free, t.sent("bank_free"))
                elif g.kind == "relu2":
                    v.tensor_tensor(
                        lo_sum, bank[:, 0:256], lo_sum, ALU.add).then_inc(self.bank_free, t.sent("bank_free"))
                else:
                    x = self.x[:, tile * 256:tile * 256 + 256]
                    if g.mode == "wide":
                        l, m = g.kw["gate"]
                        for s, res in ((0, self.x), (1, self.ctx_)):
                            r = res[:, tile * 256:tile * 256 + 256]
                            gate = self.mods[l][:, (m * 8 + tile) * 2 + s:(m * 8 + tile) * 2 + s + 1]
                            ins = v.scalar_tensor_tensor(
                                r, bank[:, s * 256:s * 256 + 256], gate, r, ALU.mult, ALU.add)
                            if s:
                                ins.then_inc(self.bank_free, t.sent("bank_free"))
                            else:
                                ins.then_inc(self.x_ready, t.sent("x_ready"))
                        continue
                    v.tensor_tensor(
                        lo_sum, bank[:, 0:256], lo_sum, ALU.add).then_inc(self.bank_free, t.sent("bank_free"))
                    dve.wait_ge(self.bank_free, t.now("bank_free"))
                    if g.kw["gate"]:
                        l, m = g.kw["gate"]
                        gate = self.mods[l][:, (m * 8 + tile) * 2:(m * 8 + tile) * 2 + 1]
                        v.scalar_tensor_tensor(
                            x, lo_sum, gate, x, ALU.mult, ALU.add).then_inc(self.x_ready, t.sent("x_ready"))
                    else:
                        v.tensor_tensor(x, lo_sum, x, ALU.add).then_inc(self.x_ready, t.sent("x_ready"))
            if g.kind == "relu2":
                dve.wait_ge(self.bank_free, t.now("bank_free"))
                dve.wait_ge(self.glu_ready, t.now("glu_ready"))
                v.scalar_tensor_tensor(tmp[:, 512:1024], tmp[:, 0:512], 0.0, tmp[:, 0:512], ALU.max, ALU.mult) \
                    .then_inc(self.a_ready, t.sent("a_ready"))
                t.add("glu_ready", 2)
            if late:
                self.dve_split(t, g.pos(k) + 2, rest)

        def guest(k):
            dve.wait_ge(self.acc_done, t.due("acc_done"))
            self.dve_split(t, g.pos(k) + 3)

        n, step = g.guests // 4 if g.guests else (g.units - 2) // g.group, g.group * g.tiles // g.units
        if g.kind == "glu":
            step = g.group
        if n > 1 and g.kind != "res":
            per = {"wh_ready": 2 * g.group, "wl_ready": 2 * g.group, "acc_done": g.parts * g.group}
            if g.guests:
                per = {"wh_ready": 4 * g.group, "wl_ready": 4 * g.group, "acc_done": (g.parts + 1) * g.group}
            tiles = g.group * g.tiles // g.units
            if g.kind != "mod":
                per["bank_free"] = tiles
            if g.mode == "cat":
                per["lo_ready"] = tiles
            if g.kind == "glu":
                per["glu_ready"] = per["th_ready"] = g.group
                per["dve_seq"] = g.group
                if g.mode == "cat":
                    per["g_ready"] = per["a_ready"] = g.group
            if g.kind == "relu2":
                per["glu_ready"] = tiles
                per["a_ready"] = g.group
            with t.loop(n, per):
                for k in range(g.group):
                    unit(k)
                    if g.guests:
                        guest(k)
        else:
            n = 0
        for k in range(n * g.group, g.units):
            unit(k)
        dve.wait_ge(self.bank_free, t.now("bank_free"))

    def pool_gemm(self, t, name):
        pool = t.eng
        g, q = self.by_name[name], self.nc.gpsimd
        n_tiles = 2 if g.kind == "relu2" else 1

        def unit(k):
            pool.wait_ge(self.a_ready, t.due("a_ready"))
            a = self.tmp[:, 1024 - 256 * n_tiles:1024].rearrange("p (j n) -> p j n", n=256)
            w = 512 * n_tiles
            dst = self.act[:, bass.ds(t.reg * (4 * w) + w * k, w)].rearrange("p (j s n) -> p j s n", s=2, n=256) \
                if t.reg is not None else \
                self.act[:, w * k:w * k + w].rearrange("p (j s n) -> p j s n", s=2, n=256)
            hi, lo = dst[:, :, 0, :], dst[:, :, 1, :]
            q.tensor_copy(hi, a).then_inc(self.pool_seq, t.sent("pool_seq"))
            pool.wait_ge(self.pool_seq, t.now("pool_seq"))
            q.tensor_tensor(lo, a, hi.bitcast(F32), ALU.subtract).then_inc(self.glu_ready, t.sent("glu_ready", n_tiles))

        n = g.units // 4
        with t.loop(n, {"a_ready": 4, "pool_seq": 4, "glu_ready": 4 * n_tiles}):
            for k in range(4):
                unit(k)
        for k in range(4 * n, g.units):
            unit(k)

    T_OH, T_REL, T_OUT = 1024, 1536, 8192

    def pe_start(self, t):
        pe = t.eng
        pe.wait_ge(self.table_ready, t.due("table_ready", 2 * 16))
        pe.wait_ge(self.rel_ready, t.due("rel_ready"))
        self.nc.tensor.matmul(self.X[3][0:16, 0:2 * SEQ - 1], self.a(self.T_REL, 16, 0, 33),
                              self.a(self.T_OH, 2 * SEQ - 1, 0, 33), start=True, stop=True) \
            .then_inc(self.table_done, t.sent("table_done"))

    def act_start(self, t):
        act = t.eng
        self.nc.scalar.dma_start(self.a(self.T_OH, 2 * SEQ - 1, 0, 33), self.io["bucket"]) \
            .then_inc(self.table_ready, t.sent("table_ready", 16))
        self.nc.scalar.dma_start(self.a(self.T_REL, 16, 0, 32), self.io["rel_bias"]) \
            .then_inc(self.table_ready, t.sent("table_ready", 16))
        act.wait_ge(self.loaded, t.due("loaded", 5 * 16))
        self.nc.scalar.activation(
            self.tmp[:, 16:32], self.vec[:, V_C:V_C + 16], ACT.Tanh, scale=0.5) \
            .then_inc(self.csq_ready, t.sent("csq_ready"))
        t.add("bank_free", 4)
        t.add("glu_ready")
        t.add("a_ready")
        act.wait_ge(self.table_done, t.due("table_done"))
        self.nc.scalar.activation(
            self.a(self.T_OUT, 2 * SEQ - 1, 0, 16), self.X[3][0:16, 0:2 * SEQ - 1], ACT.Copy) \
            .then_inc(self.table_taken, t.sent("table_taken"))
        act.wait_ge(self.table_taken, t.now("table_taken"))
        rows = self.a(self.T_OUT, 2 * SEQ - 1, 0, 16).unsqueeze(1).broadcast_to([16, P, 2 * SEQ - 1])
        self.nc.scalar.dma_start(self.dist_bias[:].rearrange("p h m -> h p m"), rows) \
            .then_inc(self.table_kept, t.sent("table_kept", 16))

    def pool_start(self, t):
        pool = t.eng
        self.nc.gpsimd.memset(self.mhalf[:], -0.5).then_inc(self.pool_seq, t.sent("pool_seq"))
        pool.wait_ge(self.pool_seq, t.now("pool_seq"))
        t.add("a_ready")

    def dve_start(self, t):
        dve = t.eng
        v = self.nc.vector
        v.memset(self.ms[:], 0.0).then_inc(self.bank_free, t.sent("bank_free", 4))
        v.memset(self.rstd[:], 0.0).then_inc(self.glu_ready, t.sent("glu_ready"))
        v.memset(self.tmp[:, 1020:1024], 0.0).then_inc(self.a_ready, t.sent("a_ready"))
        v.memset(self.a(self.T_REL, 16, 32, 33), -1e30).then_inc(self.rel_ready, t.sent("rel_ready"))
        dve.wait_ge(self.loaded, t.due("loaded", 5 * 16))
        dve.wait_ge(self.csq_ready, t.due("csq_ready"))
        th, c = self.tmp[:, 16:32], self.vec[:, V_C:V_C + 16]
        v.scalar_tensor_tensor(th, th, 1.0, c, ALU.add, ALU.mult).then_inc(self.dve_seq, t.sent("dve_seq"))
        dve.wait_ge(self.dve_seq, t.now("dve_seq"))
        sc = self.tmp[:, 0:16]
        v.tensor_scalar(sc, th, 0.5, None, ALU.mult).then_inc(self.dve_seq, t.sent("dve_seq"))
        dve.wait_ge(self.dve_seq, t.now("dve_seq"))
        parts = self.c_parts[:].rearrange("p (k h s) -> p k h s", k=KT, h=2)
        sc = sc.rearrange("p (k s) -> p k s", k=KT)
        v.tensor_copy(parts[:, :, 0, :], sc).then_inc(self.dve_seq, t.sent("dve_seq"))
        dve.wait_ge(self.dve_seq, t.now("dve_seq"))
        v.tensor_tensor(parts[:, :, 1, :], sc, parts[:, :, 0, :].bitcast(F32), ALU.subtract) \
            .then_inc(self.csil_ready, t.sent("csil_ready"))

    def pe_mod_unit(self, t, k, w, bank):
        pe = t.eng
        for half in range(2):
            pe.wait_ge(self.wl_ready, t.due("wl_ready"))
            for j in (2 * half, 2 * half + 1):
                kt = 4 * (k % 2) + j
                for low, part in enumerate((self.wh[w], self.wl[w])):
                    ins = self.nc.tensor.matmul(bank[0:4, :], self.c_parts[:, 4 * kt:4 * kt + 4],
                                                part[:, 512 * j:512 * j + 512], start=kt == 0 and not low,
                                                stop=kt == KT - 1 and low == 1)
        ins.then_inc(self.acc_done, t.sent("acc_done"))

    def pe_mod_columns(self, t, bank, rows, g, i):
        pe = t.eng
        pe.wait_ge(self.rows_ready, t.due("rows_ready"))
        for j in range(4):
            ins = self.nc.tensor.matmul(bank[:, bass.ds(i * 16 + (8 * g + 2 * j), 2)],
                                        self.a(rows + 512 * g + P * j, P, 0, 4), self.vec[0:4, V_PAIR:V_PAIR + 2],
                                        start=True, stop=True)
        return ins

    def pe_mod(self, t):
        pe = t.eng
        pe.wait_ge(self.csil_ready, t.due("csil_ready"))
        with t.loop(9, {"wl_ready": 8, "acc_done": 4, "rows_ready": 2, "mod_done": 1}) as i:
            for k in range(4):
                self.pe_mod_unit(t, k, k % 2, self.acc[k // 2])
                if k == 2:
                    self.pe_mod_columns(t, self.X[0], 0, 0, i)
            self.pe_mod_columns(t, self.X[0], 0, 1, i).then_inc(self.mod_done, t.sent("mod_done"))

    def dve_mod_bias(self, t, l, tile, n):
        dve = t.eng
        dve.wait_ge(self.mod_done, t.due("mod_done", n // 8))
        b = self.vec[:, V_BMOD + 72 * l + tile:V_BMOD + 72 * l + tile + n].unsqueeze(2).broadcast_to([P, n, 2])
        self.nc.vector.tensor_tensor(
            self.mods[l][:, 2 * tile:2 * tile + 2 * n].rearrange("p (a b) -> p a b", b=2),
            self.X[l][:, 0:2 * n].rearrange("p (a b) -> p a b", b=2), b, ALU.add) \
            .then_inc(self.dve_seq, t.sent("dve_seq"))
        dve.wait_ge(self.dve_seq, t.now("dve_seq"))

    def dve_mod(self, t, l):
        dve = t.eng
        v, m = self.nc.vector, self.mods[l]
        for scale, gain, gate in ((1, V_FFN1, 2), (4, V_MIX, None), (7, V_FFN2, 8)):
            cut = m[:, scale * 16:scale * 16 + 16].rearrange("p (a b) -> p a b", b=2)
            gb = self.vec[:, gain + 8 * l:gain + 8 * l + 8].unsqueeze(2).broadcast_to([P, 8, 2])
            v.scalar_tensor_tensor(cut, cut, 1.0, gb, ALU.add, ALU.mult).then_inc(self.dve_seq, t.sent("dve_seq"))
            if gate:
                cut = m[:, gate * 16:gate * 16 + 16]
                v.tensor_scalar(cut, cut, 0.5, None, ALU.mult).then_inc(self.dve_seq, t.sent("dve_seq"))
        dve.wait_ge(self.dve_seq, t.now("dve_seq"))
        v.memset(self.ms[:, 0:1], 0.0).then_inc(self.mods_ready, t.sent("mods_ready"))
        dve.wait_ge(self.mods_ready, t.now("mods_ready"))

    def norm_cols(self, what, s):
        if what[0] == "mod":
            _, l, m = what
            return (lambda kt: self.mods[l][:, ((m + 1) * 8 + kt) * 2 + s:((m + 1) * 8 + kt) * 2 + s + 1],
                    lambda kt: self.mods[l][:, (m * 8 + kt) * 2 + s:(m * 8 + kt) * 2 + s + 1])
        return (lambda kt: self.vec[:, what[1] + kt:what[1] + kt + 1]), (lambda kt: 0.0)

    def norm_dst(self, wide, s, kt):
        if wide:
            return [self.h[:, kt * 1024 + 512 * p + 256 * s:kt * 1024 + 512 * p + 256 * s + 256] for p in (0, 1)]
        return [self.h[:, kt * 512 + 256 * p:kt * 512 + 256 * p + 256] for p in (0, 1)]

    def streams(self, wide):
        return (self.x, self.ctx_) if wide else (self.x,)

    def norm_y(self, wide, kt):
        return self.a(A_OUT + 512 * (kt % 3), 512 if wide else 256)

    def norm_sq(self, wide):
        return self.tmp[:, 0:512] if wide else self.tmp[:, 768:1024]

    def act_square(self, t, kt, wide):
        act = t.eng
        if kt:
            act.wait_ge(self.sum_ready, t.due("sum_ready"))
        for s, src in enumerate(self.streams(wide)):
            ins = self.nc.scalar.activation(self.norm_sq(wide)[:, 256 * s:256 * s + 256],
                                            src[:, kt * 256:kt * 256 + 256], ACT.Square)
        ins.then_inc(self.square_ready, t.sent("square_ready"))

    def pool_sums(self, t, wide):
        pool = t.eng
        g, w = self.nc.gpsimd, 512 if wide else 256
        total, sq = self.tmp[:, N_SUM:N_SUM + w], self.norm_sq(wide)
        for kt in range(KT - 1):
            pool.wait_ge(self.square_ready, t.due("square_ready"))
            if kt == 0:
                g.tensor_copy(total, sq).then_inc(self.sum_ready, t.sent("sum_ready"))
            else:
                pool.wait_ge(self.sum_ready, t.now("sum_ready"))
                g.tensor_tensor(total, total, sq, ALU.add).then_inc(self.sum_ready, t.sent("sum_ready"))
        t.add("square_ready")

    def act_norm(self, t, what, wide):
        act = t.eng
        nc = self.nc
        if what[0] == "mod":
            act.wait_ge(self.mods_ready, t.at("mods_ready", what[1] + 1))
            act.wait_ge(self.table_kept, t.now("table_kept"))
        for kt in range(KT):
            y = self.norm_y(wide, kt)
            act.wait_ge(self.xn_ready, t.due("xn_ready"))
            for s, src in enumerate(self.streams(wide)):
                a, b = self.norm_cols(what, s)
                ys = y[:, 256 * s:256 * s + 256]
                if what[0] == "final":
                    ins = nc.scalar.activation(src[:, kt * 256:kt * 256 + 256], ys, ACT.Identity, scale=a(kt))
                else:
                    ins = nc.scalar.activation(ys, ys, ACT.Identity, scale=a(kt), bias=b(kt))
            ins.then_inc(self.y_ready, t.sent("y_ready"))
            if what[0] == "final":
                act.wait_ge(self.y_ready, t.now("y_ready"))
                self.act_square(t, kt, wide)
            if kt % 2 and what[0] != "final":
                act.wait_ge(self.y_ready, t.now("y_ready"))
                w = 512 if wide else 256
                nc.scalar.activation(self.h[:, kt * 2 * w:kt * 2 * w + w], y, ACT.Copy) \
                    .then_inc(self.act_hi_ready, t.sent("act_hi_ready"))

    def pe_norm(self, t, what, wide):
        pe = t.eng
        nc, w = self.nc, 512 if wide else 256
        if what[0] == "mod":
            pe.wait_ge(self.mods_ready, t.at("mods_ready", what[1] + 1))
        pe.wait_ge(self.sum_ready, t.due("sum_ready", KT - 1))
        for k, sq in enumerate((self.tmp[:, N_SUM:N_SUM + w], self.norm_sq(wide))):
            if k:
                pe.wait_ge(self.square_ready, t.due("square_ready", KT))
            for tt in range(w // P):
                ins = nc.tensor.matmul(self.X[0][:, tt:tt + 1], sq[:, tt * P:tt * P + P], self.ones[:, 0:1],
                                       start=k == 0 and tt == 0, stop=k == 1 and tt == w // P - 1)
        ins.then_inc(self.stat_ready, t.sent("stat_ready"))
        t.add("rstd_ready")
        pe.wait_ge(self.diag_ready, t.due("diag_ready"))
        nc.tensor.matmul(self.X[1][:, 0:w], self.ones[:], self.tmp[:, N_SUM:N_SUM + w], start=True, stop=True) \
            .then_inc(self.bc_ready, t.sent("bc_ready"))

    def pool_norm(self, t, what, wide):
        pool = t.eng
        g, w = self.nc.gpsimd, 512 if wide else 256
        self.pool_sums(t, wide)
        pool.wait_ge(self.ms_ready, t.due("ms_ready"))
        g.tensor_tensor(self.rstd[:, 0:w // P], self.ms[:, 0:w // P], self.mhalf[:, 0:w // P], ALU.pow) \
            .then_inc(self.rstd_ready, t.sent("rstd_ready"))
        if what[0] == "final":
            t.add("y_ready", KT)
            return
        for kt in range(0, KT, 2):
            pool.wait_ge(self.y_ready, t.due("y_ready", 2 if kt else 1))
            hi = self.h[:, kt * 2 * w:kt * 2 * w + w]
            g.tensor_copy(hi, self.norm_y(wide, kt)).then_inc(self.hi_ready, t.sent("hi_ready"))
        t.add("y_ready")

    def dve_norm(self, t, what, wide):
        dve = t.eng
        v, w = self.nc.vector, 512 if wide else 256
        rs = self.X[1][:, 0:w]
        dve.wait_ge(self.stat_ready, t.due("stat_ready"))
        dve.wait_ge(self.dve_seq, t.now("dve_seq"))
        v.tensor_scalar(self.ms[:, 0:w // P], self.X[0][:, 0:w // P], 1.0 / D, EPS, ALU.mult, ALU.add) \
            .then_inc(self.ms_ready, t.sent("ms_ready"))
        if t.begun("x_ready"):
            dve.wait_ge(self.x_ready, t.now("x_ready"))
        dve.wait_ge(self.bank_free, t.now("bank_free"))
        dve.wait_ge(self.rstd_ready, t.due("rstd_ready"))
        v.tensor_tensor(self.tmp[:, N_SUM:N_SUM + w].rearrange("p (a b) -> p a b", b=P),
                        self.ident[:].unsqueeze(1).broadcast_to([P, w // P, P]),
                        self.rstd[:, 0:w // P].unsqueeze(2).broadcast_to([P, w // P, P]), ALU.mult) \
            .then_inc(self.diag_ready, t.sent("diag_ready"))
        dve.wait_ge(self.bc_ready, t.due("bc_ready"))

        def low(kt):
            if what[0] == "final":
                dve.wait_ge(self.y_ready, t.due("y_ready"))
                return
            if kt % 2:
                dve.wait_ge(self.act_hi_ready, t.due("act_hi_ready"))
            else:
                dve.wait_ge(self.hi_ready, t.due("hi_ready"))
            hi, lo = self.h[:, kt * 2 * w:kt * 2 * w + w], self.h[:, kt * 2 * w + w:kt * 2 * w + 2 * w]
            v.tensor_tensor(lo, self.norm_y(wide, kt), hi.bitcast(F32), ALU.subtract) \
                .then_inc(self.h_ready, t.sent("h_ready"))

        for kt in range(KT):
            if kt >= 3 and what[0] != "final":
                dve.wait_ge(self.h_ready, t.now("h_ready"))
            y = self.norm_y(wide, kt)
            for s, src in enumerate(self.streams(wide)):
                ins = v.tensor_tensor(y[:, 256 * s:256 * s + 256], src[:, kt * 256:kt * 256 + 256],
                                      rs[:, 256 * s:256 * s + 256], ALU.mult)
            ins.then_inc(self.xn_ready, t.sent("xn_ready"))
            if kt >= 2:
                low(kt - 2)
        low(KT - 2)
        low(KT - 1)
        if what[0] != "final":
            dve.wait_ge(self.h_ready, t.now("h_ready"))
            t.add("y_ready", KT)

    def load_consts(self, t, parts):
        for dst, src in parts:
            self.nc.scalar.dma_start(dst, src).then_inc(self.cst_ready, t.sent("cst_ready", 16))

    def a(self, col, n, p0=0, p1=P):
        return self.ar[p0:p1, col:col + n]

    def dve_stat(self, t, src, dst, d, ready="stat_ready", n=1):
        dve = t.eng
        dve.wait_ge({"stat_ready": self.stat_ready, "ost_ready": self.ost_ready}[ready], t.due(ready, n))
        self.nc.vector.tensor_scalar(
            dst, src, 1.0 / d, EPS, ALU.mult, ALU.add).then_inc(self.ms_ready, t.sent("ms_ready"))
        dve.wait_ge(self.ms_ready, t.now("ms_ready"))

    def pool_stat(self, t, r, n):
        pool = t.eng
        pool.wait_ge(self.ms_ready, t.due("ms_ready"))
        self.nc.gpsimd.tensor_tensor(
            r, r, self.mhalf[:, 0:n], ALU.pow).then_inc(self.rstd_ready, t.sent("rstd_ready"))

    def dve_parts(self, t, y, hi, lo):
        dve = t.eng
        v = self.nc.vector
        v.tensor_copy(hi, y).then_inc(self.dve_seq, t.sent("dve_seq"))
        dve.wait_ge(self.dve_seq, t.now("dve_seq"))
        v.tensor_tensor(lo, y, hi.bitcast(F32), ALU.subtract).then_inc(self.h_ready, t.sent("h_ready"))

    def pe_transpose(self, out, in_):
        return self.nc.tensor.transpose(out, in_, self.ident[0:in_.shape[0], 0:in_.shape[0]])

    F_G, F_Y, F_CS, F_DN, F_VH, F_SQ, F_BS, F_WS, F_R = 8192, 9216, 13312, 13568, 14592, 16640, 18688, 19200, 19712

    def f_tile(self, t):
        return self.a(A_OUT + 512 * t, 512)

    def f_consts(self, t):
        io = self.io
        self.load_consts(t, [(self.a(self.F_CS, 256), io["dft_ch"]), (self.a(self.F_DN, 1024), io["dft_tok"]),
                             (self.a(self.F_WS, 512), io["w_s"]),
                             (self.a(self.F_BS, 512), io["b_s"].partition_broadcast(P))])

    def pe_fourier(self, t):
        pe = t.eng
        nc = self.nc
        pe.wait_ge(self.cst_ready, t.due("cst_ready", 4 * 16))
        pe.wait_ge(self.bank_free, t.now("bank_free") + 4)
        cs = self.a(self.F_CS, 256)
        for n in range(4):
            for half in range(2):
                k = 2 * n + half
                if k >= 2:
                    pe.wait_ge(self.yev_ready, t.due("yev_ready"))
                for gg in range(2):
                    g = 2 * half + gg
                    ins = nc.tensor.matmul(self.X[k % 2][:, gg * 256:gg * 256 + 256],
                                           self.a(A_OUT + 512 * g + n * P, P), cs, start=True, stop=True)
                ins.then_inc(self.y_done, t.sent("y_done"))
        pe.wait_ge(self.yev_ready, t.due("yev_ready", 2))
        h0 = self.h_total["in_ab"]
        for k in range(8):
            s, g = k // 4, k % 4
            if k >= 2:
                pe.wait_ge(self.h_ready, t.at("h_ready", h0 + k - 1))
            for tt in range(TT):
                y = self.F_Y + ((2 * s + tt) * 4 + g) * 256
                for part in range(2):
                    ins = nc.tensor.matmul(self.X[2 + k % 2][:, 0:256], self.a(y + part * P, P),
                                           self.a(self.F_DN + (2 * tt + part) * 256, 256),
                                           start=tt == 0 and part == 0, stop=tt == 1 and part == 1)
            ins.then_inc(self.fo_done, t.sent("fo_done"))
        pe.wait_ge(self.sq_ready, t.due("sq_ready", 4))
        for n in range(4):
            for g in range(4):
                ins = nc.tensor.matmul(self.X[0][:, 4 * n + g:4 * n + g + 1],
                                       self.a(self.F_SQ + 512 * g + n * P, P), self.ones[:, 0:1], start=True,
                                       stop=True)
        ins.then_inc(self.stat_ready, t.sent("stat_ready"))
        pe.wait_ge(self.ms_ready, t.at("ms_ready", 3))
        t.add("rstd_ready")
        for n in range(4):
            if n >= 2:
                pe.wait_ge(self.vt_ready, t.due("vt_ready"))
            for g in range(4):
                ins = self.pe_transpose(self.X[n % 2][:, g * P:g * P + P], self.a(A_OUT + 512 * (8 + g) + n * P, P))
            ins.then_inc(self.vt_done, t.sent("vt_done"))
        pe.wait_ge(self.vt_ready, t.due("vt_ready", 2))
        pe.wait_ge(self.h_ready, t.at("h_ready", h0 + 8))
        for g in range(4):
            if g >= 2:
                pe.wait_ge(self.h_ready, t.at("h_ready", h0 + 8 + g - 1))
            for n in range(4):
                ins = nc.tensor.matmul(self.X[2 + g % 2][:, n * P:n * P + P],
                                       self.a(self.F_VH + 512 * n + g * P, P), self.a(self.F_WS + g * P, P),
                                       start=True, stop=True)
            ins.then_inc(self.mix_done, t.sent("mix_done"))

    def act_fourier(self, t):
        act = t.eng
        nc = self.nc
        for k in range(8):
            act.wait_ge(self.y_done, t.due("y_done"))
            nc.scalar.activation(
                self.a(self.F_Y + 512 * k, 512), self.X[k % 2][:], ACT.Copy) \
                .then_inc(self.yev_ready, t.sent("yev_ready"))
        act.wait_ge(self.bank_free, t.at("bank_free", self.evacuated["in_ab"]))

        def tanh(k):
            act.wait_ge(self.gelu_b, t.due("gelu_b"))
            nc.scalar.activation(
                self.a(self.F_G + 512 * (k % 2), 512), self.a(self.F_G + 512 * (k % 2), 512), ACT.Tanh) \
                .then_inc(self.gelu_c, t.sent("gelu_c"))

        for k, tile in enumerate(self.GELU):
            if k >= 2:
                act.wait_ge(self.gelu_d, t.due("gelu_d"))
            nc.scalar.activation(
                self.a(self.F_G + 512 * (k % 2), 512), self.f_tile(tile), ACT.Square) \
                .then_inc(self.gelu_a, t.sent("gelu_a"))
            if k >= 1:
                tanh(k - 1)
            if 2 <= k < 6:
                nc.scalar.activation(
                    self.a(self.F_SQ + 512 * (k - 2), 512), self.f_tile(8 + k - 2), ACT.Square) \
                    .then_inc(self.sq_ready, t.sent("sq_ready"))
        tanh(7)
        act.wait_ge(self.gelu_d, t.due("gelu_d", 2))
        t.add("vt_done", 4)

    GELU = (8, 9, 10, 11, 4, 5, 6, 7)

    def dve_fourier(self, t):
        dve = t.eng
        v = self.nc.vector

        def poly(k):
            s, z = self.a(self.F_G + 512 * (k % 2), 512), self.f_tile(self.GELU[k])
            dve.wait_ge(self.gelu_a, t.due("gelu_a"))
            v.tensor_scalar(
                s, s, 0.044715 * 0.7978845608028654, 0.7978845608028654, ALU.mult, ALU.add) \
                .then_inc(self.dve_seq, t.sent("dve_seq"))
            dve.wait_ge(self.dve_seq, t.now("dve_seq"))
            v.tensor_tensor(s, s, z, ALU.mult).then_inc(self.gelu_b, t.sent("gelu_b"))

        def fin(k):
            s, z = self.a(self.F_G + 512 * (k % 2), 512), self.f_tile(self.GELU[k])
            dve.wait_ge(self.gelu_c, t.due("gelu_c"))
            v.scalar_tensor_tensor(z, s, 1.0, z, ALU.add, ALU.mult).then_inc(self.dve_seq, t.sent("dve_seq"))
            dve.wait_ge(self.dve_seq, t.now("dve_seq"))
            v.tensor_scalar(z, z, 0.5, None, ALU.mult).then_inc(self.gelu_d, t.sent("gelu_d"))

        for k in range(8):
            poly(k)
            if k >= 1:
                fin(k - 1)
            s, g = k // 4, k % 4
            dve.wait_ge(self.fo_done, t.due("fo_done"))
            hi, lo = self.norm_dst(True, s, g)
            self.dve_parts(t, self.X[2 + k % 2][:, 0:256], hi, lo)
        fin(7)
        r = self.a(self.F_R, 16)
        self.dve_stat(t, self.X[0][:, 0:16], r, P)
        dve.wait_ge(self.rstd_ready, t.due("rstd_ready"))
        for n in range(4):
            dve.wait_ge(self.vt_done, t.due("vt_done"))
            v.tensor_tensor(
                self.a(self.F_VH + 512 * n, 512).rearrange("p (g d) -> p g d", g=4),
                self.X[n % 2][:].rearrange("p (g d) -> p g d", g=4),
                self.a(self.F_R + 4 * n, 4).unsqueeze(2).broadcast_to([P, 4, P]), ALU.mult) \
                .then_inc(self.vt_ready, t.sent("vt_ready"))
        dve.wait_ge(self.cst_ready, t.due("cst_ready", 4 * 16))
        dve.wait_ge(self.gelu_d, t.now("gelu_d"))
        for g in range(4):
            dve.wait_ge(self.mix_done, t.due("mix_done"))
            y = self.a(self.F_G + 512 * (g % 2), 512)
            bs = self.a(self.F_BS + g * P, P).unsqueeze(1).broadcast_to([P, 4, P])
            if g >= 2:
                dve.wait_ge(self.h_ready, t.now("h_ready"))
            v.scalar_tensor_tensor(
                y.rearrange("p (n d) -> p n d", n=4), self.X[2 + g % 2][:].rearrange("p (n d) -> p n d", n=4),
                self.vec[:, V_GV + g:V_GV + g + 1], bs, ALU.mult, ALU.add).then_inc(self.dve_seq, t.sent("dve_seq"))
            dve.wait_ge(self.dve_seq, t.now("dve_seq"))
            v.tensor_tensor(y, y, self.f_tile(4 + g), ALU.mult).then_inc(self.dve_seq, t.sent("dve_seq"))
            dve.wait_ge(self.dve_seq, t.now("dve_seq"))
            c = (4 + g) * 1024
            self.dve_parts(t, y, self.h[:, c:c + 512], self.h[:, c + 512:c + 1024])
        dve.wait_ge(self.h_ready, t.now("h_ready"))

    WHERE = {"gqa": dict(q=2048, k=4096, v=10752, vw=256, p=11776, pt=12800, r=16000, sm=16032),
             "moba": dict(q=2048, k=4096, v=12288, vw=1024, p=8192, pt=9216, r=15616, sm=15680),
             "diff": dict(q=2048, k=4096, v=12288, vw=1024, p=8192, pt=9216, r=15616, sm=15680)}
    BIAS = 16384
    O_TILES = 10240

    def s_bank(self, n, a):
        return (self.X[n % 2], self.acc[1 + n % 2])[a]

    def att(self, kind, n):
        i, qt = n // 2, n % 2
        if kind == "gqa":
            return i, qt, 512, 1, [0, P, 2 * P, 3 * P]
        nk = P * (qt + 1)
        return i, qt, nk, 2, [a * 256 + b * P for a in range(2 if kind == "moba" else 1) for b in range(qt + 1)]

    def pe_attention(self, t, kind):
        pe = t.eng
        nc, w = self.nc, self.WHERE[kind]
        evac = "o_evac" if kind == "diff" else "h_ready"
        base = t.count.get(evac, 0)

        def scores(n):
            i, qt, nk, na, _ = self.att(kind, n)
            if n >= 2:
                pe.wait_ge(self.p_ready, t.due("p_ready"))
            for a in range(na):
                p0, p1 = (0, P) if na == 1 else (64 * a, 64 * a + 64)
                kc = w["k"] + (512 * (i // 4) if kind == "gqa" else 256 * i)
                ins = nc.tensor.matmul(self.s_bank(n, a)[:, 0:nk],
                                       self.a(w["q"] + 256 * i + qt * P, P, p0, p1), self.a(kc, nk, p0, p1),
                                       start=True, stop=True)
            ins.then_inc(self.s_done, t.sent("s_done"))

        def turn(n):
            if n >= 1:
                pe.wait_ge(self.pt_ready, t.due("pt_ready"))
            pe.wait_ge(self.pn_ready, t.due("pn_ready"))
            for b, c in enumerate(self.att(kind, n)[4]):
                ins = self.pe_transpose(self.X[2][:, b * P:b * P + P], self.a(w["p"] + 512 * (n % 2) + c, P))
            ins.then_inc(self.t_done, t.sent("t_done"))

        def values(n):
            i, qt, nk, na, blocks = self.att(kind, n)
            if n >= 2:
                pe.wait_ge(self.o_evac if kind == "diff" else self.h_ready, t.at(evac, base + n - 1))
            nb = len(blocks) // (2 if kind == "moba" else 1)
            for a in range(2 if kind == "moba" else 1):
                p0, p1 = (64 * a, 64 * a + 64) if kind == "moba" else (0, P)
                vc = {"gqa": P * (i // 4), "moba": 64 * (2 * i + a), "diff": P * i}[kind]
                for b in range(nb):
                    ins = nc.tensor.matmul((self.X[3], self.acc[0])[n % 2][p0:p1, 0:P],
                                           self.a(w["v"] + w["vw"] * b + vc, p1 - p0),
                                           self.a(w["pt"] + 512 * (n % 2) + (a * nb + b) * P, P),
                                           start=b == 0, stop=b == nb - 1)
            ins.then_inc(self.pv_done, t.sent("pv_done"))

        scores(0)
        scores(1)
        for n in range(16):
            if n < 14:
                scores(n + 2)
            turn(n)
            if n >= 1:
                values(n - 1)
            if kind == "diff" and n % 2 and n >= 5:
                self.pe_sub_sum(t, (n - 5) // 2)
        pe.wait_ge(self.pt_ready, t.due("pt_ready"))
        values(15)
        pe.wait_ge(self.p_ready, t.due("p_ready", 2))
        if kind == "diff":
            t.count[evac] = base + 16

    def act_attention(self, t, kind):
        act = t.eng
        nc, w = self.nc, self.WHERE[kind]

        def exps(n):
            i, qt, nk, na, _ = self.att(kind, n)
            sm = w["sm"] + 8 * (n % 2)
            p = w["p"] + 512 * (n % 2)
            act.wait_ge(self.nm_ready, t.due("nm_ready"))
            for a in range(na):
                dst = self.a(p + 256 * a, nk)
                src, scale = (self.X[n % 2][:], self.a(w["r"] + 8 * qt + i, 1)) if kind == "gqa" else (dst, 1.0)
                ins = nc.scalar.activation(dst, src, ACT.Exp, bias=self.a(sm + a, 1), scale=scale,
                                           accum_out=self.a(sm + 2 + a, 1))
                if a == na - 1:
                    ins.then_inc(self.p_ready, t.sent("p_ready"))
                else:
                    ins.then_inc(self.act_seq, t.sent("act_seq"))

        def copy(n):
            width = P * len(self.att(kind, n)[4])
            act.wait_ge(self.t_done, t.due("t_done"))
            if n >= 2:
                act.wait_ge(self.pv_done, t.due("pv_done"))
            nc.scalar.activation(
                self.a(w["pt"] + 512 * (n % 2), width), self.X[2][:, 0:width], ACT.Copy) \
                .then_inc(self.pt_ready, t.sent("pt_ready"))

        exps(0)
        for n in range(16):
            if n < 15:
                exps(n + 1)
            copy(n)
            if kind == "diff" and n % 2 and n >= 3:
                self.act_sub(t, (n - 3) // 2)
        act.wait_ge(self.pv_done, t.due("pv_done", 2))
        if kind == "diff":
            self.act_sub(t, 7)

    def dve_attention(self, t, kind):
        dve = t.eng
        v, w = self.nc.vector, self.WHERE[kind]

        def front(n):
            i, qt, nk, na, _ = self.att(kind, n)
            sm, p = w["sm"] + 8 * (n % 2), w["p"] + 512 * (n % 2)
            dve.wait_ge(self.s_done, t.due("s_done"))
            if kind == "gqa":
                v.reduce_max(self.a(sm + 4, 1), self.X[n % 2][:], AX).then_inc(self.dve_seq, t.sent("dve_seq"))
                dve.wait_ge(self.dve_seq, t.now("dve_seq"))
                v.scalar_tensor_tensor(
                    self.a(sm, 1), self.a(sm + 4, 1), -1.0, self.a(w["r"] + 8 * qt + i, 1), ALU.mult, ALU.mult) \
                    .then_inc(self.nm_ready, t.sent("nm_ready"))
                return
            if n >= 2:
                dve.wait_ge(self.t_done, t.due("t_done"))
            for a in range(2):
                h = 2 * i + a
                bias = self.a(self.BIAS + (P * h if qt == 0 else 2048 + 256 * h), nk)
                v.scalar_tensor_tensor(
                    self.a(p + 256 * a, nk), self.s_bank(n, a)[:, 0:nk], self.a(w["r"] + 16 * qt + h, 1), bias,
                    ALU.mult, ALU.add).then_inc(self.dve_seq, t.sent("dve_seq"))
            dve.wait_ge(self.dve_seq, t.now("dve_seq"))
            v.reduce_max(
                self.a(sm + 4, 2), self.a(p, 512).rearrange("p (a k) -> p a k", a=2)[:, :, 0:nk], AX) \
                .then_inc(self.dve_seq, t.sent("dve_seq"))
            dve.wait_ge(self.dve_seq, t.now("dve_seq"))
            v.tensor_scalar(
                self.a(sm, 2), self.a(sm + 4, 2), -1.0, None, ALU.mult).then_inc(self.nm_ready, t.sent("nm_ready"))

        def normalise(n):
            i, qt, nk, na, _ = self.att(kind, n)
            sm, p = w["sm"] + 8 * (n % 2), w["p"] + 512 * (n % 2)
            dve.wait_ge(self.p_ready, t.due("p_ready"))
            v.reciprocal(self.a(sm + 6, na), self.a(sm + 2, na)).then_inc(self.dve_seq, t.sent("dve_seq"))
            dve.wait_ge(self.dve_seq, t.now("dve_seq"))
            if kind == "gqa":
                v.tensor_scalar(
                    self.a(p, nk), self.a(p, nk), self.a(sm + 6, 1), None, ALU.mult) \
                    .then_inc(self.pn_ready, t.sent("pn_ready"))
            elif kind == "moba":
                v.tensor_scalar(
                    self.a(p, nk), self.a(p, nk), self.a(sm + 6, 1), None, ALU.mult) \
                    .then_inc(self.dve_seq, t.sent("dve_seq"))
                dve.wait_ge(self.dve_seq, t.now("dve_seq"))
                v.tensor_scalar(
                    self.a(p + 256, nk), self.a(p + 256, nk), self.a(sm + 7, 1), None, ALU.mult) \
                    .then_inc(self.pn_ready, t.sent("pn_ready"))
            else:
                v.tensor_tensor(
                    self.a(sm + 7, 1), self.a(sm + 7, 1), self.a(self.D_NL, 1), ALU.mult) \
                    .then_inc(self.dve_seq, t.sent("dve_seq"))
                v.tensor_scalar(
                    self.a(p, nk), self.a(p, nk), self.a(sm + 6, 1), None, ALU.mult) \
                    .then_inc(self.dve_seq, t.sent("dve_seq"))
                dve.wait_ge(self.dve_seq, t.now("dve_seq"))
                v.scalar_tensor_tensor(
                    self.a(p, nk), self.a(p + 256, nk), self.a(sm + 7, 1), self.a(p, nk), ALU.mult, ALU.add) \
                    .then_inc(self.pn_ready, t.sent("pn_ready"))

        def take(n):
            i, qt = n // 2, n % 2
            dve.wait_ge(self.pv_done, t.due("pv_done"))
            o = (self.X[3], self.acc[0])[n % 2][:, 0:P]
            if kind == "diff":
                v.tensor_copy(self.a(self.O_TILES + 256 * i + P * qt, P), o).then_inc(self.o_evac, t.sent("o_evac"))
                return
            c = 512 * i + P * qt
            self.dve_parts(t, o, self.h[:, c:c + P], self.h[:, c + 256:c + 256 + P])

        front(0)
        for n in range(16):
            if n < 15:
                front(n + 1)
            normalise(n)
            if n >= 2:
                take(n - 2)
        take(14)
        take(15)
        dve.wait_ge(self.t_done, t.due("t_done", 2 if kind != "gqa" else 16))
        dve.wait_ge(self.h_ready, t.now("h_ready"))
        dve.wait_ge(self.pn_ready, t.now("pn_ready"))

    G_SQ, G_QG, G_T, G_COS, G_SIN, G_ROT, G_SEL, G_RT, G_R = 6144, 9216, 9728, 13824, 14080, 14336, 14464, 15488, 16000

    def g_consts(self, t):
        io = self.io
        self.load_consts(t, [(self.a(self.G_COS, 640), io["rope"]), (self.a(self.G_SEL, 1024, 0, 8), io["sel_head"])])

    def pe_gqa(self, t):
        pe = t.eng
        nc = self.nc
        pe.wait_ge(self.cst_ready, t.due("cst_ready", 2 * 16))
        pe.wait_ge(self.bank_free, t.now("bank_free") + 4)
        for n in range(4):
            for j in range(2):
                c = (n % 2) * 256 + j * P
                ins = self.pe_transpose(self.X[1 + n // 2][:, c:c + P], self.a(A_OUT + 3072 + 512 * j + n * P, P))
            if n % 2:
                ins.then_inc(self.vt_done, t.sent("vt_done"))
        pe.wait_ge(self.sq_ready, t.due("sq_ready", 10))
        for tt in range(TT):
            for h in range(8):
                ins = nc.tensor.matmul(self.X[0][:, 8 * tt + h:8 * tt + h + 1],
                                       self.a(self.G_SQ + 256 * h + tt * P, P), self.ones[:, 0:1], start=True,
                                       stop=True)
        for n in range(4):
            for j in range(2):
                ins = nc.tensor.matmul(self.X[0][:, 16 + 2 * n + j:17 + 2 * n + j],
                                       self.a(self.G_SQ + 2048 + 512 * j + n * P, P), self.ones[:, 0:1], start=True,
                                       stop=True)
        ins.then_inc(self.stat_ready, t.sent("stat_ready"))
        pe.wait_ge(self.vt_ready, t.due("vt_ready", 2))
        pe.wait_ge(self.ms_ready, t.at("ms_ready", 7))
        for k in range(10):
            pe.wait_ge(self.qg_ready, t.due("qg_ready"))
            if k >= 2:
                pe.wait_ge(self.rope_ready, t.due("rope_ready"))
            ins = nc.tensor.matmul(self.X[k % 2][:, 0:256], self.a(self.G_ROT, P),
                                   self.a(self.G_QG + 256 * (k % 2), 256), start=True, stop=True)
            ins.then_inc(self.rot_done, t.sent("rot_done"))
        pe.wait_ge(self.rstd_ready, t.due("rstd_ready"))
        for n in range(4):
            ins = self.pe_transpose(self.X[3][0:2, n * P:n * P + P], self.a(self.G_R + 16 + 2 * n, 2))
        ins.then_inc(self.rt_done, t.sent("rt_done"))
        pe.wait_ge(self.rt_ready, t.due("rt_ready"))
        for j in range(2):
            ins = nc.tensor.matmul(self.X[2 + j][:], self.a(self.G_SEL + j * P, P, 0, 2), self.a(self.G_RT, 512, 0, 2),
                                   start=True, stop=True)
            ins.then_inc(self.hb_done, t.sent("hb_done"))
        pe.wait_ge(self.rope_ready, t.due("rope_ready", 2))
        pe.wait_ge(self.rk_ready, t.due("rk_ready", 2))

    def g_src(self, k):
        return self.a(A_OUT + 256 * k, 256) if k < 8 else self.a(A_OUT + 2048 + 512 * (k - 8), 256)

    def act_gqa(self, t):
        act = t.eng
        nc = self.nc
        act.wait_ge(self.bank_free, t.at("bank_free", self.evacuated["kv"]))
        for h in range(8):
            nc.scalar.activation(
                self.a(self.G_SQ + 256 * h, 256), self.g_src(h), ACT.Square) \
                .then_inc(self.sq_ready, t.sent("sq_ready"))
        for j in range(2):
            nc.scalar.activation(
                self.a(self.G_SQ + 2048 + 512 * j, 512), self.a(A_OUT + 2048 + 512 * j, 512), ACT.Square) \
                .then_inc(self.sq_ready, t.sent("sq_ready"))
        act.wait_ge(self.sq_ready, t.now("sq_ready"))
        for b in range(2):
            act.wait_ge(self.vt_done, t.due("vt_done"))
            nc.scalar.activation(
                self.a(self.WHERE["gqa"]["v"] + 512 * b, 512), self.X[1 + b][:], ACT.Copy) \
                .then_inc(self.vt_ready, t.sent("vt_ready"))
        for j in range(2):
            kc = self.a(A_OUT + 2048 + 512 * j + 256, 256)
            nc.scalar.activation(
                kc, kc, ACT.Copy, scale=self.vec[:, V_GK:V_GK + 1]).then_inc(self.act_seq, t.sent("act_seq"))
            act.wait_ge(self.act_seq, t.now("act_seq"))
        for k in range(10):
            if k >= 2:
                act.wait_ge(self.rope_ready, t.due("rope_ready"))
            gain = V_GQ if k < 8 else V_GK
            nc.scalar.activation(
                self.a(self.G_QG + 256 * (k % 2), 256), self.g_src(k), ACT.Copy, scale=self.vec[:, gain:gain + 1]) \
                .then_inc(self.qg_ready, t.sent("qg_ready"))
        act.wait_ge(self.rope_ready, t.due("rope_ready", 2))

    def dve_gqa(self, t):
        dve = t.eng
        v = self.nc.vector
        self.dve_stat(t, self.X[0][:, 0:24], self.a(self.G_R, 24), P)
        dve.wait_ge(self.cst_ready, t.due("cst_ready", 2 * 16))
        for k in range(10):
            dve.wait_ge(self.rot_done, t.due("rot_done"))
            c = self.a(self.G_T + 256 * (k % 2), 256)
            dst = self.g_src(k)
            v.tensor_tensor(
                c, self.a(self.G_QG + 256 * (k % 2), 256), self.a(self.G_COS, 256), ALU.mult) \
                .then_inc(self.dve_seq, t.sent("dve_seq"))
            v.tensor_tensor(
                dst, self.X[k % 2][:, 0:256], self.a(self.G_SIN, 256), ALU.mult) \
                .then_inc(self.dve_seq, t.sent("dve_seq"))
            dve.wait_ge(self.dve_seq, t.now("dve_seq"))
            v.tensor_tensor(dst, dst, c, ALU.add).then_inc(self.rope_ready, t.sent("rope_ready"))
            dve.wait_ge(self.rope_ready, t.now("rope_ready"))
        t.add("vt_done", 2)
        dve.wait_ge(self.rstd_ready, t.due("rstd_ready"))
        dve.wait_ge(self.rt_done, t.due("rt_done"))
        v.tensor_copy(self.a(self.G_RT, 512, 0, 2), self.X[3][0:2, :]).then_inc(self.rt_ready, t.sent("rt_ready"))
        v.tensor_scalar(
            self.a(self.G_R, 16), self.a(self.G_R, 16), P ** -0.5, None, ALU.mult) \
            .then_inc(self.dve_seq, t.sent("dve_seq"))
        dve.wait_ge(self.dve_seq, t.now("dve_seq"))
        for j in range(2):
            dve.wait_ge(self.hb_done, t.due("hb_done"))
            k = self.a(A_OUT + 2048 + 512 * j, 512)
            v.tensor_tensor(k, k, self.X[2 + j][:], ALU.mult).then_inc(self.rk_ready, t.sent("rk_ready"))
        dve.wait_ge(self.rk_ready, t.now("rk_ready"))

    M_SQ, M_SEL, M_RT, M_R, M_SM, D_LAM, D_NL, M_GC, M_HALF, D_SEL = (
        8192, 14336, 15360, 15616, 15680, 15704, 15700, 15698, 15696, 0)

    def m_consts(self, t, kind):
        io = self.io
        parts = [(self.a(self.M_SEL, 1024, 0, 16), io["sel_pair"]), (self.a(self.M_HALF, 2), io["halves"])]
        if kind == "moba":
            for qt in range(TT):
                nk = P * (qt + 1)
                row = 2 * SEQ - 1
                window = bass.AP(self.dist_bias, SEQ - 1 - P * qt, [[16 * row - 1, P], [row, 16], [1, nk]])
                dst = self.a(self.BIAS + (0 if qt == 0 else 16 * P), 16 * nk).rearrange("p (h j) -> p h j", h=16)
                parts.append((dst, window))
        else:
            parts += [(self.a(self.D_LAM, 256), io["diff_lambda"].partition_broadcast(P)),
                      (self.a(self.D_SEL, 1024, 0, 8), io["sel_head"])]
        self.load_consts(t, parts)

    def pe_heads(self, t, kind):
        pe = t.eng
        nc = self.nc
        pe.wait_ge(self.cst_ready, t.due("cst_ready", 4 * 16))
        pe.wait_ge(self.bank_free, t.now("bank_free") + 4)

        def turned(b):
            for c in range(4):
                tile, tt = 4 * (b % 2) + c, b // 2
                ins = self.pe_transpose(self.X[1 + b % 2][:, c * P:c * P + P],
                                        self.a(A_OUT + 4096 + 256 * tile + tt * P, P))
            ins.then_inc(self.vt_done, t.sent("vt_done"))

        def stats(first, bank):
            pe.wait_ge(self.sq_ready, t.due("sq_ready", 8))
            for tt in range(TT):
                for c in range(8):
                    ins = nc.tensor.matmul(bank[:, 16 * tt + 2 * c:16 * tt + 2 * c + 2],
                                           self.a(self.M_SQ + 256 * (first + c) + tt * P, P),
                                           self.a(self.M_HALF, 2), start=True, stop=True)
            ins.then_inc(self.stat_ready, t.sent("stat_ready"))

        turned(0)
        turned(1)
        stats(8, self.X[0])
        for b in (2, 3):
            pe.wait_ge(self.vt_ready, t.due("vt_ready"))
            turned(b)
        stats(0, self.acc[0])
        pe.wait_ge(self.vt_ready, t.due("vt_ready", 2))
        pe.wait_ge(self.rstd_ready, t.due("rstd_ready"))
        t.add("rstd_ready")
        for tt in range(TT):
            ins = self.pe_transpose(self.X[3][0:16, tt * P:tt * P + P], self.a(self.M_R + 32 + 16 * tt, 16))
        ins.then_inc(self.rt_done, t.sent("rt_done"))
        pe.wait_ge(self.rt_ready, t.due("rt_ready"))
        for k in range(8):
            if k >= 2:
                pe.wait_ge(self.rk_ready, t.due("rk_ready"))
            ins = nc.tensor.matmul(self.X[k % 2][:, 0:256], self.a(self.M_SEL + k * P, P, 0, 16),
                                   self.a(self.M_RT, 256, 0, 16), start=True, stop=True)
            ins.then_inc(self.hb_done, t.sent("hb_done"))
        pe.wait_ge(self.rk_ready, t.due("rk_ready", 2))

    def act_heads(self, t, kind):
        act = t.eng
        nc = self.nc
        act.wait_ge(self.bank_free, t.at("bank_free", self.evacuated[kind + "_in"]))
        for half in range(2):
            for c in range(8 - 8 * half, 16 - 8 * half):
                nc.scalar.activation(
                    self.a(self.M_SQ + 256 * c, 256), self.a(A_OUT + 256 * c, 256), ACT.Square) \
                    .then_inc(self.sq_ready, t.sent("sq_ready"))
            for b in (2 * half, 2 * half + 1):
                act.wait_ge(self.vt_done, t.due("vt_done"))
                nc.scalar.activation(
                    self.a(self.WHERE[kind]["v"] + 1024 * (b // 2) + 512 * (b % 2), 512), self.X[1 + b % 2][:],
                    ACT.Copy).then_inc(self.vt_ready, t.sent("vt_ready"))
        if kind == "diff":
            act.wait_ge(self.lam_a, t.due("lam_a"))
            nc.scalar.activation(
                self.a(self.D_NL, 2), self.a(self.D_NL, 2), ACT.Exp).then_inc(self.lam_ready, t.sent("lam_ready"))

    def dve_heads(self, t, kind):
        dve = t.eng
        v = self.nc.vector
        gq, gk = (V_MQ, V_MK) if kind == "moba" else (V_DQ, V_DK)
        gc = self.a(self.M_GC, 1)
        t.add("vt_done", 4)
        v.scalar_tensor_tensor(
            gc, self.vec[:, gq:gq + 1], 64.0 ** -0.5, self.vec[:, gk:gk + 1], ALU.mult, ALU.mult) \
            .then_inc(self.dve_seq, t.sent("dve_seq"))
        dve.wait_ge(self.dve_seq, t.now("dve_seq"))
        if kind == "diff":
            dve.wait_ge(self.cst_ready, t.due("cst_ready", 8 * 16))
            lam = self.a(self.D_LAM, 256).rearrange("p (a b d) -> p a b d", a=2, b=2)
            v.tensor_tensor(
                lam[:, :, 0, :], lam[:, :, 0, :], lam[:, :, 1, :], ALU.mult).then_inc(self.dve_seq, t.sent("dve_seq"))
            dve.wait_ge(self.dve_seq, t.now("dve_seq"))
            v.reduce_sum(self.a(self.D_NL, 2), lam[:, :, 0, :], AX).then_inc(self.lam_a, t.sent("lam_a"))
            dve.wait_ge(self.lam_ready, t.due("lam_ready"))
            nl = self.a(self.D_NL, 1)
            v.scalar_tensor_tensor(
                nl, nl, -1.0, self.a(self.D_NL + 1, 1), ALU.mult, ALU.add).then_inc(self.dve_seq, t.sent("dve_seq"))
            dve.wait_ge(self.dve_seq, t.now("dve_seq"))
            v.tensor_scalar(nl, nl, LAMBDA_INIT, None, ALU.subtract).then_inc(self.dve_seq, t.sent("dve_seq"))
            dve.wait_ge(self.dve_seq, t.now("dve_seq"))
        self.dve_stat(t, self.X[0][:, 0:32], self.a(self.M_R + 32, 32), 64)
        self.dve_stat(t, self.acc[0][:, 0:32], self.a(self.M_R, 32), 64)
        dve.wait_ge(self.rstd_ready, t.due("rstd_ready"))
        dve.wait_ge(self.rt_done, t.due("rt_done"))
        v.tensor_copy(
            self.a(self.M_RT, 256, 0, 16), self.X[3][0:16, 0:256]).then_inc(self.rt_ready, t.sent("rt_ready"))
        for c in range(8):
            dve.wait_ge(self.hb_done, t.due("hb_done"))
            k = self.a(A_OUT + 2048 + 256 * c, 256)
            v.scalar_tensor_tensor(
                k, k, gc, self.X[c % 2][:, 0:256], ALU.mult, ALU.mult).then_inc(self.rk_ready, t.sent("rk_ready"))
        dve.wait_ge(self.rstd_ready, t.due("rstd_ready"))
        dve.wait_ge(self.rk_ready, t.now("rk_ready"))

    def act_sub(self, t, c):
        act = t.eng
        act.wait_ge(self.o_evac, t.due("o_evac", 2))
        self.nc.scalar.activation(
            self.a(A_OUT + 256 * c, 256), self.a(self.O_TILES + 256 * c, 256), ACT.Square) \
            .then_inc(self.sq_ready, t.sent("sq_ready"))

    def pe_sub_sum(self, t, c):
        pe = t.eng
        pe.wait_ge(self.sq_ready, t.due("sq_ready"))
        for tt in range(TT):
            ins = self.nc.tensor.matmul(self.acc[3][:, 8 * tt + c:8 * tt + c + 1],
                                        self.a(A_OUT + 256 * c + tt * P, P), self.ones[:, 0:1], start=True,
                                        stop=True)
        return ins

    def pe_sub(self, t):
        pe = t.eng
        nc = self.nc
        self.pe_sub_sum(t, 6)
        self.pe_sub_sum(t, 7).then_inc(self.stat_ready, t.sent("stat_ready"))
        pe.wait_ge(self.rstd_ready, t.due("rstd_ready"))
        for tt in range(TT):
            ins = self.pe_transpose(self.X[3][0:8, tt * P:tt * P + P], self.a(self.M_R + 8 * tt, 8))
        ins.then_inc(self.rt_done, t.sent("rt_done"))
        pe.wait_ge(self.rt_ready, t.due("rt_ready"))
        h0 = self.h_total["diff_in"]
        for k in range(8):
            if k >= 2:
                pe.wait_ge(self.h_ready, t.at("h_ready", h0 + k - 1))
            ins = nc.tensor.matmul(self.X[k % 2][:, 0:256], self.a(self.D_SEL + k * P, P, 0, 8),
                                   self.a(self.M_RT, 256, 0, 8), start=True, stop=True)
            ins.then_inc(self.hb_done, t.sent("hb_done"))

    def dve_sub(self, t):
        dve = t.eng
        v = self.nc.vector
        gc = self.a(self.M_GC, 1)
        v.tensor_scalar(
            gc, self.vec[:, V_SUB:V_SUB + 1], 1.0 - LAMBDA_INIT, None, ALU.mult) \
            .then_inc(self.dve_seq, t.sent("dve_seq"))
        dve.wait_ge(self.dve_seq, t.now("dve_seq"))
        self.dve_stat(t, self.acc[3][:, 0:16], self.a(self.M_R, 16), P)
        dve.wait_ge(self.rstd_ready, t.due("rstd_ready"))
        dve.wait_ge(self.rt_done, t.due("rt_done"))
        v.tensor_copy(self.a(self.M_RT, 256, 0, 8), self.X[3][0:8, 0:256]).then_inc(self.rt_ready, t.sent("rt_ready"))
        dve.wait_ge(self.o_evac, t.now("o_evac"))
        for c in range(8):
            dve.wait_ge(self.hb_done, t.due("hb_done"))
            o = self.a(self.O_TILES + 256 * c, 256)
            v.scalar_tensor_tensor(
                o, o, gc, self.X[c % 2][:, 0:256], ALU.mult, ALU.mult).then_inc(self.dve_seq, t.sent("dve_seq"))
            dve.wait_ge(self.dve_seq, t.now("dve_seq"))
            hi, lo = self.norm_dst(False, 0, c)
            self.dve_parts(t, o, hi, lo)
        dve.wait_ge(self.h_ready, t.now("h_ready"))

    R_COS, R_DEC, R_V, R_TP, R_ST, R_SQ, R_SEL, R_RT, R_R = (
        0, 512, 14336, 20480, 6144, 6912, 7936, 8960, 9216)
    R_O = 18432

    def r_consts(self, t):
        io = self.io
        self.load_consts(t, [(self.a(self.R_COS, 512), io["rotary"]), (self.a(self.R_DEC, 1536), io["decay"])])

    def pool_rotary(self, t, base, tmp):
        pool, g = t.eng, self.nc.gpsimd
        x = self.a(base, 2048).rearrange("p (h s n) -> p h s n", h=4, s=2)
        x1, x2 = x[:, :, 0, :], x[:, :, 1, :]
        ta, tb = (self.a(tmp + 1024 * k, 1024).rearrange("p (h n) -> p h n", h=4) for k in range(2))
        cos, sin = (self.a(self.R_COS + 256 * k, 256).unsqueeze(1).broadcast_to([P, 4, 256]) for k in range(2))
        g.tensor_tensor(ta, x1, sin, ALU.mult).then_inc(self.pool_seq, t.sent("pool_seq"))
        g.tensor_tensor(tb, x2, sin, ALU.mult).then_inc(self.pool_seq, t.sent("pool_seq"))
        pool.wait_ge(self.pool_seq, t.now("pool_seq"))
        g.tensor_tensor(x1, x1, cos, ALU.mult).then_inc(self.pool_seq, t.sent("pool_seq"))
        g.tensor_tensor(x2, x2, cos, ALU.mult).then_inc(self.pool_seq, t.sent("pool_seq"))
        pool.wait_ge(self.pool_seq, t.now("pool_seq"))
        g.tensor_tensor(x1, x1, tb, ALU.subtract).then_inc(self.pool_seq, t.sent("pool_seq"))
        pool.wait_ge(self.pool_seq, t.now("pool_seq"))
        g.tensor_tensor(x2, x2, ta, ALU.add).then_inc(self.kr_ready, t.sent("kr_ready"))
        pool.wait_ge(self.kr_ready, t.now("kr_ready"))

    def pe_retention(self, t, j):
        pe = t.eng
        nc = self.nc
        pe.wait_ge(self.cst_ready, t.due("cst_ready", 2 * 16))
        pe.wait_ge(self.bank_free, t.now("bank_free") + 4)
        for b in range(8):
            if b >= 2:
                pe.wait_ge(self.vt_ready, t.due("vt_ready"))
            for c in range(4):
                tile, tt = 4 * (b % 4) + c, b // 4
                ins = self.pe_transpose(self.X[1 + b % 2][:, c * P:c * P + P],
                                        self.a(A_OUT + 4096 + 256 * tile + tt * P, P))
            ins.then_inc(self.vt_done, t.sent("vt_done"))
        pe.wait_ge(self.vt_ready, t.due("vt_ready", 2))
        pe.wait_ge(self.kr_ready, t.due("kr_ready", 2))
        q, k = A_OUT, A_OUT + 2048

        def scores(h):
            bank = self.acc[1 + h % 2]
            for jt, n in ((0, 256), (1, P)):
                for c in range(2):
                    tile = 256 * (2 * h + c)
                    ins = nc.tensor.matmul(bank[:, jt * 256:jt * 256 + n], self.a(k + tile + jt * P, P),
                                           self.a(q + tile + jt * P, n), start=c == 0, stop=c == 1)
            ins.then_inc(self.st_done, t.sent("st_done"))

        def values(h):
            pe.wait_ge(self.st_ready, t.due("st_ready"))
            if h >= 1:
                pe.wait_ge(self.o_evac, t.due("o_evac"))
            for c in range(4):
                o = self.X[1 + c // 2]
                at = (c % 2) * 256
                v = self.R_V + 512 * h + P * c
                st = self.R_ST + 384 * (h % 2)
                nc.tensor.matmul(o[:, at:at + P], self.a(v, P), self.a(st, P), start=True, stop=True)
                nc.tensor.matmul(o[:, at + P:at + 256], self.a(v, P), self.a(st + P, P), start=True, stop=False)
                ins = nc.tensor.matmul(o[:, at + P:at + 256], self.a(v + 2048, P), self.a(st + 256, P), start=False,
                                       stop=True)
            ins.then_inc(self.od_done, t.sent("od_done"))

        def stats(h):
            pe.wait_ge(self.sq_ready, t.due("sq_ready"))
            if h == 3:
                pe.wait_ge(self.o_evac, t.due("o_evac"))
            for tt in range(TT):
                for c in range(4):
                    ins = nc.tensor.matmul(self.acc[0][:, 4 * tt + h:4 * tt + h + 1],
                                           self.a(self.R_SQ + 256 * c + tt * P, P), self.ones[:, 0:1],
                                           start=c == 0, stop=c == 3)
            ins.then_inc(self.ost_ready, t.sent("ost_ready"))

        scores(0)
        scores(1)
        for h in range(4):
            values(h)
            if h >= 1:
                stats(h - 1)
            if h + 2 < 4:
                scores(h + 2)
        stats(3)
        pe.wait_ge(self.rstd_ready, t.due("rstd_ready"))
        for tt in range(TT):
            ins = self.pe_transpose(self.X[3][0:4, tt * P:tt * P + P], self.a(self.R_R + 4 * tt, 4))
        ins.then_inc(self.rt_done, t.sent("rt_done"))
        pe.wait_ge(self.rt_ready, t.due("rt_ready"))
        pe.wait_ge(self.cst_ready, t.due("cst_ready", 16))
        for h in range(4):
            ins = nc.tensor.matmul(self.X[h][:, 0:256],
                                   self.a(self.R_SEL + h * P, P, 0, 4), self.a(self.R_RT, 256, 0, 4), start=True,
                                   stop=True)
            ins.then_inc(self.hb_done, t.sent("hb_done"))

    def act_retention(self, t, j):
        act = t.eng
        nc = self.nc
        act.wait_ge(self.bank_free, t.at("bank_free", self.evacuated[f"ret_in{j}"]))
        for b in range(8):
            act.wait_ge(self.vt_done, t.due("vt_done"))
            nc.scalar.activation(
                self.a(self.R_V + 2048 * (b // 4) + 512 * (b % 4), 512), self.X[1 + b % 2][:], ACT.Copy) \
                .then_inc(self.vt_ready, t.sent("vt_ready"))
            if b % 2:
                k = b // 2
                if k:
                    act.wait_ge(self.silu_a, t.due("silu_a"))
                nc.scalar.activation(
                    self.tmp[:], self.a(A_OUT + 8192 + 1024 * k, 1024), ACT.Tanh, scale=0.5) \
                    .then_inc(self.th_ready, t.sent("th_ready"))
        act.wait_ge(self.silu_a, t.due("silu_a"))
        self.load_consts(t, [(self.a(self.R_SEL, 1024, 0, 8), self.io["sel_head"])])
        for h in range(4):
            act.wait_ge(self.o_evac, t.due("o_evac"))
            if h:
                act.wait_ge(self.ost_ready, t.due("ost_ready"))
            nc.scalar.activation(
                self.a(self.R_SQ, 1024), self.a(self.R_O + 1024 * h, 1024), ACT.Square) \
                .then_inc(self.sq_ready, t.sent("sq_ready"))
        act.wait_ge(self.ost_ready, t.due("ost_ready"))

    def pool_retention(self, t, j):
        pool = t.eng
        g = self.nc.gpsimd
        pool.wait_ge(self.cst_ready, t.due("cst_ready", 2 * 16))
        for part in range(2):
            pool.wait_ge(self.bank_free, t.at("bank_free", self.evacuated[f"ret_in{j}"] - 40 + 8 * part))
            self.pool_rotary(t, A_OUT + 2048 * part, self.R_TP)
        t.add("cst_ready", 16)
        for h in range(4):
            pool.wait_ge(self.ost_ready, t.due("ost_ready"))
            o = self.a(self.R_O + 1024 * h, 1024)
            g.tensor_tensor(
                o, o, self.a(A_OUT + 8192 + 1024 * h, 1024), ALU.mult).then_inc(self.og_ready, t.sent("og_ready"))
        self.pool_stat(t, self.a(self.R_R, 8), 8)

    def dve_retention(self, t, j):
        dve = t.eng
        v = self.nc.vector
        dve.wait_ge(self.cst_ready, t.due("cst_ready", 2 * 16))
        for k in range(4):
            dve.wait_ge(self.th_ready, t.due("th_ready"))
            g = self.a(A_OUT + 8192 + 1024 * k, 1024)
            v.scalar_tensor_tensor(g, self.tmp[:], 1.0, g, ALU.add, ALU.mult).then_inc(self.silu_a, t.sent("silu_a"))
        dve.wait_ge(self.silu_a, t.now("silu_a"))
        dve.wait_ge(self.vt_done, t.due("vt_done", 8))
        dve.wait_ge(self.kr_ready, t.due("kr_ready", 2))

        def decay(h):
            dve.wait_ge(self.st_done, t.due("st_done"))
            v.tensor_tensor(
                self.a(self.R_ST + 384 * (h % 2), 384), self.acc[1 + h % 2][:, 0:384],
                self.a(self.R_DEC + 384 * h, 384), ALU.mult).then_inc(self.st_ready, t.sent("st_ready"))

        def take(h):
            dve.wait_ge(self.od_done, t.due("od_done"))
            v.tensor_copy(self.a(self.R_O + 1024 * h, 512), self.X[1][:]).then_inc(self.dve_seq, t.sent("dve_seq"))
            dve.wait_ge(self.dve_seq, t.now("dve_seq"))
            v.tensor_copy(
                self.a(self.R_O + 1024 * h + 512, 512), self.X[2][:]).then_inc(self.o_evac, t.sent("o_evac"))

        decay(0)
        decay(1)
        for h in range(4):
            take(h)
            if h + 2 < 4:
                decay(h + 2)
        self.dve_stat(t, self.acc[0][:, 0:8], self.a(self.R_R, 8), 512, "ost_ready", 4)
        dve.wait_ge(self.rstd_ready, t.due("rstd_ready"))
        dve.wait_ge(self.rt_done, t.due("rt_done"))
        v.tensor_scalar(
            self.a(self.R_RT, 256, 0, 4), self.X[3][0:4, 0:256], 0.5, None, ALU.mult) \
            .then_inc(self.rt_ready, t.sent("rt_ready"))
        t.add("cst_ready", 16)
        for h in range(4):
            dve.wait_ge(self.hb_done, t.due("hb_done"))
            dve.wait_ge(self.og_ready, t.due("og_ready"))
            o = self.a(self.R_O + 1024 * h, 1024).rearrange("p (c n) -> p c n", c=4)
            bc = self.X[h][:, 0:256].unsqueeze(1).broadcast_to([P, 4, 256])
            v.tensor_tensor(o, o, bc, ALU.mult).then_inc(self.dve_seq, t.sent("dve_seq"))
            dve.wait_ge(self.dve_seq, t.now("dve_seq"))
            parts = self.h[:, 2048 * h:2048 * h + 2048].rearrange("p (c s n) -> p c s n", c=4, s=2)
            hi, lo = parts[:, :, 0, :], parts[:, :, 1, :]
            v.tensor_copy(hi, o).then_inc(self.dve_seq, t.sent("dve_seq"))
            dve.wait_ge(self.dve_seq, t.now("dve_seq"))
            v.tensor_tensor(lo, o, hi.bitcast(F32), ALU.subtract).then_inc(self.h_ready, t.sent("h_ready", 4))
        dve.wait_ge(self.h_ready, t.now("h_ready"))

    def tensor_program(self, pe):
        t = Track(pe)
        self.pe_start(t)
        self.pe_mod(t)
        for l in range(2):
            for m, name in ((0, "1"), (3, "mix"), (6, "2")):
                wide = not (l == 1 and m == 6)
                self.pe_norm(t, ("mod", l, m), wide)
                if name != "mix":
                    self.pe_gemm(t, f"gu{name}_{l}")
                    self.pe_gemm(t, f"down{name}_{l}")
                elif l == 0:
                    self.pe_gemm(t, "in_ab")
                    self.pe_fourier(t)
                    self.pe_gemm(t, "out_ab")
                else:
                    self.pe_gemm(t, "q")
                    self.pe_gemm(t, "kv")
                    self.pe_gqa(t)
                    self.pe_attention(t, "gqa")
                    self.pe_gemm(t, "o")
        self.pe_norm(t, ("final", V_FINAL), False)
        for i in range(4):
            self.pe_norm(t, ("gain", V_N1 + 8 * i), False)
            if i % 3 == 0:
                self.pe_gemm(t, f"ret_in{i // 3}")
                self.pe_retention(t, i // 3)
                self.pe_gemm(t, f"ret_out{i // 3}")
            else:
                kind = ("moba", "diff")[i - 1]
                self.pe_gemm(t, kind + "_in")
                self.pe_heads(t, kind)
                self.pe_attention(t, kind)
                if kind == "diff":
                    self.pe_sub(t)
                self.pe_gemm(t, kind + "_out")
            self.pe_norm(t, ("gain", V_N2 + 8 * i), False)
            self.pe_gemm(t, f"up{i}")
            self.pe_gemm(t, f"down{i}")

    def scalar_program(self, act):
        t = Track(act)
        self.act_start(t)
        act.wait_ge(self.csil_ready, t.due("csil_ready"))
        for kt in range(KT):
            self.act_square(t, kt, True)
        self.act_gemm(t, "mod0")
        for l in range(2):
            for m, name in ((0, "1"), (3, "mix"), (6, "2")):
                wide = not (l == 1 and m == 6)
                self.act_norm(t, ("mod", l, m), wide)
                if name != "mix":
                    self.act_gemm(t, f"gu{name}_{l}")
                    self.act_gemm(t, f"down{name}_{l}")
                elif l == 0:
                    self.f_consts(t)
                    self.act_gemm(t, "in_ab")
                    self.act_fourier(t)
                    self.act_gemm(t, "out_ab")
                else:
                    self.g_consts(t)
                    self.act_gemm(t, "q")
                    self.act_gemm(t, "kv")
                    self.act_gqa(t)
                    self.act_attention(t, "gqa")
                    self.act_gemm(t, "o")
        self.act_norm(t, ("final", V_FINAL), False)
        for i in range(4):
            self.act_norm(t, ("gain", V_N1 + 8 * i), False)
            if i % 3 == 0:
                self.r_consts(t)
                self.act_gemm(t, f"ret_in{i // 3}")
                self.act_retention(t, i // 3)
                self.act_gemm(t, f"ret_out{i // 3}")
            else:
                kind = ("moba", "diff")[i - 1]
                self.m_consts(t, kind)
                self.act_gemm(t, kind + "_in")
                self.act_heads(t, kind)
                self.act_attention(t, kind)
                self.act_gemm(t, kind + "_out")
            self.act_norm(t, ("gain", V_N2 + 8 * i), False)
            self.act_gemm(t, f"up{i}")
            self.act_gemm(t, f"down{i}")

    def vector_program(self, dve):
        t = Track(dve)
        self.dve_start(t)
        self.dve_gemm(t, "mod0")
        self.dve_mod_bias(t, 0, 0, 72)
        self.dve_mod(t, 0)
        for l in range(2):
            for m, name in ((0, "1"), (3, "mix"), (6, "2")):
                wide = not (l == 1 and m == 6)
                self.dve_norm(t, ("mod", l, m), wide)
                if name != "mix":
                    self.dve_gemm(t, f"gu{name}_{l}")
                    if l == 0:
                        self.dve_mod_bias(t, 1, 0 if m == 0 else 40, 40 if m == 0 else 32)
                    if (l, m) == (0, 6):
                        self.dve_mod(t, 1)
                    self.dve_gemm(t, f"down{name}_{l}")
                elif l == 0:
                    self.dve_gemm(t, "in_ab")
                    self.dve_fourier(t)
                    self.dve_gemm(t, "out_ab")
                else:
                    self.dve_gemm(t, "q")
                    self.dve_gemm(t, "kv")
                    self.dve_gqa(t)
                    self.dve_attention(t, "gqa")
                    self.dve_gemm(t, "o")
        self.dve_norm(t, ("final", V_FINAL), False)
        for i in range(4):
            self.dve_norm(t, ("gain", V_N1 + 8 * i), False)
            if i % 3 == 0:
                self.dve_gemm(t, f"ret_in{i // 3}")
                self.dve_retention(t, i // 3)
                self.dve_gemm(t, f"ret_out{i // 3}")
            else:
                kind = ("moba", "diff")[i - 1]
                self.dve_gemm(t, kind + "_in")
                self.dve_heads(t, kind)
                self.dve_attention(t, kind)
                if kind == "diff":
                    self.dve_sub(t)
                self.dve_gemm(t, kind + "_out")
            self.dve_norm(t, ("gain", V_N2 + 8 * i), False)
            self.dve_gemm(t, f"up{i}")
            self.dve_gemm(t, f"down{i}")

    def pool_program(self, pool):
        t = Track(pool)
        self.pool_start(t)
        for l in range(2):
            for m in (0, 3, 6):
                self.pool_norm(t, ("mod", l, m), not (l == 1 and m == 6))
                if m == 3:
                    self.pool_stat(t, self.a(self.F_R, 16) if l == 0 else self.a(self.G_R, 24), 16 if l == 0 else 24)
        self.pool_gemm(t, "gu2_1")
        t.add("cst_ready", 6 * 16)
        self.pool_norm(t, ("final", V_FINAL), False)
        for i in range(4):
            self.pool_norm(t, ("gain", V_N1 + 8 * i), False)
            if i % 3 == 0:
                self.pool_retention(t, i // 3)
            else:
                self.pool_stat(t, self.a(self.M_R + 32, 32), 32)
                self.pool_stat(t, self.a(self.M_R, 32), 32)
                if i == 2:
                    self.pool_stat(t, self.a(self.M_R, 16), 16)
                t.add("cst_ready", 4 * 16)
            self.pool_norm(t, ("gain", V_N2 + 8 * i), False)
            self.pool_gemm(t, f"up{i}")


def build(nc, io):
    prog = Program(nc, io)
    with ExitStack() as ctx:
        prog.allocate(ctx)
        block = ctx.enter_context(nc.Block())

        @block.sync
        def _(sp):
            prog.sync_program(sp)

        @block.gpsimd
        def _(pool):
            prog.pool_program(pool)

        @block.scalar
        def _(act):
            prog.scalar_program(act)

        @block.vector
        def _(dve):
            prog.vector_program(dve)

        @block.tensor
        def _(pe):
            prog.tensor_program(pe)


def _units(np, w, order=None, kpad=None, nb=16):
    k, m = w.shape
    if kpad:
        full = np.zeros((kpad, m), w.dtype)
        full[:k] = w
        w, k = full, kpad
    b = w.reshape(k // 128, 128, m // 128, 128).transpose(2, 0, 1, 3)
    if order is not None:
        b = b[order]
    b = b.reshape(-1, nb, 128, 128).transpose(0, 2, 1, 3)
    return np.ascontiguousarray(b.reshape(b.shape[0], 128, nb * 128))


def _gate_up(np, w):
    ff = w.shape[1] // 2
    full = np.zeros((w.shape[0], 2 * FF_T * 128), w.dtype)
    full[:, :ff] = w[:, :ff]
    full[:, FF_T * 128:FF_T * 128 + ff] = w[:, ff:]
    order = [t + s * FF_T for t in range(FF_T) for s in range(2)]
    return _units(np, full, order=order)


def _col(np, v):
    return v.reshape(-1, 128).T


def _tables(np):
    f = np.float32
    n, c = np.arange(SEQ), np.arange(128)
    scale = 1.0 / np.sqrt(SEQ * 128.0)
    ch = 2 * np.pi * np.outer(c, c) / 128
    tok = 2 * np.pi * np.outer(n, n) / SEQ
    dft_ch = np.concatenate([np.cos(ch), np.sin(ch)], 1) * scale
    dft_tok = np.concatenate([x[tt * 128:tt * 128 + 128] for tt in range(2) for x in (np.cos(tok), -np.sin(tok))], 1)
    inv = f(10000.0) ** (-np.arange(0, 64, 2, dtype=f) / f(64))
    pos = np.stack([n // 64, n % 64]).astype(f)
    ang = np.concatenate([np.concatenate([inv[:, None] * pos[a]] * 2, 0) for a in range(2)], 0).astype(f)
    rot = np.zeros((128, 128))
    for a in (0, 64):
        for i in range(32):
            rot[a + i, a + 32 + i] = -1.0
            rot[a + 32 + i, a + i] = 1.0
    rope = np.concatenate([np.cos(ang.astype(np.float64)), np.sin(ang.astype(np.float64)), rot.T], 1)
    inv = f(10000.0) ** (-np.arange(0, 256, 2, dtype=f) / f(256))
    ang = (inv[:, None] * n.astype(f)[None, :]).astype(f).astype(np.float64)
    rotary = np.concatenate([np.cos(ang), np.sin(ang)], 1)
    decay = []
    for h in range(4):
        gamma = 1.0 - 2.0 ** (-5.0 - h)
        for jt in range(2):
            j, i = jt * 128 + c[:, None], np.arange(jt * 128, 256)[None, :]
            decay.append(np.where(i >= j, gamma ** np.maximum(i - j, 0), 0.0) / 16.0)
    dist = np.arange(-255, 256)
    nn = np.maximum(dist, 0)
    large = 16 + (np.log(np.maximum(nn, 1).astype(f) / f(16)) / f(np.log(64.0)) * f(16)).astype(np.int32)
    bucket = np.where(nn < 16, nn, np.minimum(large, 31))
    onehot = np.zeros((33, 511))
    onehot[bucket, np.arange(511)] = 1.0
    onehot[:32, dist < 0] = 0.0
    onehot[32, dist < 0] = 1.0
    onehot = onehot[:, ::-1]
    sel_head = np.zeros((8, 8, 128))
    for t in range(8):
        sel_head[t, t] = 1.0
    sel_pair = np.zeros((16, 8, 128))
    for t in range(8):
        sel_pair[2 * t, t, :64] = 1.0
        sel_pair[2 * t + 1, t, 64:] = 1.0
    halves = np.zeros((128, 2))
    halves[:64, 0] = 1.0
    halves[64:, 1] = 1.0
    out = dict(dft_ch=dft_ch, dft_tok=dft_tok, rope=rope, rotary=rotary, decay=np.concatenate(decay, 1),
               bucket=onehot, sel_head=sel_head.reshape(8, 1024), sel_pair=sel_pair.reshape(16, 1024),
               halves=halves, ones=np.ones((128, 128)), ident=np.eye(128))
    return {k: np.ascontiguousarray(v, f) for k, v in out.items()}


def _layout(np, i):
    a = {k: np.asarray(v) for k, v in i.items()}
    out = _tables(np)
    for name in ("x", "ctx"):
        out[name] = np.ascontiguousarray(a[name][0].T.reshape(8, 128, 256).transpose(1, 0, 2).reshape(128, 2048))
    c2 = np.stack([_col(np, a["c"][0]), _col(np, a["c_ctx"])], 2).reshape(128, 16)
    twice = [np.concatenate([a[n][0], a[n][0]])[:, None] for n in
             ("moba_q_norm_2", "moba_k_norm_2", "diff_q_norm_2", "diff_k_norm_2")]
    out["vectors"] = np.ascontiguousarray(np.concatenate(
        [_col(np, a[n][l]) for n in ("g_ffn1", "g_mix", "g_ffn2") for l in range(2)] + [_col(np, a["g_final"])]
        + [_col(np, a[n][l]) for n in ("norm1_2", "norm2_2") for l in range(4)]
        + [a["g_v"][0].T, a["g_q"][0][:, None], a["g_k"][0][:, None]] + twice + [a["diff_subln_2"][0][:, None], c2]
        + [_col(np, a["b_mod"][l]) for l in range(2)]
        + [np.tile(np.eye(2, dtype=np.float32), (64, 1))], 1))
    out["w_s"] = np.ascontiguousarray(a["w_s"][0].transpose(2, 0, 1).reshape(128, 512))
    out["b_s"] = a["b_s"][0].reshape(512)
    out["rel_bias"] = a["rel_bias_2"]
    out["diff_lambda"] = a["diff_lambda_2"][0].reshape(256)
    for l in range(2):
        out[f"mod{l}"] = np.ascontiguousarray(a["w_mod"][l].reshape(2, 4, 128, 18, 512).transpose(3, 0, 2, 1, 4)
                                              .reshape(36, 128, 2048))
        for n in "12":
            out[f"gu{n}_{l}"] = _gate_up(np, a[f"w_ffn{n}_gu"][l])
            out[f"down{n}_{l}"] = _units(np, a[f"w_ffn{n}_down"][l], kpad=FF_T * 128, nb=11)
    out["in_ab"], out["out_ab"] = _units(np, a["w_in_ab"][0]), _units(np, a["w_out_ab"][0])
    out["q"], out["kv"] = _units(np, a["w_qkv"][0][:, :1024]), _units(np, a["w_qkv"][0][:, 1024:])
    out["o"] = _units(np, a["w_o"][0])
    for j in range(2):
        out[f"ret_in{j}"], out[f"ret_out{j}"] = _units(np, a["ret_w_in_2"][j]), _units(np, a["ret_w_out_2"][j])
    for kind in ("moba", "diff"):
        out[kind + "_in"], out[kind + "_out"] = _units(np, a[kind + "_w_in_2"][0]), _units(np, a[kind + "_w_out_2"][0])
    for i in range(4):
        out[f"up{i}"], out[f"down{i}"] = _units(np, a["w_up_2"][i]), _units(np, a["w_down_2"][i])
    return out


def kernel(**inputs):
    import numpy as np
    import concourse.bacc as bacc
    from concourse.bass_utils import run_bass_kernel_spmd

    nc = bacc.Bacc("TRN2", target_bir_lowering=False, num_devices=1)
    arrays = _layout(np, inputs)
    io = {name: nc.dram_tensor(f"in_{name}", a.shape, F32, kind="ExternalInput").ap() for name, a in arrays.items()}
    io["out"] = nc.dram_tensor("out_x", (128, 2048), F32, kind="ExternalOutput").ap()
    build(nc, io)
    r = run_bass_kernel_spmd(nc, [{f"in_{name}": a for name, a in arrays.items()}], core_ids=[0])
    y = r.results[0]["out_x"]
    return np.ascontiguousarray(y.reshape(128, 8, 256).transpose(2, 1, 0).reshape(1, 256, 1024))
```
